# Optimizing a Trainium2 kernel written in Bass

```python
import jax
import jax.numpy as jnp
from jax import lax
import numpy as np

D_MODEL = 2048
BATCH = 1
SEQ = 256
DEPTH = 1

CHUNK = 64
D_MIX = D_MODEL
N_GROUPS = 4
GROUP_W = D_MIX // N_GROUPS
HEAD_DIM = 64
A_HEADS = GROUP_W // HEAD_DIM
A_HEAD_DIM = HEAD_DIM
A_LORA_W = 64
A_LORA_A = 64
A_LORA_G = 128
A_GN_EPS = A_HEAD_DIM * 1e-5
B_HEADS = GROUP_W // HEAD_DIM
B_HEAD_DIM = HEAD_DIM
IDX_HEADS = 4
IDX_DIM = 64
TOPK_MAX = 256
Q_BLOCK = 128
C_HEADS = GROUP_W // HEAD_DIM
C_HEAD_DIM = HEAD_DIM
LEFT_CHUNKS = 8
REL_CLIP = 256
D_HEADS = GROUP_W // HEAD_DIM
D_KEY_DIM = HEAD_DIM // 2
D_VAL_DIM = HEAD_DIM
RET_GN_EPS = 1e-5
D_FF = 256 * ((8 * D_MODEL // 3 + 255) // 256)
CONV_W = 3
LN_EPS = 1e-5
DEEPNORM_ALPHA = (2 * DEPTH) ** 0.25
DEEPNORM_BETA = (8 * DEPTH) ** -0.25

A_SPLITS = (GROUP_W, GROUP_W, GROUP_W, A_LORA_W, A_LORA_A, A_LORA_G)
B_SPLITS = (GROUP_W, B_HEAD_DIM, B_HEAD_DIM, IDX_HEADS * IDX_DIM, IDX_DIM, IDX_HEADS)
C_SPLITS = (GROUP_W, GROUP_W, GROUP_W)
D_SPLITS = (D_HEADS * D_KEY_DIM, D_HEADS * D_KEY_DIM, GROUP_W, GROUP_W)
A_COLS = sum(A_SPLITS)
B_COLS = sum(B_SPLITS)
C_COLS = sum(C_SPLITS)
D_COLS = sum(D_SPLITS)
N_IN = A_COLS + B_COLS + C_COLS + D_COLS

kernel_name = 'hybrid_stream_encoder'

F32 = jnp.float32

def _split(x, sizes):
    return jnp.split(x, np.cumsum(sizes)[:-1].tolist(), axis=-1)

def _layer_norm(x, g, b):
    xf = x.astype(F32)
    mu = jnp.mean(xf, -1, keepdims=True)
    var = jnp.mean(jnp.square(xf - mu), -1, keepdims=True)
    return ((xf - mu) * lax.rsqrt(var + LN_EPS)).astype(x.dtype) * g + b

def _norm_last(y, eps):
    yf = y.astype(F32)
    mu = jnp.mean(yf, -1, keepdims=True)
    var = jnp.mean(jnp.square(yf - mu), -1, keepdims=True)
    return (yf - mu) * lax.rsqrt(var + eps)

def _shift_right(x):
    return jnp.pad(x, ((0, 0), (1, 0), (0, 0)))[:, :-1]

def _alibi_slopes(n):
    return 2.0 ** (-8.0 * jnp.arange(1, n + 1, dtype=F32) / n)

def _rwkv7_mix(p, mu, w0, w2, a0, a2, g2, k_k, k_a, r_k, ln_g, ln_b):
    bsz, t_len, _ = p.shape
    p = p + (_shift_right(p) - p) * mu
    r, k, v, wl, al, gl = _split(p, A_SPLITS)
    w_log = -jax.nn.softplus(-(w0 + jnp.tanh(wl) @ w2)) - 0.5
    decay = jnp.exp(-jnp.exp(w_log.astype(F32)))
    a = jax.nn.sigmoid(a0 + al @ a2)
    g = jax.nn.sigmoid(gl) @ g2
    hs = lambda z: z.reshape(bsz, t_len, A_HEADS, A_HEAD_DIM)
    kk = hs(k * k_k).astype(F32)
    kk = kk / jnp.maximum(jnp.sqrt(jnp.sum(kk * kk, -1, keepdims=True)), 1e-12)
    k = k * (1.0 + (a - 1.0) * k_a)
    r_h, k_h, v_h, a_h = hs(r), hs(k), hs(v), hs(a)
    seq = tuple(jnp.moveaxis(z.astype(F32), 1, 0) for z in
                (r_h, hs(decay), k_h, v_h, -kk, kk * a_h))

    def step(state, inp):
        r_t, w_t, k_t, v_t, a_t, b_t = inp
        sa = jnp.einsum('bhvk,bhk->bhv', state, a_t)
        state = (state * w_t[:, :, None, :] + sa[..., None] * b_t[:, :, None, :]
                 + v_t[..., None] * k_t[:, :, None, :])
        return state, jnp.einsum('bhvk,bhk->bhv', state, r_t)

    s0 = jnp.zeros((bsz, A_HEADS, A_HEAD_DIM, A_HEAD_DIM), F32)
    _, y = lax.scan(step, s0, seq)
    y = jnp.moveaxis(y, 0, 1)
    y = _norm_last(y, A_GN_EPS).reshape(bsz, t_len, GROUP_W) * ln_g + ln_b
    bonus = jnp.sum(r_h * k_h * r_k, -1, keepdims=True) * v_h
    return (y + bonus.reshape(bsz, t_len, GROUP_W)) * g

def _dsa_mix(q, k, v, qi, ki, wi):
    bsz, t_len, _ = q.shape
    topk = min(TOPK_MAX, t_len // 4)
    nb = t_len // Q_BLOCK
    q = jnp.moveaxis(q.reshape(bsz, nb, Q_BLOCK, B_HEADS, B_HEAD_DIM), 1, 0)
    qi = jnp.moveaxis(qi.reshape(bsz, nb, Q_BLOCK, IDX_HEADS, IDX_DIM), 1, 0)
    wi = jnp.moveaxis(wi.reshape(bsz, nb, Q_BLOCK, IDX_HEADS), 1, 0) * (IDX_HEADS ** -0.5)
    key_pos = jnp.arange(t_len)
    slopes = _alibi_slopes(B_HEADS)
    gather = jax.vmap(lambda table, idx: table[idx])

    def block(args):
        n, qb, qib, wib = args
        t = n * Q_BLOCK + jnp.arange(Q_BLOCK)
        limit = (t // CHUNK + 1) * CHUNK
        logits = jnp.einsum('bqhd,bsd->bqhs', qib, ki) * (IDX_DIM ** -0.5)
        score = jnp.einsum('bqhs,bqh->bqs', jax.nn.relu(logits), wib).astype(F32)
        score = jnp.where(key_pos[None, None, :] < limit[None, :, None], score, -jnp.inf)
        _, idx = lax.top_k(score, topk)
        sel_ok = idx < limit[None, :, None]
        k_sel = gather(k, idx)
        v_sel = gather(v, idx)
        s = jnp.einsum('bqhd,bqkd->bqhk', qb, k_sel).astype(F32) * (B_HEAD_DIM ** -0.5)
        dist = jnp.abs(t[None, :, None] - idx).astype(F32)
        s = s - slopes[None, None, :, None] * dist[:, :, None, :]
        s = jnp.where(sel_ok[:, :, None, :], s, -jnp.inf)
        pr = jax.nn.softmax(s, axis=-1).astype(v.dtype)
        return jnp.einsum('bqhk,bqkd->bqhd', pr, v_sel)

    out = lax.map(block, (jnp.arange(nb), q, qi, wi))
    return jnp.moveaxis(out, 0, 1).reshape(bsz, t_len, GROUP_W)

def _chunk_attn_mix(q, k, v, rel_bias):
    bsz, t_len, _ = q.shape
    nc = t_len // CHUNK
    band = (LEFT_CHUNKS + 1) * CHUNK
    pad = LEFT_CHUNKS * CHUNK
    q = jnp.moveaxis(q.reshape(bsz, nc, CHUNK, C_HEADS, C_HEAD_DIM), 1, 0)
    kp = jnp.pad(k.reshape(bsz, t_len, C_HEADS, C_HEAD_DIM), ((0, 0), (pad, 0), (0, 0), (0, 0)))
    vp = jnp.pad(v.reshape(bsz, t_len, C_HEADS, C_HEAD_DIM), ((0, 0), (pad, 0), (0, 0), (0, 0)))
    i = jnp.arange(CHUNK)[:, None]
    j = jnp.arange(band)[None, :]
    rel = jnp.clip(i - j + pad, -REL_CLIP, REL_CLIP) + REL_CLIP
    bias = rel_bias[:, rel].astype(F32)

    def chunk(args):
        n, qc = args
        kc = lax.dynamic_slice_in_dim(kp, n * CHUNK, band, axis=1)
        vc = lax.dynamic_slice_in_dim(vp, n * CHUNK, band, axis=1)
        s = jnp.einsum('bqhd,bkhd->bhqk', qc, kc).astype(F32) * (C_HEAD_DIM ** -0.5) + bias[None]
        ok = j >= pad - n * CHUNK
        s = jnp.where(ok[None, None], s, -jnp.inf)
        pr = jax.nn.softmax(s, axis=-1).astype(vc.dtype)
        return jnp.einsum('bhqk,bkhd->bqhd', pr, vc)

    out = lax.map(chunk, (jnp.arange(nc), q))
    return jnp.moveaxis(out, 0, 1).reshape(bsz, t_len, GROUP_W)

def _retention_mix(q, k, v, g):
    bsz, t_len, _ = q.shape
    nc = t_len // CHUNK
    q = q.reshape(bsz, nc, CHUNK, D_HEADS, D_KEY_DIM)
    k = k.reshape(bsz, nc, CHUNK, D_HEADS, D_KEY_DIM) * (D_KEY_DIM ** -0.5)
    v = v.reshape(bsz, nc, CHUNK, D_HEADS, D_VAL_DIM)
    log_gamma = jnp.log1p(-(2.0 ** (-5.0 - jnp.arange(D_HEADS, dtype=F32))))
    pos = jnp.arange(CHUNK, dtype=F32)
    diff = pos[:, None] - pos[None, :]
    intra_decay = jnp.where(diff >= 0, jnp.exp(log_gamma[:, None, None] * jnp.maximum(diff, 0.0)), 0.0)
    kv_decay = jnp.exp(log_gamma[:, None] * (CHUNK - 1 - pos)[None, :])
    q_decay = jnp.exp(log_gamma[:, None] * (pos + 1)[None, :])
    chunk_decay = jnp.exp(log_gamma * CHUNK)
    s = jnp.einsum('bnihd,bnjhd->bnhij', q, k).astype(F32) * intra_decay
    intra = jnp.einsum('bnhij,bnjhe->bnihe', s, v.astype(F32))
    kv = jnp.einsum('bnjhd,bnjhe,hj->nbhde', k.astype(F32), v.astype(F32), kv_decay)

    def step(state, kv_n):
        return state * chunk_decay[None, :, None, None] + kv_n, state

    r0 = jnp.zeros((bsz, D_HEADS, D_KEY_DIM, D_VAL_DIM), F32)
    _, r_prev = lax.scan(step, r0, kv)
    inter = jnp.einsum('bnihd,hi,nbhde->bnihe', q.astype(F32), q_decay, r_prev)
    y = _norm_last(intra + inter, RET_GN_EPS).reshape(bsz, t_len, GROUP_W)
    return y * jax.nn.silu(g)

def _causal_dwconv(x, w, b):
    out = lax.conv_general_dilated(
        x, w[:, None, :].astype(x.dtype), window_strides=(1,),
        padding=((CONV_W - 1, 0),), dimension_numbers=('NWC', 'WIO', 'NWC'),
        feature_group_count=x.shape[-1])
    return out + b

def setup_inputs(seed: int = 0) -> dict:
    key = jax.random.key(seed)
    ks = iter(jax.random.split(key, 32))
    nrm = lambda shape, scale: jax.random.normal(next(ks), shape, F32) * scale
    L = DEPTH
    return {
        'x': nrm((BATCH, SEQ, D_MODEL), 1.0),
        'c': nrm((BATCH, D_MODEL), 1.0),
        'w_mod': nrm((L, D_MODEL, 6 * D_MODEL), 0.2 * D_MODEL ** -0.5),
        'b_mod': nrm((L, 6 * D_MODEL), 0.01),
        'w_in': nrm((L, D_MODEL, N_IN), D_MODEL ** -0.5),
        'rwkv_mu': jax.random.uniform(next(ks), (L, A_COLS), F32),
        'rwkv_w0': jax.random.uniform(next(ks), (L, GROUP_W), F32, -6.0, 1.0),
        'rwkv_w2': nrm((L, A_LORA_W, GROUP_W), 0.1 * A_LORA_W ** -0.5),
        'rwkv_a0': nrm((L, GROUP_W), 0.1),
        'rwkv_a2': nrm((L, A_LORA_A, GROUP_W), 0.1 * A_LORA_A ** -0.5),
        'rwkv_g2': nrm((L, A_LORA_G, GROUP_W), A_LORA_G ** -0.5),
        'rwkv_kk': 0.85 + nrm((L, GROUP_W), 0.05),
        'rwkv_ka': 1.0 + nrm((L, GROUP_W), 0.05),
        'rwkv_rk': nrm((L, A_HEADS, A_HEAD_DIM), 0.1),
        'rwkv_ln_g': 1.0 + nrm((L, GROUP_W), 0.02),
        'rwkv_ln_b': nrm((L, GROUP_W), 0.02),
        'chunk_rel_bias': nrm((L, C_HEADS, 2 * REL_CLIP + 1), 0.1),
        'w_out': nrm((L, D_MIX, D_MODEL), DEEPNORM_BETA * D_MIX ** -0.5),
        'ln1_g': 1.0 + nrm((L, D_MODEL), 0.02),
        'ln1_b': nrm((L, D_MODEL), 0.02),
        'w_up': nrm((L, D_MODEL, 2 * D_FF), D_MODEL ** -0.5),
        'conv_w': nrm((L, CONV_W, D_FF), CONV_W ** -0.5),
        'conv_b': nrm((L, D_FF), 0.02),
        'w_down': nrm((L, D_FF, D_MODEL), DEEPNORM_BETA * D_FF ** -0.5),
        'ln2_g': 1.0 + nrm((L, D_MODEL), 0.02),
        'ln2_b': nrm((L, D_MODEL), 0.02),
    }

def reference(x, c, w_mod, b_mod, w_in, rwkv_mu, rwkv_w0, rwkv_w2, rwkv_a0, rwkv_a2,
              rwkv_g2, rwkv_kk, rwkv_ka, rwkv_rk, rwkv_ln_g, rwkv_ln_b, chunk_rel_bias,
              w_out, ln1_g, ln1_b, w_up, conv_w, conv_b, w_down, ln2_g, ln2_b):
    c_act = jax.nn.silu(c)
    for l in range(DEPTH):
        mod = c_act @ w_mod[l] + b_mod[l]
        sh1, sc1, gt1, sh2, sc2, gt2 = [m[:, None, :] for m in jnp.split(mod, 6, axis=-1)]

        h = x * (1.0 + sc1) + sh1
        proj = h @ w_in[l]
        p_a, p_b, p_c, p_d = _split(proj, (A_COLS, B_COLS, C_COLS, D_COLS))
        y_a = _rwkv7_mix(p_a, rwkv_mu[l], rwkv_w0[l], rwkv_w2[l], rwkv_a0[l], rwkv_a2[l],
                         rwkv_g2[l], rwkv_kk[l], rwkv_ka[l], rwkv_rk[l], rwkv_ln_g[l], rwkv_ln_b[l])
        qb, kb, vb, qib, kib, wib = _split(p_b, B_SPLITS)
        y_b = _dsa_mix(qb, kb, vb, qib, kib, wib)
        qc, kc, vc = _split(p_c, C_SPLITS)
        y_c = _chunk_attn_mix(qc, kc, vc, chunk_rel_bias[l])
        qd, kd, vd, gd = _split(p_d, D_SPLITS)
        y_d = _retention_mix(qd, kd, vd, gd)
        mix = jnp.concatenate([y_a, y_b, y_c, y_d], axis=-1) @ w_out[l]
        x = _layer_norm(DEEPNORM_ALPHA * x + (1.0 + gt1) * mix, ln1_g[l], ln1_b[l])

        h = x * (1.0 + sc2) + sh2
        gate, up = _split(h @ w_up[l], (D_FF, D_FF))
        f = jax.nn.silu(_causal_dwconv(gate, conv_w[l], conv_b[l])) * up
        x = _layer_norm(DEEPNORM_ALPHA * x + (1.0 + gt2) * (f @ w_down[l]), ln2_g[l], ln2_b[l])
    return x


_drawn_inputs = setup_inputs


def setup_inputs(seed=0):
    import zlib

    import numpy as np

    out = dict(_drawn_inputs(seed))
    spreads = {}
    factors = {'b_mod': 3.5,
     'rwkv_w2': 8.0,
     'rwkv_a0': 8.0,
     'rwkv_a2': 8.0,
     'rwkv_kk': 8.0,
     'rwkv_ka': 7.767,
     'rwkv_ln_g': 25.128,
     'rwkv_ln_b': 26.469,
     'chunk_rel_bias': 41.836,
     'ln1_g': 2.714,
     'ln1_b': 2.771,
     'conv_b': 8.0,
     'ln2_g': 22.997,
     'ln2_b': 22.07}
    for name, (base, spread) in spreads.items():
        noise = np.random.default_rng([zlib.crc32(name.encode()), seed]).standard_normal(out[name].shape)
        drawn = base * np.exp(spread * noise) if base else spread * noise
        out[name] = jnp.asarray(drawn.astype(out[name].dtype))
    for name, factor in factors.items():
        out[name] = (out[name] * factor).astype(out[name].dtype)
    return out
```

```python
import concourse.bass as bass
from concourse import mybir
from contextlib import ExitStack

D, T, P = 2048, 256, 128
KT = D // P
CHUNK, HD = 64, 64
GW = 512
HEADS = GW // HD
D_FF = 256 * ((8 * D // 3 + 255) // 256)
FT = D_FF // P
A_COLS, B_COLS, C_COLS, D_COLS = 3 * GW + 256, GW + 2 * HD + 4 * 64 + 64 + 4, 3 * GW, 2 * 256 + 2 * GW
B0, C0, D0 = A_COLS, A_COLS + B_COLS, A_COLS + B_COLS + C_COLS
ALPHA = 2.0 ** 0.25
KAPPA = 0.6065306597126334
BIG = 1.0e30
TAKEN = -3.0e38
LN_EPS, A_EPS, RET_EPS = 1e-5, HD * 1e-5, 1e-5
TOPK = T // 4

RING = 4
AHEAD = 4
N_IN_BLOCKS, N_OUT_BLOCKS, N_UP, N_DOWN_BLOCKS = 12, 4, D_FF // 512, 4
CH_IN = KT // 2
CH_DOWN = FT // 2
N0_OUT = N_IN_BLOCKS * CH_IN
N0_UP = N0_OUT + N_OUT_BLOCKS * CH_IN
N0_DOWN = N0_UP + 2 * N_UP * CH_IN
N_ALL = N0_DOWN + N_DOWN_BLOCKS * CH_DOWN

MOD_W = 1024
MOD_PARTS = 6 * D // MOD_W
SH1, SC1, GT1, SH2, SC2, GT2 = (16 * i for i in range(6))

CF = dict(ident=0, ones=128, heads2=256, flip=384, decay=512)
CF_W = 512 + 1024
N_EVAC_IN = [4, 4, 4, 3, 2, 2, 2, 2, 2, 2, 2, 2]
LEVELS = 6
CB = dict(ident=0, level=128, level0t=128 + 7 * 128, su=128 + 8 * 128, iu=128 + 9 * 128,
          ret=128 + 10 * 128, slope=128 + 13 * 128, dist=128 + 21 * 128, band=128 + 24 * 128)
CB_W = 128 + 27 * 128
PR = dict(mu=0, w0=14, a0=18, kk=22, ka=26, rk=30, conv_b=34, conv2=34 + FT,
          conv0=128, conv1=128 + FT, ln1_g=128 + 2 * FT, ln1_b=128 + 2 * FT + 16)

RW = ["lora", "turn", "gram"] + [f"{s}{l}" for l in range(1, LEVELS + 1) for s in ("ld", "dx")] + \
     ["gram2", "rhs0", "sa0", "state", "rhs1", "sa1", "y1"]
RW_ACT = ["gates", "decays", "turned", "rhs0", "sa0", "y0", "rhs1", "sa1", "y1"]
RW_DVE = ["cum", "hats", "inv0"] + [f"{s}{l}" for l in range(1, LEVELS + 1) for s in ("x", "d")] + \
         ["gf", "state"]
UNITS = HEADS // 2


def step(names, name, u):
    return u * len(names) + names.index(name) + 1


def encoder_layer(nc, x, c, w_mod, b_mod, w_in, rwkv_mu, rwkv_w0, rwkv_w2, rwkv_a0, rwkv_a2, rwkv_g2,
                  rwkv_kk, rwkv_ka, rwkv_rk, rwkv_ln_g, rwkv_ln_b, chunk_rel_bias, w_out, ln1_g, ln1_b,
                  w_up, conv_w, conv_b, w_down, ln2_g, ln2_b, const_f, const_b, out):
    f32, f32r, bf16 = mybir.dt.float32, mybir.dt.float32r, mybir.dt.bfloat16
    ALU, ACT, AX = mybir.AluOpType, mybir.ActivationFunctionType, mybir.AxisListType
    ds = bass.ds
    base = (nc.sbuf_base + 63) // 64 * 64

    def sb(name, shape, off_kb, dt=f32):
        return nc.alloc_sbuf_tensor_at(name, shape, dt, offset=base + int(off_kb * 1024))

    RAW = sb("RAW", [P, RING, 2, 512], 0)
    WHI = sb("WHI", [P, RING, 2, 512], 16, f32r)
    WLO = sb("WLO", [P, RING, 2, 512], 32, f32r)
    HHI = sb("HHI", [P, KT, T], 48, f32r)
    HLO = sb("HLO", [P, KT, T], 64, f32r)
    LN2G, LN2B = sb("LN2G", [P, D], 48), sb("LN2B", [P, D], 56)
    GB2, DGM2, ZT2 = sb("GB2", [P, D], 64), sb("DGM2", [P, 2, 512], 72), sb("ZT2", [P, 512], 76)
    FHI = sb("FHI", [P, FT, T], 80, f32r)
    FLO = sb("FLO", [P, FT, T], 80 + FT, f32r)
    MODR = sb("MODR", [P, RING, MOD_W], 80)
    ACC = sb("ACC", [P, 2, MOD_W], 96)
    PA = sb("PA", [P, 14, T], 104)
    DQK, DV, DG = sb("DQK", [P, 4, T], 104), sb("DV", [P, 2, GW], 108), sb("DG", [P, 2, GW], 112)
    BQ, BK = sb("BQ", [P, 4, T], 118), sb("BK", [P, 2, T], 122)
    BQI, BVW = sb("BQI", [P, 2, T], 124), sb("BVW", [P, 2, 68], 126)
    CQ, CK, CV = sb("CQ", [P, 4, T], 127), sb("CK", [P, 4, T], 131), sb("CV", [P, 2, GW], 135)
    W2A2, G2 = sb("W2A2", [P, GW], 139), sb("G2", [P, GW], 141)
    LNAG, LNAB = sb("LNAG", [P, GW], 143), sb("LNAB", [P, GW], 145)
    SIG, AL, EM = sb("SIG", [P, T], 147), sb("AL", [P, T], 148), sb("EM", [P, 2, P], 149)
    KKN, TA = sb("KKN", [P, T], 150), sb("TA", [P, T], 151)
    CU, EP = sb("CU", [P, 2, 129], 152), sb("EP", [P, 2, 129], 153.0625)
    LT, DI, DT = sb("LT", [P, 4, P], 154.25), sb("DI", [P, 4, P], 156.25), sb("DT", [P, 4, P], 158.25)
    XI, ET = sb("XI", [P, 4, P], 160.25), sb("ET", [P, 4, P], 162.25)
    GTR, FTR = sb("GTR", [P, 4, P], 154.25), sb("FTR", [P, 4, P], 156.25)
    VTA = sb("VTA", [P, 2, GW], 164.25)
    YSQ = sb("YSQ", [P, 2, GW], 168.25)
    MST = sb("MST", [P, HD], 172.5)
    TB, RK = sb("TB", [P, 2, 2, P], 180), sb("RK", [P, T], 182)
    RH, SA = sb("RH", [P, P], 183), sb("SA", [P, P], 183.5)
    AR, BH, KH = sb("AR", [P, 2, 2, P], 184), sb("BH", [P, T], 186), sb("KH", [P, T], 187)
    RN, SQ = sb("RN", [P, 4, T], 188), sb("SQ", [P, 4, T], 154.25)
    PB, PTB = sb("PB", [P, 2, 384], 147), sb("PTB", [P, 2, 384], 150)
    SC, RL, SEL = sb("SC", [P, 384], 153), sb("RL", [P, 2, T], 154.5), sb("SEL", [P, 384], 156.5, bf16)
    STD, BIA = sb("STD", [P, 2, 384], 157.25), sb("BIA", [P, HEADS, T], 160.25)
    X0, X1 = sb("X0", [P, 2, D], 176), sb("X1", [P, 2, D], 176)
    YG = [sb(f"Y{g}", [P, 2, GW], 176 + 4 * i) for i, g in enumerate("ABCD")]
    YA, YD = YG[0], YG[3]
    XT, HTMP = sb("XT", [P, KT, T], 120), sb("HTMP", [P, 4, T], 172)
    XR, GB1 = sb("XR", [P, 2, D], 104), sb("GB1", [P, D], 120)
    DGM1, ZT1 = sb("DGM1", [P, 2, 512], 150), sb("ZT1", [P, 512], 154)
    LN1G, LN1B = sb("LN1G", [P, D], 156), sb("LN1B", [P, D], 164)
    CFT = sb("CFT", [P, CF_W], 192)
    PCOL, BMC, MC = sb("PCOL", [P, 256], 198), sb("BMC", [P, 96], 199), sb("MC", [P, 96], 199.5)
    SM = sb("SM", [P, 224], 199.875)
    CBT = sb("CBT", [P, CB_W], 200.75, bf16)
    PROW = sb("PROW", [P, 3, P], 172)
    GF, SF = sb("GF", [P, 4, T], 194), sb("SF", [P, 4, T], 201)

    def cf(name, n=128):
        return CFT[:, CF[name]:CF[name] + n]

    def cb(name, n=128, i=0):
        return CBT[:, CB[name] + i * 128:CB[name] + i * 128 + n]

    def pc(name, i=0):
        return PCOL[:, PR[name] + i:PR[name] + i + 1]

    def bc(ap, shape):
        return ap.unsqueeze(len(shape) - 1).broadcast_to(shape)

    IDENT, ONES, HEADS2, FLIP = cf("ident"), cf("ones"), cf("heads2"), cf("flip")
    IDB = cb("ident")
    OMU, CC = SM[:, 0:14], SM[:, 16:32]
    KMID, NKMID, IMID = SM[:, 32:34], SM[:, 34:36], SM[:, 36:38]
    BON = SM[:, 40:56]
    NM, SUM, REC = SM[:, 56:72], SM[:, 72:104], SM[:, 104:120]
    S1, S2, RS = SM[:, 120:136], SM[:, 136:152], SM[:, 152:168]
    W4, T8, CSG, EPS = SM[:, 168:176], SM[:, 176:184], SM[:, 184:200], SM[:, 200:203]
    CCOL = SM[:, 204:220]
    BST, MV = SM[:, 56:104], SM[:, 104:112]
    SCG, SHB, CONV = SM[:, 120:136], SM[:, 136:152], SM[:, 152:168]
    SPARE = SM[:, 112:120]

    with ExitStack() as ctx:
        def sem(name):
            return ctx.enter_context(nc.semaphore(name))

        G = [ctx.enter_context(nc.psum_tensor(f"G{i}", [P, 512], f32)) for i in range(4)]
        M = [ctx.enter_context(nc.psum_tensor(f"M{i}", [P, 512], f32)) for i in range(4)]

        raw_in = [sem(f"raw_in{i}") for i in range(RING)]
        mod_in = [sem(f"mod_in{i}") for i in range(RING)]
        hi_done, lo_done = sem("hi_done"), sem("lo_done")
        w_used = sem("w_used")
        evac = [sem("evac_even"), sem("evac_odd")]
        mod_done, mod_sum, mod_col = sem("mod_done"), sem("mod_sum"), sem("mod_col")
        c_in, cf_in, x_in, prow_in = sem("c_in"), sem("cf_in"), sem("x_in"), sem("prow_in")
        late_in, lnp_in, ln2_in, bias_in = sem("late_in"), sem("lnp_in"), sem("ln2_in"), sem("bias_in")
        pcol_pe, pcol_done, silu_c = sem("pcol_pe"), sem("pcol_done"), sem("silu_c")
        xt_pe, xt_act = sem("xt_pe"), sem("xt_act")
        h_new, h_hi, h_lo = sem("h_new"), sem("h_hi"), sem("h_lo")
        mixed, gates = sem("mixed"), sem("gates")
        kn_sq, kn_pe, kn_sqrt, kn_done = sem("kn_sq"), sem("kn_pe"), sem("kn_sqrt"), sem("kn_done")
        rw_pe, rw_act, rw_dve = sem("rw_pe"), sem("rw_act"), sem("rw_dve")
        centred, squared, var_sum, std_done = sem("centred"), sem("squared"), sem("var_sum"), sem("std_done")
        a_gate, a_done = sem("a_gate"), sem("a_done")
        ix_pe, ix_act, ix_dve, sel_done = sem("ix_pe"), sem("ix_act"), sem("ix_dve"), sem("sel_done")
        at_s, at_max, at_exp, at_turn, at_pt, at_pv, at_y = (sem("at_" + n) for n in
                                                            ("s", "max", "exp", "turn", "pt", "pv", "y"))
        ret_s, ret_m, ret_pv, ret_y, d_done = (sem("ret_" + n) for n in ("s", "m", "pv", "y", "done"))
        y_pe, y_hi, y_lo = sem("y_pe"), sem("y_hi"), sem("y_lo")
        gb_dve, gb_pe, gb_act = sem("gb_dve"), sem("gb_pe"), sem("gb_act")
        ln_var, ln_std, zn_done, zn_pe = sem("ln_var"), sem("ln_std"), sem("zn_done"), sem("zn_pe")
        conv_cp, g_pre, g_sig = sem("conv_cp"), sem("g_pre"), sem("g_sig")
        f_hi, f_lo = sem("f_hi"), sem("f_lo")
        out_ready, out_sent = sem("out_ready"), sem("out_sent")
        dve_own, zeroed = sem("dve_own"), sem("zeroed")

        EV = []
        for b in range(N_IN_BLOCKS):
            EV.append(N_EVAC_IN[b] + (EV[b - 2] if b >= 2 else 0))
        EV0 = EV[-2:]
        EV1 = [EV0[0] + 4, EV0[1] + 4]
        EV2 = [EV1[0] + 4 * N_UP, EV1[1] + 2 * N_UP]

        def raw_count(n):
            double = sum(1 for m in range(n % RING, n + 1, RING) if m // CH_IN in (3, 5))
            return 16 * (n // RING + 1 + double)

        RAW_SHIFT = raw_count(N0_OUT) - 16 * (N0_OUT // RING + 1)

        def pair(b):
            return G[2 * (b % 2)], G[2 * (b % 2) + 1]

        def dup_views(dst, s):
            d, r = dst[:, s, :, :], RAW[:, s, :, :]
            two = lambda lo: r[:, :, lo:lo + 64].unsqueeze(2).broadcast_to((P, 2, 2, 64))
            return [(d[:, :, 0:128].rearrange("p k (a n) -> p k a n", a=2), two(0)),
                    (d[:, :, 128:256].rearrange("p k (a n) -> p k a n", a=2), two(128)),
                    (d[:, :, 256:320], r[:, :, 64:128]), (d[:, :, 320:324], r[:, :, 192:196])]

        block = ctx.enter_context(nc.Block())

        @block.sync
        def _(sp):
            sp.dma_start(CCOL, c.rearrange("a (p t) -> (a p) t", t=KT)).then_inc(c_in, 16)
            sp.dma_start(CFT[:, :], const_f).then_inc(cf_in, 16)
            xv = x.rearrange("a (t p) d -> (a p) t d", p=P)
            for t in range(2):
                sp.dma_start(X0[:, t, :], xv[:, t, :]).then_inc(x_in, 16)
            r128 = lambda ap: ap.rearrange("a (j p) -> (a j) p", p=P)
            cw = lambda i: conv_w[0, i, :].rearrange("(j p) -> j p", p=P)
            for g, name, src, n in [
                    (0, "mu", r128(rwkv_mu), 14), (0, "w0", r128(rwkv_w0), 4), (0, "a0", r128(rwkv_a0), 4),
                    (0, "kk", r128(rwkv_kk), 4), (0, "ka", r128(rwkv_ka), 4),
                    (0, "rk", rwkv_rk.rearrange("a (j h) d -> (a j) (h d)", h=2), 4),
                    (0, "conv_b", r128(conv_b), FT), (0, "conv2", cw(2), FT), (1, "conv0", cw(0), FT),
                    (1, "conv1", cw(1), FT), (1, "ln1_g", r128(ln1_g), KT), (1, "ln1_b", r128(ln1_b), KT)]:
                r = PR[name] - 128 * g
                sp.dma_start(PROW[r:r + n, g, :], src).then_inc(prow_in, 16)
            sp.dma_start(PROW[0:96, 2, :], r128(b_mod)).then_inc(prow_in, 16)
            sp.dma_start(CBT[:, :], const_b.bitcast(bf16)).then_inc(late_in, 16)
            sp.dma_start(W2A2[0:64, :], rwkv_w2[0]).then_inc(late_in, 16)
            sp.dma_start(W2A2[64:128, :], rwkv_a2[0]).then_inc(late_in, 16)
            sp.dma_start(G2[:, :], rwkv_g2[0]).then_inc(late_in, 16)
            sp.dma_start(LNAG[:, :], rwkv_ln_g[0, :].partition_broadcast(P)).then_inc(late_in, 16)
            sp.dma_start(LNAB[:, :], rwkv_ln_b[0, :].partition_broadcast(P)).then_inc(late_in, 16)

            wi, wo, wu, wd = (w[0].rearrange("(t p) n -> p t n", p=P) for w in (w_in, w_out, w_up, w_down))
            bkv, bqi = B0 + GW, B0 + GW + 2 * HD
            cols = [[(0, GW)], [(GW, GW)], [(2 * GW, GW)], [(3 * GW, 256), (bqi, 256)], [(B0, GW)],
                    [(bkv, 128), (bqi + 256, 68)], [(C0, GW)], [(C0 + GW, GW)], [(C0 + 2 * GW, GW)],
                    [(D0, GW)], [(D0 + GW, GW)], [(D0 + 2 * GW, GW)]]
            for n in range(N0_OUT):
                b, j = divmod(n, CH_IN)
                if n >= RING:
                    sp.wait_ge(lo_done, n - RING + 1)
                at = 0
                for c0, w in cols[b]:
                    sp.dma_start(RAW[:, n % RING, :, at:at + w], wi[:, 2 * j:2 * j + 2, c0:c0 + w])\
                      .then_inc(raw_in[n % RING], 16)
                    at += w
            sp.wait_ge(a_done, 1)
            sp.dma_start(BIA[:, :, :], bass.AP(tensor=chunk_rel_bias.tensor, offset=129,
                                               ap=[[1, P], [513, HEADS], [1, T]])).then_inc(bias_in, 16)
            with sp.Fori(0, N_OUT_BLOCKS) as b:
                for j in range(CH_IN):
                    sp.wait_ge(lo_done, b * CH_IN + (N0_OUT + j - RING + 1))
                    sp.dma_start(RAW[:, j % RING, :, :], wo[:, 2 * j:2 * j + 2, ds(b * 512, 512)])\
                      .then_inc(raw_in[j % RING], 16)
            with sp.Fori(0, N_UP) as i:
                for j in range(2 * CH_IN):
                    half, jj = divmod(j, CH_IN)
                    sp.wait_ge(lo_done, i * (2 * CH_IN) + (N0_UP + j - RING + 1))
                    sp.dma_start(RAW[:, j % RING, :, :],
                                 wu[:, 2 * jj:2 * jj + 2, ds(i * 512 + half * D_FF, 512)])\
                      .then_inc(raw_in[j % RING], 16)
            for b in range(N_DOWN_BLOCKS):
                for j in range(CH_DOWN):
                    n = N0_DOWN + b * CH_DOWN + j
                    sp.wait_ge(lo_done, n - RING + 1)
                    sp.dma_start(RAW[:, n % RING, :, :], wd[:, 2 * j:2 * j + 2, b * 512:(b + 1) * 512])\
                      .then_inc(raw_in[n % RING], 16)
                if b == 0:
                    sp.wait_ge(w_used, N0_DOWN)
                    sp.dma_start(LN2G[:, :], ln2_g[0, :].partition_broadcast(P)).then_inc(ln2_in, 16)
                    sp.dma_start(LN2B[:, :], ln2_b[0, :].partition_broadcast(P)).then_inc(ln2_in, 16)
            ov = out.rearrange("a (t p) d -> (a p) t d", p=P)
            for t in range(2):
                sp.wait_ge(out_ready, t + 1)
                sp.dma_start(ov[:, t, :], X1[:, t, :]).then_inc(out_sent, 16)
            sp.wait_ge(out_sent, 32)

        @block.gpsimd
        def _(pool):
            pool.memset(CU[:, :, 0:1], 0.0).then_inc(zeroed, 1)
            pool.memset(EPS[:, 0:1], LN_EPS).then_inc(zeroed, 1)
            wm = w_mod[0].rearrange("(p t) n -> p t n", t=KT)
            for t in range(KT):
                if t >= RING:
                    pool.wait_ge(mod_done, t - RING + 1)
                pool.dma_start(MODR[:, t % RING, :], wm[:, t, 0:MOD_W]).then_inc(mod_in[t % RING], 16)

            def parts(first, last):
                with pool.Fori(first, last) as m:
                    for t in range(KT):
                        pool.wait_ge(mod_done, m * KT + (t - RING + 1))
                        pool.dma_start(MODR[:, t % RING, :], wm[:, t, ds(m * MOD_W, MOD_W)])\
                            .then_inc(mod_in[t % RING], 16)

            parts(1, MOD_PARTS - 2)
            pool.wait_ge(y_lo, 8)
            xv = x.rearrange("a (t p) d -> (a p) t d", p=P)
            for t in range(2):
                pool.dma_start(XR[:, t, :], xv[:, t, :]).then_inc(lnp_in, 16)
            pool.dma_start(LN1G[:, :], ln1_g[0, :].partition_broadcast(P)).then_inc(lnp_in, 16)
            pool.dma_start(LN1B[:, :], ln1_b[0, :].partition_broadcast(P)).then_inc(lnp_in, 16)
            parts(MOD_PARTS - 2, MOD_PARTS)

        @block.scalar
        def _(act):
            def split_hi(n):
                if n >= N_ALL:
                    return
                s = n % RING
                act.wait_ge(raw_in[s], raw_count(n))
                if n >= RING:
                    act.wait_ge(w_used, n - RING + 1)
                if n // CH_IN == 5:
                    for dst, src in dup_views(WHI, s):
                        ins = act.activation(dst, src, ACT.Copy)
                    ins.then_inc(hi_done, 1)
                else:
                    act.activation(WHI[:, s, :, :], RAW[:, s, :, :], ACT.Copy).then_inc(hi_done, 1)

            def split_hi_at(s, groups, n):
                act.wait_ge(raw_in[s], groups * 16 + (RAW_SHIFT + 16))
                act.wait_ge(w_used, n + (1 - RING))
                act.activation(WHI[:, s, :, :], RAW[:, s, :, :], ACT.Copy).then_inc(hi_done, 1)

            act.wait_ge(c_in, 16)
            act.activation(CSG, CCOL, ACT.Sigmoid).then_inc(silu_c, 1)
            for g, (dst, n) in enumerate([(PCOL[:, 0:122], 122), (PCOL[:, 128:248], 120), (BMC[:, :], 96)]):
                act.wait_ge(pcol_pe, g + 1)
                act.activation(dst, M[g][:, 0:n], ACT.Copy).then_inc(pcol_done, 1)
            for r in range(8):
                act.wait_ge(xt_pe, r + 1)
                act.activation(XT[:, 2 * r:2 * r + 2, :], G[r % 4][:, :], ACT.Copy).then_inc(xt_act, 1)
            for n in range(AHEAD):
                split_hi(n)
            for kt in range(KT):
                act.wait_ge(h_new, kt + 1)
                act.activation(HHI[:, kt, :], HTMP[:, kt % 4, :], ACT.Copy).then_inc(h_hi, 1)

            def evac_in(b):
                act.wait_ge(w_used, (b + 1) * CH_IN)
                e, banks = evac[b % 2], pair(b)
                if b <= 3:
                    for i in range(4 if b < 3 else 2):
                        act.activation(PA[:, 4 * b + i, :], banks[i // 2][:, (i % 2) * T:(i % 2) * T + T],
                                       ACT.Copy, scale=OMU[:, 4 * b + i:4 * b + i + 1]).then_inc(mixed, 1)
                    if b == 3:
                        act.activation(BQI[:, :, :], banks[1][:, :], ACT.Copy).then_inc(e, 1)
                elif b in (4, 6):
                    for i in range(2):
                        act.activation((BQ if b == 4 else CQ)[:, 2 * i:2 * i + 2, :], banks[i][:, :], ACT.Copy,
                                       scale=HD ** -0.5).then_inc(e, 1)
                elif b == 5:
                    act.activation(BK[:, :, :], banks[0][:, :], ACT.Copy).then_inc(e, 1)
                    act.activation(BVW[:, :, :], banks[1][:, 0:256].rearrange("p (t n) -> p t n", t=2)[:, :, 0:68],
                                   ACT.Copy).then_inc(e, 1)
                elif b == 7:
                    for i in range(2):
                        act.activation(CK[:, 2 * i:2 * i + 2, :], banks[i][:, :], ACT.Copy).then_inc(e, 1)
                elif b in (8, 10):
                    for i in range(2):
                        act.activation((CV if b == 8 else DV)[:, i, :], banks[i][:, :], ACT.Copy).then_inc(e, 1)
                elif b == 11:
                    for i in range(2):
                        act.activation(DG[:, i, :], banks[i][:, :], ACT.Sigmoid).then_inc(gates, 1)

            def key_norms():
                act.wait_ge(evac[1], EV[3])
                act.activation(PA[0:64, 12, :], PA[0:64, 12, :], ACT.Tanh)
                act.activation(PA[:, 13, :], PA[:, 13, :], ACT.Sigmoid).then_inc(gates, 1)
                for u in range(UNITS):
                    act.activation(SQ[:, u, :], PA[:, 4 + u, :], ACT.Square, scale=pc("kk", u)).then_inc(kn_sq, 1)
                for i in range(2):
                    act.wait_ge(kn_pe, i + 1)
                    act.activation(RN[:, 2 * i:2 * i + 2, :], M[i][:, :], ACT.Sqrt).then_inc(kn_sqrt, 1)

            def rwkv(u, stage):
                def pe():
                    act.wait_ge(rw_pe, step(RW, stage, u))
                if stage == "lora":
                    pe()
                    act.activation(SIG[:, :], M[0][:, 0:T], ACT.Sigmoid, bias=pc("w0", u))
                    act.activation(AL[:, :], M[1][:, 0:T], ACT.Sigmoid, bias=pc("a0", u)).then_inc(rw_act, 1)
                    act.wait_ge(rw_dve, step(RW_DVE, "cum", u))
                    for i in range(2):
                        act.activation(EP[:, i, :], CU[:, i, :], ACT.Exp, scale=-KAPPA, bias=KMID[:, i:i + 1])
                        act.activation(EM[:, i, :], CU[:, i, 1:129], ACT.Exp, scale=KAPPA, bias=NKMID[:, i:i + 1])
                    act.activation(IMID, NKMID, ACT.Exp).then_inc(rw_act, 1)
                elif stage == "turn":
                    pe()
                    act.activation(TB[:, :, :, :], M[2][:, :], ACT.Copy)
                    act.activation(VTA[:, :, u * P:(u + 1) * P], M[3][:, 0:256], ACT.Copy)
                    act.activation(BON.rearrange("p (c h) -> p c h", c=2)[:, :, 2 * u:2 * u + 2],
                                   M[3][:, 256:260], ACT.Copy).then_inc(rw_act, 1)
                elif stage == "rhs0":
                    pe()
                    act.activation(RH[:, :], M[2][:, 0:128], ACT.Copy).then_inc(rw_act, 1)
                elif stage == "sa0":
                    pe()
                    act.activation(SA[:, :], M[3][:, 0:128], ACT.Copy).then_inc(rw_act, 1)
                elif stage == "state":
                    pe()
                    act.activation(YA[:, 0, u * P:(u + 1) * P], M[0][:, 0:128], ACT.Copy).then_inc(rw_act, 1)
                elif stage == "rhs1":
                    pe()
                    act.activation(RH[:, 0:64], M[2][:, 0:64], ACT.Copy)
                    act.activation(RH[:, 64:128], M[3][:, 0:64], ACT.Copy).then_inc(rw_act, 1)
                elif stage == "sa1":
                    pe()
                    act.activation(SA[:, :], M[0][:, 0:128], ACT.Copy).then_inc(rw_act, 1)
                elif stage == "y1":
                    pe()
                    act.activation(YA[:, 1, u * P:u * P + 64], M[2][:, 0:64], ACT.Copy)
                    act.activation(YA[:, 1, u * P + 64:(u + 1) * P], M[3][:, 0:64], ACT.Copy).then_inc(rw_act, 1)

            def head_norm(y, g):
                act.wait_ge(centred, g + 1)
                act.activation(YSQ[:, :, :], y[:, :, :], ACT.Square).then_inc(squared, 1)
                act.wait_ge(var_sum, g + 1)
                act.activation(RS, S2, ACT.Sqrt).then_inc(std_done, 1)

            def indexer():
                for i in range(8):
                    t = i // 4
                    act.wait_ge(ix_pe, i + 1)
                    if i >= 2:
                        act.wait_ge(ix_dve, i - 1)
                    w = P * (t + 1)
                    act.activation(RL[:, i % 2, 0:w], M[i % 2][:, 0:w], ACT.Relu).then_inc(ix_act, 1)

            def attention(g):
                for h in range(HEADS + 1):
                    if h < HEADS:
                        i = g * HEADS + h
                        act.wait_ge(at_max, i + 1)
                        if i >= 2:
                            act.wait_ge(at_turn, i - 1)
                        for t, (a, b) in enumerate([(0, 128), (128, 384)]):
                            k = g * 16 + t * 8 + h
                            ins = act.activation(PB[:, i % 2, a:b], M[i % 2][:, a:b], ACT.Exp,
                                                 bias=NM[:, 2 * h + t:2 * h + t + 1], accum_out=SUM[:, k:k + 1])
                        ins.then_inc(at_exp, 1)
                    if h >= 1:
                        i = g * HEADS + h - 1
                        act.wait_ge(at_turn, i + 1)
                        if i >= 2:
                            act.wait_ge(at_pv, i - 1)
                        act.activation(PTB[:, i % 2, :], M[2][:, 0:384], ACT.Copy).then_inc(at_pt, 1)

            def retention():
                act.wait_ge(ret_pv, HEADS)
                for t in range(2):
                    act.activation(YD[:, t, :], M[2 + t][:, :], ACT.Copy).then_inc(ret_y, 1)

            for n in range(N0_OUT):
                split_hi(n + AHEAD)
                if n % CH_IN == CH_IN - 1:
                    b = n // CH_IN
                    if b == 8:
                        evac_in(b)
                        for u in range(UNITS):
                            for stage in RW:
                                rwkv(u, stage)
                        head_norm(YA, 0)
                        act.wait_ge(a_done, 1)
                    else:
                        evac_in(b)
                    if b == 3:
                        key_norms()
            indexer()
            attention(0)
            act.wait_ge(bias_in, 16)
            attention(1)
            retention()
            head_norm(YD, 1)

            for r in range(8):
                act.wait_ge(y_pe, r + 1)
                act.activation(HHI[:, 2 * r:2 * r + 2, :], G[r % 4][:, :], ACT.Copy).then_inc(y_hi, 1)
            for nb in range(4):
                act.wait_ge(gb_pe, nb + 1)
                act.activation(GB1[:, nb * 512:(nb + 1) * 512], M[nb][:, :], ACT.Copy).then_inc(gb_act, 1)
            with act.Fori(0, N_OUT_BLOCKS) as b:
                for j in range(CH_IN):
                    split_hi_at(j % RING, b * (CH_IN // RING) + (N0_OUT + j + AHEAD) // RING,
                                b * CH_IN + (N0_OUT + j + AHEAD))
            for t in range(2):
                act.wait_ge(ln_var, t + 1)
                act.activation(MV[:, 4 * t + 2:4 * t + 3], MV[:, 4 * t + 1:4 * t + 2], ACT.Sqrt,
                               bias=EPS[:, 0:1]).then_inc(ln_std, 1)
            for kt in range(KT):
                act.wait_ge(h_new, KT + kt + 1)
                act.activation(HHI[:, kt, :], HTMP[:, kt % 4, :], ACT.Copy).then_inc(h_hi, 1)
            with act.Fori(0, N_UP) as i:
                for j in range(2 * CH_IN):
                    split_hi_at(j % RING, i * (2 * CH_IN // RING) + (N0_UP + j + AHEAD) // RING,
                                i * (2 * CH_IN) + (N0_UP + j + AHEAD))
                    if j == CH_IN - 1:
                        act.wait_ge(conv_cp, i + 1)
                        for k in range(4):
                            act.activation(GF[:, k, :], G[k // 2][:, (k % 2) * T:(k % 2) * T + T], ACT.Identity,
                                           scale=CONV[:, 4 + k:5 + k], bias=CONV[:, k:k + 1]).then_inc(g_pre, 1)
                        act.wait_ge(evac[0], i * 4 + (EV1[0] + 4))
                        act.activation(SF[:, :, :], GF[:, :, :], ACT.Sigmoid).then_inc(g_sig, 1)
                    if j == 2 * CH_IN - 1:
                        act.wait_ge(evac[1], i * 2 + (EV1[1] + 2))
                        act.activation(FHI[:, ds(i * 4, 4), :], GF[:, :, :], ACT.Copy).then_inc(f_hi, 1)
            for nb in range(4):
                act.wait_ge(gb_pe, 5 + nb)
                act.activation(GB2[:, nb * 512:(nb + 1) * 512], M[nb][:, :], ACT.Copy).then_inc(gb_act, 1)
            for n in range(N0_DOWN, N_ALL):
                split_hi(n + AHEAD)
            for t in range(2):
                act.wait_ge(ln_var, 3 + t)
                act.activation(MV[:, 4 * t + 2:4 * t + 3], MV[:, 4 * t + 1:4 * t + 2], ACT.Sqrt,
                               bias=EPS[:, 0:1]).then_inc(ln_std, 1)

        @block.vector
        def _(dve):
            own = [0, None]

            def mark(ins):
                own[0] += 1
                return ins.then_inc(dve_own, 1)

            def settle():
                dve.wait_ge(dve_own, own[0] if own[1] is None else own[1] + own[0])

            def split_lo(n):
                if n >= N_ALL:
                    return
                s = n % RING
                dve.wait_ge(hi_done, n + 1)
                if n // CH_IN == 5:
                    for (dst, src), (h, _) in zip(dup_views(WLO, s), dup_views(WHI, s)):
                        ins = dve.tensor_tensor(dst, src, h.bitcast(f32), ALU.subtract)
                    ins.then_inc(lo_done, 1)
                else:
                    dve.tensor_tensor(WLO[:, s, :, :], RAW[:, s, :, :], WHI[:, s, :, :].bitcast(f32),
                                      ALU.subtract).then_inc(lo_done, 1)
                return

            def split_lo_at(s, n):
                dve.wait_ge(hi_done, n + 1)
                dve.tensor_tensor(WLO[:, s, :, :], RAW[:, s, :, :], WHI[:, s, :, :].bitcast(f32),
                                  ALU.subtract).then_inc(lo_done, 1)

            def mod_add(m, t, turns=None):
                q = m * KT + t
                dve.wait_ge(mod_in[t % RING], 16 * (q // RING + 1))
                a, w, ck = ACC[:, m % 2, :], MODR[:, t % RING, :], CC[:, t:t + 1]
                if t == 0:
                    if m >= 2:
                        dve.wait_ge(mod_sum, m - 1)
                    ins = dve.tensor_scalar(a, w, ck, None, ALU.mult)
                else:
                    dve.wait_ge(mod_done, q)
                    ins = dve.scalar_tensor_tensor(a, w, ck, a, ALU.mult, ALU.add)
                ins.then_inc(mod_done, 1)

            def mod_cols(m):
                dve.wait_ge(mod_sum, m + 1)
                dve.tensor_tensor(MC[:, 8 * m:8 * m + 8], M[3][:, 0:8], BMC[:, 8 * m:8 * m + 8], ALU.add)\
                   .then_inc(mod_col, 1)

            dve.wait_ge(silu_c, 1)
            dve.wait_ge(c_in, 16)
            mark(dve.tensor_tensor(CC, CCOL, CSG, ALU.mult))
            settle()
            for t in range(KT):
                mod_add(0, t)
            dve.wait_ge(pcol_done, 3)
            mark(dve.tensor_scalar(OMU, PCOL[:, 0:14], -1.0, 1.0, ALU.mult, ALU.add))
            mark(dve.tensor_scalar(BMC[:, SC1:SH2], BMC[:, SC1:SH2], 1.0, None, ALU.add))
            mark(dve.tensor_scalar(BMC[:, SC2:96], BMC[:, SC2:96], 1.0, None, ALU.add))
            settle()
            mod_cols(0)
            for m in range(1, 4):
                for t in range(KT):
                    mod_add(m, t)
                mod_cols(m)
            for n in range(AHEAD):
                split_lo(n)

            def h_split(kt, done):
                dve.wait_ge(h_hi, done + kt + 1)
                dve.tensor_tensor(HLO[:, kt, :], HTMP[:, kt % 4, :], HHI[:, kt, :].bitcast(f32), ALU.subtract)\
                   .then_inc(h_lo, 1)

            dve.wait_ge(mod_col, 4)
            dve.wait_ge(xt_act, 8)
            for kt in range(KT):
                if kt >= 4:
                    dve.wait_ge(h_lo, kt - 3)
                dve.tensor_scalar(HTMP[:, kt % 4, :], XT[:, kt, :], MC[:, SC1 + kt:SC1 + kt + 1],
                                  MC[:, SH1 + kt:SH1 + kt + 1], ALU.mult, ALU.add).then_inc(h_new, 1)
                if kt >= 2:
                    h_split(kt - 2, 0)
            h_split(KT - 2, 0)
            h_split(KT - 1, 0)

            def evac_in(b):
                e, banks = evac[b % 2], pair(b)
                if b <= 3:
                    for i in range(4 if b < 3 else 2):
                        j = 4 * b + i
                        dve.wait_ge(mixed, 4 * b + 2 * (i // 2) + 2)
                        dve.scalar_tensor_tensor(PA[:, j, 1:T], banks[i // 2][:, (i % 2) * T:(i % 2) * T + T - 1],
                                                 pc("mu", j), PA[:, j, 1:T], ALU.mult, ALU.add).then_inc(e, 1)
                elif b == 9:
                    dve.wait_ge(w_used, (b + 1) * CH_IN)
                    for i in range(2):
                        dve.tensor_tensor(DQK[:, 2 * i:2 * i + 2, :], banks[i][:, :],
                                          cf("decay", 1024)[:, i * 512:(i + 1) * 512], ALU.mult).then_inc(e, 1)
                elif b == 11:
                    dve.wait_ge(gates, 3)
                    for i in range(2):
                        dve.tensor_tensor(DG[:, i, :], DG[:, i, :], banks[i][:, :], ALU.mult).then_inc(e, 1)

            def key_norms():
                for i in range(2):
                    dve.wait_ge(kn_sqrt, i + 1)
                    r = RN[:, 2 * i:2 * i + 2, :]
                    mark(dve.tensor_scalar(r, r, 1e-12, None, ALU.max))
                    settle()
                    mark(dve.reciprocal(r, r))
                settle()

            def rwkv(u, stage):
                def done(ins):
                    ins.then_inc(rw_dve, 1)

                def pe():
                    dve.wait_ge(rw_pe, step(RW, stage, u))

                r, k = PA[:, u, :], PA[:, 4 + u, :]
                v4 = lambda t: t[:, :, :].rearrange("p (h c) n -> p h c n", h=2)
                two = lambda ap: ap.rearrange("p (c n) -> p c n", c=2)
                if stage == "lora":
                    dve.wait_ge(rw_act, step(RW_ACT, "gates", u))
                    for i in range(2):
                        s = SIG[:, i * P:(i + 1) * P]
                        mark(dve.tensor_tensor_scan(CU[:, i, 1:129], s, s, 0.0, ALU.add, ALU.bypass))
                    settle()
                    mark(dve.tensor_scalar(KMID, CU[:, :, 64], KAPPA, None, ALU.mult))
                    done(dve.tensor_scalar(NKMID, CU[:, :, 64], -KAPPA, None, ALU.mult))
                    mark(dve.scalar_tensor_tensor(KKN[:, :], k, pc("kk", u), RN[:, u, :], ALU.mult, ALU.mult))
                    mark(dve.tensor_scalar(TA[:, :], AL[:, :], -1.0, pc("ka", u), ALU.add, ALU.mult))
                    settle()
                    mark(dve.tensor_tensor(BH[:, :], KKN[:, :], AL[:, :], ALU.mult))
                    mark(dve.scalar_tensor_tensor(TA[:, :], TA[:, :], 1.0, k, ALU.add, ALU.mult))
                    dve.wait_ge(rw_act, step(RW_ACT, "decays", u))
                    settle()
                    mark(dve.scalar_tensor_tensor(AR[:, :, 0, :], two(KKN[:, :]), -1.0, EP[:, :, 0:128],
                                                  ALU.mult, ALU.mult))
                    mark(dve.tensor_tensor(AR[:, :, 1, :], two(r), EP[:, :, 1:129], ALU.mult))
                    mark(dve.tensor_tensor(BH[:, :], BH[:, :], EM[:, :, :].rearrange("p c n -> p (c n)"), ALU.mult))
                    mark(dve.tensor_tensor(KH[:, :], TA[:, :], EM[:, :, :].rearrange("p c n -> p (c n)"), ALU.mult))
                    done(dve.scalar_tensor_tensor(RK[:, :], r, pc("rk", u), TA[:, :], ALU.mult, ALU.mult))
                elif stage == "gram":
                    pe()
                    for h in range(2):
                        le = M[h][:, :].rearrange("p (c w n) -> p c w n", c=2, w=2)
                        mark(dve.tensor_tensor(LT[:, 2 * h:2 * h + 2, :], le[:, :, 0, :],
                                               cb("su").unsqueeze(1).broadcast_to((P, 2, P)), ALU.mult))
                        mark(dve.tensor_tensor(ET[:, 2 * h:2 * h + 2, :], le[:, :, 1, :],
                                               cb("iu").unsqueeze(1).broadcast_to((P, 2, P)), ALU.mult))
                        mark(dve.tensor_tensor(XI[:, 2 * h:2 * h + 2, :],
                                               M[2 + h][:, 0:256].rearrange("p (c n) -> p c n", c=2),
                                               cb("level").unsqueeze(1).broadcast_to((P, 2, P)), ALU.mult))
                    settle()
                    idb = IDENT.unsqueeze(1).broadcast_to((P, 4, P))
                    mark(dve.tensor_tensor(DT[:, :, :], LT[:, :, :],
                                           cb("level0t").unsqueeze(1).broadcast_to((P, 4, P)), ALU.mult))
                    mark(dve.tensor_tensor(DI[:, :, :], XI[:, :, :], idb, ALU.add))
                    settle()
                    done(dve.tensor_tensor(DT[:, :, :], DT[:, :, :], idb, ALU.add))
                elif stage.startswith("ld"):
                    pe()
                    done(dve.tensor_tensor(XI[:, :, :], M[2][:, :].rearrange("p (a n) -> p a n", a=4),
                                           cb("level", i=int(stage[2:])).unsqueeze(1).broadcast_to((P, 4, P)),
                                           ALU.mult))
                elif stage.startswith("dx"):
                    pe()
                    if stage != f"dx{LEVELS}":
                        mark(dve.tensor_tensor(DI[:, :, :].rearrange("p a n -> p (a n)"), M[0][:, :],
                                               DI[:, :, :].rearrange("p a n -> p (a n)"), ALU.add))
                    done(dve.tensor_tensor(DT[:, :, :].rearrange("p a n -> p (a n)"), M[1][:, :],
                                           DT[:, :, :].rearrange("p a n -> p (a n)"), ALU.add))
                elif stage == "gram2":
                    pe()
                    for h in range(2):
                        gf = M[h][:, :].rearrange("p (c w n) -> p c w n", c=2, w=2)
                        mark(dve.tensor_tensor(GTR[:, 2 * h:2 * h + 2, :], gf[:, :, 0, :],
                                               cb("su").unsqueeze(1).broadcast_to((P, 2, P)), ALU.mult))
                        ins = dve.tensor_tensor(FTR[:, 2 * h:2 * h + 2, :], gf[:, :, 1, :],
                                                cb("iu").unsqueeze(1).broadcast_to((P, 2, P)), ALU.mult)
                    done(ins)
                elif stage == "state":
                    pe()
                    for h in range(2):
                        p0 = 64 * h
                        ins = dve.tensor_scalar(MST[p0:p0 + 64, :], M[1][p0:p0 + 64, p0:p0 + 64],
                                                EP[p0:p0 + 64, 0, 128:129], IMID[p0:p0 + 64, 1:2],
                                                ALU.mult, ALU.mult)
                    done(ins)

            def head_norm(y, g, eps):
                yv = y[:, :, :].rearrange("p t (h n) -> p (t h) n", n=HD)
                sv = YSQ[:, :, :].rearrange("p t (h n) -> p (t h) n", n=HD)
                mark(dve.tensor_reduce(S1, yv, AX.X, ALU.add))
                settle()
                mark(dve.tensor_scalar(S1, S1, -1.0 / HD, None, ALU.mult))
                settle()
                dve.tensor_tensor(yv, yv, bc(S1, (P, 16, HD)), ALU.add).then_inc(centred, 1)
                dve.wait_ge(squared, g + 1)
                mark(dve.tensor_reduce(S2, sv, AX.X, ALU.add))
                settle()
                dve.tensor_scalar(S2, S2, 1.0 / HD, eps, ALU.mult, ALU.add).then_inc(var_sum, 1)
                dve.wait_ge(std_done, g + 1)
                mark(dve.reciprocal(RS, RS))
                settle()
                mark(dve.tensor_tensor(yv, yv, bc(RS, (P, 16, HD)), ALU.mult))
                settle()

            def finish_a():
                dve.wait_ge(rw_act, UNITS * len(RW_ACT))
                head_norm(YA, 0, A_EPS)
                ya = YA[:, :, :]
                mark(dve.tensor_tensor(VTA[:, :, :].rearrange("p t (h n) -> p (t h) n", n=HD),
                                       VTA[:, :, :].rearrange("p t (h n) -> p (t h) n", n=HD),
                                       bc(BON, (P, 16, HD)), ALU.mult))
                mark(dve.tensor_tensor(ya, ya, LNAG[:, :].unsqueeze(1).broadcast_to((P, 2, GW)), ALU.mult))
                settle()
                mark(dve.tensor_tensor(ya, ya, LNAB[:, :].unsqueeze(1).broadcast_to((P, 2, GW)), ALU.add))
                settle()
                mark(dve.tensor_tensor(ya, ya, VTA[:, :, :], ALU.add))
                settle()
                for t in range(2):
                    dve.wait_ge(a_gate, t + 1)
                    ins = dve.tensor_tensor(YA[:, t, :], M[t][:, :], YA[:, t, :], ALU.mult)
                ins.then_inc(a_done, 1)

            def indexer():
                dve.wait_ge(evac[1], EV[5])
                mark(dve.tensor_scalar(W4.rearrange("p (t h) -> p t h", t=2), BVW[:, :, 64:68],
                                       64 ** -0.5 * 4 ** -0.5, None, ALU.mult))
                settle()
                for t in range(2):
                    a, w = 128 * t, P * (t + 1)
                    sc = SC[:, a:a + w]
                    for h in range(4):
                        i = 4 * t + h
                        dve.wait_ge(ix_act, i + 1)
                        acc = CBT[:, CB["band"] + a:CB["band"] + a + w] if h == 0 else sc
                        if h:
                            dve.wait_ge(ix_dve, i)
                        dve.scalar_tensor_tensor(sc, RL[:, i % 2, 0:w], W4[:, i:i + 1], acc, ALU.mult, ALU.add)\
                           .then_inc(ix_dve, 1)
                    dve.wait_ge(ix_dve, 4 * t + 4)
                    for _ in range(TOPK // 8):
                        mark(dve.max(T8, sc))
                        settle()
                        mark(dve.match_replace(sc, T8, sc, TAKEN))
                        settle()
                    dve.tensor_scalar(SEL[:, a:a + w], sc, TAKEN, -BIG, ALU.not_equal, ALU.mult)\
                       .then_inc(sel_done, 1)

            def attention(g):
                for h in range(HEADS + 2):
                    if h < HEADS:
                        i = g * HEADS + h
                        dve.wait_ge(at_s, i + 1)
                        for t, (a, b) in enumerate([(0, 128), (128, 384)]):
                            ins = dve.tensor_reduce(NM[:, 2 * h + t:2 * h + t + 1], M[i % 2][:, a:b], AX.X, ALU.max,
                                                    negate=True)
                        ins.then_inc(at_max, 1)
                    if h in (5, 9):
                        h0 = h - 5
                        dve.wait_ge(at_pv, g * HEADS + h0 + 4)
                        if g or h0:
                            dve.wait_ge(at_y, 2 * g + h0 // 4)
                        ins = mark(dve.reciprocal(REC, SUM[:, 16 * g:16 * g + 16])) if h == 9 else \
                            mark(dve.reciprocal(REC.rearrange("p (t h) -> p t h", t=2)[:, :, 0:4],
                                                SUM[:, 16 * g:16 * g + 16].rearrange("p (t h) -> p t h", t=2)[:, :, 0:4]))
                        settle()
                        o = M[3][:, :].rearrange("p (h t n) -> p h t n", h=4, t=2)
                        for t in range(2):
                            ins = dve.tensor_tensor(
                                YG[1 + g][:, t, h0 * HD:(h0 + 4) * HD].rearrange("p (h n) -> p h n", n=HD),
                                o[:, :, t, :], bc(REC[:, 8 * t + h0:8 * t + h0 + 4], (P, 4, HD)), ALU.mult)
                        ins.then_inc(at_y, 1)

            def retention():
                for h in range(HEADS):
                    dve.wait_ge(ret_s, h + 1)
                    if h >= 2:
                        dve.wait_ge(ret_pv, h - 1)
                    dve.tensor_tensor(STD[:, h % 2, :], M[h % 2][:, 0:384], cb("ret", 384), ALU.mult)\
                       .then_inc(ret_m, 1)
                dve.wait_ge(ret_y, 2)
                head_norm(YD, 1, RET_EPS)
                dve.tensor_tensor(YD[:, :, :], YD[:, :, :], DG[:, :, :], ALU.mult).then_inc(d_done, 1)

            for n in range(N0_OUT):
                split_lo(n + AHEAD)
                m, t = divmod(4 * KT + n, KT)
                mod_add(m, t)
                if t == 2 and m > 4:
                    mod_cols(m - 1)
                if n % CH_IN == CH_IN - 1:
                    b = n // CH_IN
                    evac_in(b)
                    if b == 3:
                        key_norms()
                    if b == 8:
                        dve.wait_ge(zeroed, 2)
                        dve.wait_ge(late_in, 96)
                        for u in range(UNITS):
                            for stage in RW:
                                rwkv(u, stage)
                        finish_a()
            indexer()
            attention(0)
            attention(1)
            retention()
            for r in range(8):
                dve.wait_ge(y_hi, r + 1)
                dve.tensor_tensor(HLO[:, 2 * r:2 * r + 2, :].rearrange("p k n -> p (k n)"), G[r % 4][:, :],
                                  HHI[:, 2 * r:2 * r + 2, :].bitcast(f32).rearrange("p k n -> p (k n)"),
                                  ALU.subtract).then_inc(y_lo, 1)
            mod_cols(9)

            def gate_rows(col, dgm, done):
                for nb in range(4):
                    if nb >= 2:
                        dve.wait_ge(gb_pe, done + nb - 1)
                    dve.tensor_tensor(dgm[:, nb % 2, :].rearrange("p (a n) -> p a n", a=4),
                                      IDENT.unsqueeze(1).broadcast_to((P, 4, P)),
                                      bc(MC[:, col + 4 * nb:col + 4 * nb + 4], (P, 4, P)), ALU.mult)\
                       .then_inc(gb_dve, 1)

            dve.wait_ge(mod_col, 10)
            gate_rows(GT1, DGM1, 0)
            dve.wait_ge(gb_act, 4)
            dve.wait_ge(lnp_in, 64)

            OWN_OUT = 8
            n_own = own[0]
            with dve.Fori(0, N_OUT_BLOCKS // 2) as i:
                own[0], own[1] = n_own, i * OWN_OUT
                for j in range(2 * CH_IN):
                    split_lo_at(j % RING, i * (2 * CH_IN) + (N0_OUT + j + AHEAD))
                    dve.wait_ge(mod_in[j % RING], i * 64 + 16 * (10 * KT // RING + j // RING + 1))
                    a, w, ck = ACC[:, 0, :], MODR[:, j % RING, :], CC[:, j:j + 1]
                    if j == 0:
                        dve.wait_ge(mod_sum, i * 2 + 9)
                        dve.tensor_scalar(a, w, ck, None, ALU.mult).then_inc(mod_done, 1)
                    else:
                        dve.wait_ge(mod_done, i * KT + (10 * KT + j))
                        dve.scalar_tensor_tensor(a, w, ck, a, ALU.mult, ALU.add).then_inc(mod_done, 1)
                    if j % CH_IN == CH_IN - 1:
                        bb = j // CH_IN
                        for t in range(2):
                            at = ds(i * 1024 + bb * 512, 512)
                            mark(dve.tensor_tensor(ZT1[:, :], G[2 * bb + t][:, :], GB1[:, at], ALU.mult))
                            settle()
                            mark(dve.scalar_tensor_tensor(X1[:, t, at], XR[:, t, at], ALPHA, ZT1[:, :],
                                                          ALU.mult, ALU.add))
                            settle()
                            dve.bn_stats(BST[:, ds(i * 12 + (t * 24 + bb * 6), 6)], X1[:, t, at])\
                               .then_inc(evac[bb], 1)
                        if bb == 1:
                            dve.wait_ge(mod_sum, i + 11)
                            dve.tensor_tensor(MC[:, ds(i * 8 + 80, 8)], M[3][:, 0:8], BMC[:, ds(i * 8 + 80, 8)],
                                              ALU.add).then_inc(mod_col, 1)
                assert own[0] - n_own == OWN_OUT
            own[0], own[1] = n_own + OWN_OUT * (N_OUT_BLOCKS // 2), None

            def layer_stats(t, done):
                dve.bn_aggr(MV[:, 4 * t:4 * t + 2], BST[:, 24 * t:24 * t + 24]).then_inc(ln_var, 1)

            def normalise(t, done):
                dve.wait_ge(ln_std, done + t + 1)
                mark(dve.reciprocal(MV[:, 4 * t + 3:4 * t + 4], MV[:, 4 * t + 2:4 * t + 3]))
                settle()
                return dve.tensor_scalar(X1[:, t, :], X1[:, t, :], MV[:, 4 * t:4 * t + 1],
                                         MV[:, 4 * t + 3:4 * t + 4], ALU.subtract, ALU.mult)

            dve.wait_ge(evac[0], EV1[0])
            dve.wait_ge(evac[1], EV1[1])
            for t in range(2):
                layer_stats(t, 0)
            dve.wait_ge(mod_col, 12)
            mark(dve.tensor_tensor(SCG, PCOL[:, PR["ln1_g"]:PR["ln1_g"] + KT], MC[:, SC2:SC2 + KT], ALU.mult))
            mark(dve.tensor_tensor(SHB, PCOL[:, PR["ln1_b"]:PR["ln1_b"] + KT], MC[:, SC2:SC2 + KT], ALU.mult))
            settle()
            mark(dve.tensor_tensor(SHB, SHB, MC[:, SH2:SH2 + KT], ALU.add))
            for t in range(2):
                normalise(t, 0).then_inc(zn_done, 1)
            settle()
            for kt in range(KT):
                if kt % 2 == 0:
                    dve.wait_ge(zn_pe, kt // 2 + 1)
                if kt >= 4:
                    dve.wait_ge(h_lo, KT + kt - 3)
                dve.tensor_scalar(HTMP[:, kt % 4, :], G[kt // 2 % 4][:, (kt % 2) * T:(kt % 2) * T + T],
                                  SCG[:, kt:kt + 1], SHB[:, kt:kt + 1], ALU.mult, ALU.add).then_inc(h_new, 1)
                if kt >= 2:
                    h_split(kt - 2, KT)
            h_split(KT - 2, KT)
            h_split(KT - 1, KT)
            for t in range(2):
                mark(dve.tensor_tensor(X1[:, t, :], X1[:, t, :], LN1G[:, :], ALU.mult))
            settle()
            for t in range(2):
                mark(dve.tensor_tensor(X1[:, t, :], X1[:, t, :], LN1B[:, :], ALU.add))
            settle()

            OWN_UP = 5
            n_own = own[0]
            with dve.Fori(0, N_UP) as i:
                own[0], own[1] = n_own, i * OWN_UP
                for j in range(2 * CH_IN):
                    split_lo_at(j % RING, i * (2 * CH_IN) + (N0_UP + j + AHEAD))
                    if j == 0:
                        dve.wait_ge(evac[0], i * 4 + EV1[0])
                        for k, name in enumerate(("conv_b", "conv2", "conv1", "conv0")):
                            ins = dve.tensor_copy(CONV[:, 4 * k:4 * k + 4], PCOL[:, ds(i * 4 + PR[name], 4)])
                        ins.then_inc(conv_cp, 1)
                    if j == CH_IN - 1:
                        dve.wait_ge(conv_cp, i + 1)
                        for k in range(4):
                            g = G[k // 2][:, (k % 2) * T:(k % 2) * T + T]
                            dve.wait_ge(g_pre, i * 4 + (2 * (k // 2) + 2))
                            mark(dve.scalar_tensor_tensor(GF[:, k, 1:T], g[:, 0:T - 1], CONV[:, 8 + k:9 + k],
                                                          GF[:, k, 1:T], ALU.mult, ALU.add))
                        settle()
                        for k in range(4):
                            g = G[k // 2][:, (k % 2) * T:(k % 2) * T + T]
                            dve.scalar_tensor_tensor(GF[:, k, 2:T], g[:, 0:T - 2], CONV[:, 12 + k:13 + k],
                                                     GF[:, k, 2:T], ALU.mult, ALU.add).then_inc(evac[0], 1)
                    if j == 2 * CH_IN - 1:
                        dve.wait_ge(evac[0], i * 4 + (EV1[0] + 4))
                        dve.wait_ge(g_sig, i + 1)
                        gf, sf = GF[:, :, :].rearrange("p k n -> p (k n)"), SF[:, :, :].rearrange("p k n -> p (k n)")
                        mark(dve.tensor_tensor(gf, gf, sf, ALU.mult))
                        settle()
                        dve.wait_ge(w_used, i * (2 * CH_IN) + (N0_UP + 2 * CH_IN))
                        for k in range(2):
                            dve.tensor_tensor(gf[:, 512 * k:512 * k + 512], G[2 + k][:, :],
                                              gf[:, 512 * k:512 * k + 512], ALU.mult).then_inc(evac[1], 1)
                        dve.wait_ge(evac[1], i * 2 + (EV1[1] + 2))
                        dve.wait_ge(f_hi, i + 1)
                        dve.tensor_tensor(FLO[:, ds(i * 4, 4), :], GF[:, :, :], FHI[:, ds(i * 4, 4), :].bitcast(f32),
                                          ALU.subtract).then_inc(f_lo, 1)
                assert own[0] - n_own == OWN_UP, own[0] - n_own
            own[0], own[1] = n_own + OWN_UP * N_UP, None

            gate_rows(GT2, DGM2, 4)
            dve.wait_ge(gb_act, 8)
            for b in range(N_DOWN_BLOCKS):
                for j in range(CH_DOWN):
                    n = N0_DOWN + b * CH_DOWN + j
                    split_lo(n + AHEAD)
                at = slice(b * 512, (b + 1) * 512)
                dve.wait_ge(w_used, N0_DOWN + (b + 1) * CH_DOWN)
                for t in range(2):
                    mark(dve.tensor_tensor(ZT2[:, :], G[2 * (b % 2) + t][:, :], GB2[:, at], ALU.mult))
                    settle()
                    mark(dve.scalar_tensor_tensor(X1[:, t, at], X1[:, t, at], ALPHA, ZT2[:, :], ALU.mult, ALU.add))
                    settle()
                    mark(dve.bn_stats(BST[:, t * 24 + b * 6:t * 24 + b * 6 + 6], X1[:, t, at])) if b >= 2 else \
                        dve.bn_stats(BST[:, t * 24 + b * 6:t * 24 + b * 6 + 6], X1[:, t, at]).then_inc(evac[b % 2], 1)
            settle()
            dve.wait_ge(evac[1], EV2[1] + 2)
            dve.wait_ge(evac[0], EV2[0] + 2)
            for t in range(2):
                layer_stats(t, 2)
            dve.wait_ge(ln2_in, 32)
            for t in range(2):
                mark(normalise(t, 2))
                settle()
                mark(dve.tensor_tensor(X1[:, t, :], X1[:, t, :], LN2G[:, :], ALU.mult))
                settle()
                dve.tensor_tensor(X1[:, t, :], X1[:, t, :], LN2B[:, :], ALU.add).then_inc(out_ready, 1)

        @block.tensor
        def _(pe):
            def mm(out_, l, r, start=False, stop=False):
                return pe.matmul(out_, l, r, start=start, stop=stop, skip_group_check=True)

            def fm(s, kk, kt, banks, start, stop, tiles=4):
                for i in range(tiles):
                    o = banks[i // 2][:, (i % 2) * T:(i % 2) * T + T]
                    wh, wl = (w[:, s, kk, i * P:(i + 1) * P] for w in (WHI, WLO))
                    mm(o, wh, HHI[:, kt, :], start=start and i % 2 == 0)
                    mm(o, wh, HLO[:, kt, :])
                    ins = mm(o, wl, HHI[:, kt, :], stop=stop)
                return ins

            def tm(s, kk, kt, banks, start, stop, ahi=None, alo=None):
                ahi, alo = (HHI, HLO) if ahi is None else (ahi, alo)
                for t in range(2):
                    lh, ll = (a[:, kt, t * P:(t + 1) * P] for a in (ahi, alo))
                    mm(banks[t][:, :], lh, WHI[:, s, kk, :], start=start)
                    mm(banks[t][:, :], lh, WLO[:, s, kk, :])
                    ins = mm(banks[t][:, :], ll, WHI[:, s, kk, :], stop=stop)
                return ins

            def mod_reduce(m, i=None):
                for q in range(8):
                    ins = mm(M[3][:, q:q + 1], ACC[:, m % 2, q * P:(q + 1) * P], ONES[:, 0:1], start=True, stop=True)
                ins.then_inc(mod_sum, 1)

            pe.wait_ge(cf_in, 16)
            pe.wait_ge(prow_in, 16 * 13)
            for g, n in enumerate((122, 120, 96)):
                pe.transpose(M[g][:, 0:n], PROW[0:n, g, :], IDENT[0:n, 0:n]).then_inc(pcol_pe, 1)
            pe.wait_ge(x_in, 32)
            for r in range(8):
                if r >= 4:
                    pe.wait_ge(xt_act, r - 3)
                for q in range(4):
                    kt, t = 2 * r + q // 2, q % 2
                    ins = pe.transpose(G[r % 4][:, q * P:(q + 1) * P], X0[:, t, kt * P:(kt + 1) * P], IDENT)
                ins.then_inc(xt_pe, 1)
            for m in range(4):
                pe.wait_ge(mod_done, (m + 1) * KT)
                if m:
                    pe.wait_ge(mod_col, m)
                mod_reduce(m)

            def w_in_chunk(n):
                b, j = divmod(n, CH_IN)
                s, banks = n % RING, pair(b)
                pe.wait_ge(lo_done, n + 1)
                if b == 0:
                    pe.wait_ge(h_lo, 2 * j + 2)
                    pe.wait_ge(xt_act, 8)
                elif b >= 2 and j == 0:
                    pe.wait_ge(evac[b % 2], EV[b - 2])
                for kk in range(2):
                    kt = 2 * j + kk
                    first, last = kt == 0, kt == KT - 1
                    if b in (8, 10, 11):
                        ins = tm(s, kk, kt, banks, first, last)
                    elif b == 5:
                        fm(s, kk, kt, banks, first, last, tiles=2)
                        for t in range(2):
                            o = banks[1][:, t * P:t * P + 68]
                            lh, ll = (a[:, kt, t * P:(t + 1) * P] for a in (HHI, HLO))
                            mm(o, lh, WHI[:, s, kk, 256:324], start=first and t == 0)
                            mm(o, lh, WLO[:, s, kk, 256:324])
                            ins = mm(o, ll, WHI[:, s, kk, 256:324], stop=last)
                    else:
                        ins = fm(s, kk, kt, banks, first, last)
                ins.then_inc(w_used, 1)

            def key_norms():
                pe.wait_ge(mod_col, 4)
                for i in range(2):
                    pe.wait_ge(kn_sq, 2 * i + 2)
                    for q in range(2):
                        ins = mm(M[i][:, q * T:(q + 1) * T], HEADS2, SQ[:, 2 * i + q, :], start=q == 0, stop=True)
                    ins.then_inc(kn_pe, 1)

            rows = [slice(0, 64), slice(64, 128)]

            def rwkv(u, stage):
                def after_dve(name):
                    pe.wait_ge(rw_dve, step(RW_DVE, name, u))

                def after_act(name):
                    pe.wait_ge(rw_act, step(RW_ACT, name, u))

                def prob(h, i):
                    return 2 * h + i

                cu = slice(u * P, (u + 1) * P)
                if stage == "lora":
                    if u:
                        pe.wait_ge(rw_act, step(RW_ACT, "y1", u - 1))
                    else:
                        pe.wait_ge(gates, 1)
                        pe.wait_ge(kn_sqrt, 2)
                        pe.wait_ge(late_in, 96)
                        pe.wait_ge(mod_col, mod_before_rwkv)
                    for h in range(2):
                        ins = mm(M[h][:, 0:T], W2A2[rows[h], cu], PA[rows[h], 12, :], start=True, stop=True)
                elif stage == "turn":
                    after_dve("hats")
                    for q, src in enumerate((BH, KH)):
                        for i in range(2):
                            pe.transpose(M[2][:, (2 * q + i) * P:(2 * q + i + 1) * P], src[:, i * P:(i + 1) * P], IDENT)
                    for i in range(2):
                        pe.transpose(M[3][:, i * P:(i + 1) * P], PA[:, 8 + u, i * P:(i + 1) * P], IDENT)
                    for i in range(2):
                        ins = mm(M[3][:, 256 + 2 * i:258 + 2 * i], RK[:, i * P:(i + 1) * P], HEADS2[:, 0:128:64],
                                 start=True, stop=True)
                elif stage == "gram":
                    after_act("turned")
                    for h in range(2):
                        for i in range(2):
                            bh = BH[rows[h], i * P:(i + 1) * P]
                            mm(M[h][:, i * T:(i + 1) * T], bh, AR[rows[h], i, :, :], start=i == 0, stop=True)
                            ins = mm(M[2 + h][:, i * P:(i + 1) * P], AR[rows[h], i, 0, :], bh, start=i == 0, stop=True)
                elif stage.startswith("ld"):
                    l = int(stage[2:])
                    after_dve("inv0" if l == 1 else f"d{l - 1}")
                    for p in range(4):
                        ins = mm(M[2][:, p * P:(p + 1) * P], LT[:, p, :], DI[:, p, :], start=True, stop=True)
                elif stage.startswith("dx"):
                    l = int(stage[2:])
                    after_dve(f"x{l}")
                    for p in range(4):
                        if l < LEVELS:
                            mm(M[0][:, p * P:(p + 1) * P], DT[:, p, :], XI[:, p, :], start=True, stop=True)
                        ins = mm(M[1][:, p * P:(p + 1) * P], XI[:, p, :], DT[:, p, :], start=True, stop=True)
                elif stage == "gram2":
                    after_dve(f"d{LEVELS}")
                    for h in range(2):
                        for i in range(2):
                            ins = mm(M[h][:, i * T:(i + 1) * T], KH[rows[h], i * P:(i + 1) * P], AR[rows[h], i, :, :],
                                     start=i == 0, stop=True)
                elif stage == "rhs0":
                    after_dve("gf")
                    for h in range(2):
                        ins = mm(M[2][:, h * 64:h * 64 + 64], GTR[:, prob(h, 0), :],
                                 VTA[:, 0, u * P + h * 64:u * P + h * 64 + 64], start=True, stop=True)
                elif stage == "sa0":
                    after_act("rhs0")
                    for h in range(2):
                        ins = mm(M[3][:, h * 64:h * 64 + 64], DT[:, prob(h, 0), :], RH[:, h * 64:h * 64 + 64],
                                 start=True, stop=True)
                elif stage == "state":
                    after_act("sa0")
                    for h in range(2):
                        hc = slice(h * 64, h * 64 + 64)
                        mm(M[0][:, hc], ET[:, prob(h, 0), :], SA[:, hc], start=True)
                        mm(M[0][:, hc], FTR[:, prob(h, 0), :], VTA[:, 0, u * P + h * 64:u * P + h * 64 + 64], stop=True)
                    mm(M[1][:, 0:P], TB[:, 0, 0, :], SA[:, :], start=True)
                    ins = mm(M[1][:, 0:P], TB[:, 1, 0, :], VTA[:, 0, cu], stop=True)
                elif stage == "rhs1":
                    after_dve("state")
                    for h in range(2):
                        mm(M[2 + h][:, 0:64], AR[rows[h], 1, 0, :], MST[rows[h], :], start=True)
                        ins = mm(M[2 + h][:, 0:64], GTR[:, prob(h, 1), :],
                                 VTA[:, 1, u * P + h * 64:u * P + h * 64 + 64], stop=True)
                elif stage == "sa1":
                    after_act("rhs1")
                    for h in range(2):
                        ins = mm(M[0][:, h * 64:h * 64 + 64], DT[:, prob(h, 1), :], RH[:, h * 64:h * 64 + 64],
                                 start=True, stop=True)
                elif stage == "y1":
                    after_act("sa1")
                    for h in range(2):
                        hc = slice(h * 64, h * 64 + 64)
                        mm(M[2 + h][:, 0:64], AR[rows[h], 1, 1, :], MST[rows[h], :], start=True)
                        mm(M[2 + h][:, 0:64], ET[:, prob(h, 1), :], SA[:, hc])
                        ins = mm(M[2 + h][:, 0:64], FTR[:, prob(h, 1), :],
                                 VTA[:, 1, u * P + h * 64:u * P + h * 64 + 64], stop=True)
                ins.then_inc(rw_pe, 1)

            def finish_a():
                pe.wait_ge(rw_act, UNITS * len(RW_ACT))
                for t in range(2):
                    mm(M[t][:, :], PA[:, 13, t * P:(t + 1) * P], G2[:, :], start=True, stop=True).then_inc(a_gate, 1)

            def indexer():
                pe.wait_ge(evac[1], EV[5])
                pe.wait_ge(a_done, 1)
                for i in range(8):
                    t, h = divmod(i, 4)
                    if i >= 2:
                        pe.wait_ge(ix_act, i - 1)
                    w = P * (t + 1)
                    mm(M[h % 2][:, 0:w], BQI[rows[h % 2], h // 2, t * P:(t + 1) * P], BK[rows[h % 2], 1, 0:w],
                       start=True, stop=True).then_inc(ix_pe, 1)

            def attention(g):
                q_, k_ = (BQ, BK) if g == 0 else (CQ, CK)
                for h in range(HEADS + 2):
                    if h < HEADS:
                        i = g * HEADS + h
                        if i >= 2:
                            pe.wait_ge(at_exp, i - 1)
                        elif i == 0:
                            pe.wait_ge(ix_act, 8)
                            pe.wait_ge(sel_done, 2)
                        o, rh, kk = M[h % 2], rows[h % 2], (0 if g == 0 else h // 2)
                        if g == 0:
                            mm(o[:, 0:384], IDB, SEL[:, :], start=True)
                            mm(o[:, 0:384], cb("slope", i=h), cb("dist", 384))
                        else:
                            mm(o[:, 0:384], IDB, cb("band", 384), start=True)
                            mm(o[:, 0:128], BIA[:, h, 0:128], FLIP)
                            mm(o[:, 128:256], BIA[:, h, 128:256], FLIP)
                            mm(o[:, 256:384], BIA[:, h, 0:128], FLIP)
                        mm(o[:, 0:128], q_[rh, h // 2, 0:128], k_[rh, kk, 0:128])
                        mm(o[:, 128:384], q_[rh, h // 2, 128:256], k_[rh, kk, 0:256], stop=True).then_inc(at_s, 1)
                    if 1 <= h <= HEADS:
                        i = g * HEADS + h - 1
                        pe.wait_ge(at_exp, i + 1)
                        if i >= 1:
                            pe.wait_ge(at_pt, i)
                        for b in range(3):
                            ins = pe.transpose(M[2][:, b * P:(b + 1) * P], PB[:, i % 2, b * P:(b + 1) * P], IDENT)
                        ins.then_inc(at_turn, 1)
                    if h >= 2:
                        hh = h - 2
                        i = g * HEADS + hh
                        pe.wait_ge(at_pt, i + 1)
                        if hh % 4 == 0 and i:
                            pe.wait_ge(at_y, i // 4)
                        vals = [BVW[:, t, 0:64] for t in range(2)] if g == 0 else \
                            [CV[:, t, hh * HD:(hh + 1) * HD] for t in range(2)]
                        o = M[3][:, (hh % 4) * P:(hh % 4 + 1) * P]
                        mm(o[:, 0:64], PTB[:, i % 2, 0:128], vals[0], start=True, stop=True)
                        mm(o[:, 64:128], PTB[:, i % 2, 128:256], vals[0], start=True)
                        mm(o[:, 64:128], PTB[:, i % 2, 256:384], vals[1], stop=True).then_inc(at_pv, 1)

            def retention():
                pe.wait_ge(at_exp, 16)
                pe.wait_ge(at_pt, 16)
                pe.wait_ge(at_y, 4)
                pe.wait_ge(evac[0], EV[10])
                pe.wait_ge(evac[1], EV[11])
                for h in range(HEADS + 1):
                    if h < HEADS:
                        if h >= 2:
                            pe.wait_ge(ret_m, h - 1)
                        r, t = slice(32 * (h % 4), 32 * (h % 4) + 32), h // 4
                        o = M[h % 2]
                        mm(o[:, 0:256], DQK[r, 2 + t, 0:128], DQK[r, t, :], start=True, stop=True)
                        mm(o[:, 256:384], DQK[r, 2 + t, 128:256], DQK[r, t, 128:256], start=True, stop=True)\
                            .then_inc(ret_s, 1)
                    if h >= 1:
                        hh = h - 1
                        pe.wait_ge(ret_m, hh + 1)
                        hc, st = slice(hh * HD, (hh + 1) * HD), STD[:, hh % 2, :]
                        mm(M[2][:, hc], st[:, 0:128], DV[:, 0, hc], start=True, stop=True)
                        mm(M[3][:, hc], st[:, 128:256], DV[:, 0, hc], start=True)
                        mm(M[3][:, hc], st[:, 256:384], DV[:, 1, hc], stop=True).then_inc(ret_pv, 1)

            mod_before_rwkv = 8
            for n in range(N0_OUT):
                w_in_chunk(n)
                if n % KT == 1 and n > KT:
                    m = 4 + n // KT - 1
                    pe.wait_ge(mod_done, (m + 1) * KT)
                    if m >= 8:
                        pe.wait_ge(a_done, 1)
                    mod_reduce(m)
                if n == 4 * CH_IN + 3:
                    key_norms()
                if n == 9 * CH_IN - 1:
                    for u in range(UNITS):
                        for stage in RW:
                            rwkv(u, stage)
                    finish_a()
            indexer()
            attention(0)
            pe.wait_ge(bias_in, 16)
            attention(1)
            retention()

            pe.wait_ge(d_done, 1)
            for r in range(8):
                if r >= 4:
                    pe.wait_ge(y_lo, r - 3)
                for q in range(4):
                    kt, t = 2 * r + q // 2, q % 2
                    ins = pe.transpose(G[r % 4][:, q * P:(q + 1) * P], YG[kt // 4][:, t, (kt % 4) * P:(kt % 4 + 1) * P],
                                       IDENT)
                ins.then_inc(y_pe, 1)
            pe.wait_ge(mod_done, 10 * KT)
            mod_reduce(9)

            def gate_rows(dgm, done):
                for nb in range(4):
                    pe.wait_ge(gb_dve, done + nb + 1)
                    if nb == 3 and done == 0:
                        pe.wait_ge(mod_col, 10)
                    mm(M[nb][:, :], ONES, dgm[:, nb % 2, :], start=True, stop=True).then_inc(gb_pe, 1)

            gate_rows(DGM1, 0)
            pe.wait_ge(y_lo, 8)
            pe.wait_ge(gb_act, 4)
            with pe.Fori(0, N_OUT_BLOCKS // 2) as i:
                for bb in range(2):
                    pe.wait_ge(evac[bb], i * 2 + EV0[bb])
                    for j in range(CH_IN):
                        pe.wait_ge(lo_done, i * (2 * CH_IN) + (N0_OUT + bb * CH_IN + j + 1))
                        for kk in range(2):
                            kt = 2 * j + kk
                            ins = tm(j % RING, kk, kt, pair(bb), kt == 0, kt == KT - 1)
                        ins.then_inc(w_used, 1)
                pe.wait_ge(mod_done, i * KT + 11 * KT)
                pe.wait_ge(mod_col, i + 10)
                for q in range(8):
                    ins = mm(M[3][:, q:q + 1], ACC[:, 0, q * P:(q + 1) * P], ONES[:, 0:1], start=True, stop=True)
                ins.then_inc(mod_sum, 1)
            pe.wait_ge(zn_done, 2)
            for r in range(8):
                if r >= 4:
                    pe.wait_ge(h_new, KT + 2 * (r - 3))
                for q in range(4):
                    kt, t = 2 * r + q // 2, q % 2
                    ins = pe.transpose(G[r % 4][:, q * P:(q + 1) * P], X1[:, t, kt * P:(kt + 1) * P], IDENT)
                ins.then_inc(zn_pe, 1)
            pe.wait_ge(h_lo, 2 * KT)
            with pe.Fori(0, N_UP) as i:
                for half in range(2):
                    pe.wait_ge(evac[half], i * (4, 2)[half] + EV1[half])
                    for j in range(CH_IN):
                        pe.wait_ge(lo_done, i * (2 * CH_IN) + (N0_UP + half * CH_IN + j + 1))
                        for kk in range(2):
                            kt = 2 * j + kk
                            ins = fm(j % RING, kk, kt, pair(half), kt == 0, kt == KT - 1)
                        ins.then_inc(w_used, 1)
            gate_rows(DGM2, 4)
            pe.wait_ge(f_lo, N_UP)
            with pe.Fori(0, N_DOWN_BLOCKS // 2) as i:
                for bb in range(2):
                    pe.wait_ge(evac[bb], i * 2 + EV2[bb])
                    for j in range(CH_DOWN):
                        n = bb * CH_DOWN + j
                        pe.wait_ge(lo_done, i * (2 * CH_DOWN) + (N0_DOWN + n + 1))
                        for kk in range(2):
                            kt = 2 * j + kk
                            ins = tm(n % RING, kk, kt, pair(bb), kt == 0, kt == FT - 1, FHI, FLO)
                        ins.then_inc(w_used, 1)


_INS = ['x', 'c', 'w_mod', 'b_mod', 'w_in', 'rwkv_mu', 'rwkv_w0', 'rwkv_w2', 'rwkv_a0', 'rwkv_a2', 'rwkv_g2',
        'rwkv_kk', 'rwkv_ka', 'rwkv_rk', 'rwkv_ln_g', 'rwkv_ln_b', 'chunk_rel_bias', 'w_out', 'ln1_g', 'ln1_b',
        'w_up', 'conv_w', 'conv_b', 'w_down', 'ln2_g', 'ln2_b']


def _constants():
    import numpy as np
    p = np.arange(P)
    eye = np.eye(P)
    f = np.zeros((P, CF_W))
    f[:, 0:128] = eye
    f[:, 128:256] = 1.0
    f[:, 256:384] = (p[:, None] // HD) == (p[None, :] // HD)
    f[:, 384:512] = eye[:, ::-1]
    t = np.arange(T)
    for j in range(2):
        gamma = 1.0 - 2.0 ** (-5.0 - (4 * j + p // 32))
        f[:, 512 + j * T:512 + (j + 1) * T] = gamma[:, None] ** (t[None, :] - 128.0)
        f[:, 1024 + j * T:1024 + (j + 1) * T] = gamma[:, None] ** (128.0 - t[None, :]) * 32 ** -0.5
    b = np.zeros((P, CB_W))
    b[:, 0:128] = eye
    r, q = p[:, None], p[None, :]
    for l in range(LEVELS + 1):
        w = 2 ** l
        m = (r // (2 * w) == q // (2 * w)) & (r // w % 2 == 1) & (q // w % 2 == 0)
        b[:, CB["level"] + l * 128:CB["level"] + (l + 1) * 128] = m
        if l == 0:
            b[:, CB["level0t"]:CB["level0t"] + 128] = m.T
    b[:, CB["su"]:CB["su"] + 128] = r < q
    b[:, CB["iu"]:CB["iu"] + 128] = r <= q
    b[:, CB["ret"]:CB["ret"] + 384] = np.concatenate([r <= q, np.ones((P, P)), r <= q], 1)
    for h in range(HEADS):
        b[:, CB["slope"] + h * 128:CB["slope"] + (h + 1) * 128] = -eye * 2.0 ** -(h + 1)
    pairs = [(p, np.arange(P)), (p + P, np.arange(T))]
    b[:, CB["dist"]:CB["dist"] + 384] = np.concatenate([abs(a[:, None] - k[None, :]) for a, k in pairs], 1)
    b[:, CB["band"]:CB["band"] + 384] = np.concatenate(
        [np.where(k[None, :] < (a[:, None] // CHUNK + 1) * CHUNK, 0.0, -BIG) for a, k in pairs], 1)
    return f.astype(np.float32), (b.astype(np.float32).view(np.uint32) >> 16).astype(np.uint16)


def kernel(**inputs):
    import numpy as _np
    import concourse.bacc as _bacc
    from concourse import mybir as _mybir
    from concourse.bass_utils import run_bass_kernel_spmd as _run

    nc = _bacc.Bacc("TRN2", target_bir_lowering=False, num_devices=1)
    arrays, args = {}, []
    const_f, const_b = _constants()
    for name, a in [(n, inputs[n]) for n in _INS] + [("const_f", const_f), ("const_b", const_b)]:
        a = _np.ascontiguousarray(a)
        arrays[f"in_{name}_dram"] = a
        args.append(nc.dram_tensor(f"in_{name}_dram", a.shape, _mybir.dt.from_np(a.dtype), kind="ExternalInput").ap())
    args.append(nc.dram_tensor("out_0_dram", (1, T, D), _mybir.dt.float32, kind="ExternalOutput").ap())
    encoder_layer(nc, *args)
    r = _run(nc, [arrays], core_ids=[0])
    return r.results[0]["out_0_dram"]
```

```python
import concourse.bass as bass
from concourse import mybir
from contextlib import ExitStack

D, T, P = 2048, 256, 128
KT = D // P
CHUNK, HD = 64, 64
GW = 512
HEADS = GW // HD
D_FF = 256 * ((8 * D // 3 + 255) // 256)
FT = D_FF // P
A_COLS, B_COLS, C_COLS, D_COLS = 3 * GW + 256, GW + 2 * HD + 4 * 64 + 64 + 4, 3 * GW, 2 * 256 + 2 * GW
B0, C0, D0 = A_COLS, A_COLS + B_COLS, A_COLS + B_COLS + C_COLS
ALPHA = 2.0 ** 0.25
KAPPA = 0.6065306597126334
BIG = 1.0e30
TAKEN = -3.0e38
LN_EPS, A_EPS, RET_EPS = 1e-5, HD * 1e-5, 1e-5
TOPK = T // 4

RING = 4
AHEAD = 3
N_IN_BLOCKS, N_OUT_BLOCKS, N_UP, N_DOWN_BLOCKS = 12, 4, D_FF // 512, 4
CH_IN = KT // 2
CH_DOWN = FT // 2
N0_OUT = N_IN_BLOCKS * CH_IN
N0_UP = N0_OUT + N_OUT_BLOCKS * CH_IN
N0_DOWN = N0_UP + 2 * N_UP * CH_IN
N_ALL = N0_DOWN + N_DOWN_BLOCKS * CH_DOWN

MOD_W = 1024
MOD_PARTS = 6 * D // MOD_W
MODS_IN = (MOD_PARTS - 2) * KT
UP_MODS = 4
SH1, SC1, GT1, SH2, SC2, GT2 = (16 * i for i in range(6))

CF = dict(ident=0, ones=128, heads2=256, flip=384, decay=512)
CF_W = 512 + 1024
N_EVAC_IN = [4, 4, 4, 3, 2, 2, 2, 2, 2, 2, 2, 2]
LEVELS = 6
CB = dict(ident=0, level=128, level0t=128 + 7 * 128, su=128 + 8 * 128, iu=128 + 9 * 128,
          ret=128 + 10 * 128, slope=128 + 13 * 128, dist=128 + 21 * 128, band=128 + 24 * 128)
CB_W = 128 + 27 * 128
PR = dict(mu=0, w0=14, a0=18, kk=22, ka=26, rk=30, conv_b=34, conv2=34 + FT,
          conv0=128, conv1=128 + FT, ln1_g=128 + 2 * FT, ln1_b=128 + 2 * FT + 16)

RW = ["turn", "gram"] + [f"{s}{l}" for l in range(1, LEVELS + 1) for s in ("ld", "dx")] + \
     ["gram2", "rhs0", "sa0", "state", "rhs1", "sa1", "y1"]
RW_ACT = ["turned", "rhs0", "sa0", "y0", "rhs1", "sa1", "y1"]
RW_DVE = ["ar", "inv0"] + [f"{s}{l}" for l in range(1, LEVELS + 1) for s in ("x", "d")] + ["gf", "state"]
UNITS = HEADS // 2

SETUP = {(33, 0): "lora", (33, 1): "squares", (34, 0): "norms", (35, 0): "cumulate", (35, 1): "hats"}
RW_FROM = 36
RW_TO = RW_FROM + UNITS * len(RW) // 2
AT_FROM = RW_TO + 2
MIX = [("indexer", i) for i in range(4)] + [("attention", i) for i in range(2 * (HEADS + 2))] + \
      [("retention", i) for i in range(5)] + [("norm", i) for i in range(3)]
FINISH = ["sa0", "state", "rhs1", "y1"]


def rw_stage(n, half):
    k = 2 * (n - RW_FROM) + half
    return (k // len(RW), RW[k % len(RW)]) if 0 <= k < UNITS * len(RW) else (None, "")


def finish_step(n, half):
    u, stage = rw_stage(n, half)
    if u and stage in FINISH:
        return u - 1, FINISH.index(stage)
    k = 2 * (n - RW_TO) + half
    return (UNITS - 1, k) if 0 <= k < 4 else (None, None)


def mix_step(n, half):
    a = 2 * (n - AT_FROM) + half
    return MIX[a] if a >= 0 else (None, 0)


def mods_at(n, half):
    if n < RW_FROM:
        return int(half == 1 and n % 3 != 2)
    if n < RW_TO:
        stage = rw_stage(n, half)[1]
        return 2 if stage == "gram" else int(stage in ("turn", "gram2") or stage.startswith("dx"))
    return int(n >= AT_FROM)


def mod_turns():
    turns, part, q = {}, 4, 4 * KT
    for k in range(2 * N_IN_BLOCKS * CH_IN):
        stage = (k - 2 * RW_FROM) % len(RW)
        free = k < 60 or (3 <= stage <= 12 if k < 2 * RW_TO else k < 2 * AT_FROM + 4)
        if part <= 7 and q >= (part + 1) * KT and free:
            turns[divmod(k, 2)] = part
            part += 1
        q += mods_at(*divmod(k, 2))
    assert part == 8 and q == (MOD_PARTS - 2) * KT, (part, q)
    return turns


def step(names, name, u):
    return u * len(names) + names.index(name) + 1


def encoder_layer(nc, x, c, w_mod, b_mod, w_in, rwkv_mu, rwkv_w0, rwkv_w2, rwkv_a0, rwkv_a2, rwkv_g2,
                  rwkv_kk, rwkv_ka, rwkv_rk, rwkv_ln_g, rwkv_ln_b, chunk_rel_bias, w_out, ln1_g, ln1_b,
                  w_up, conv_w, conv_b, w_down, ln2_g, ln2_b, const_f, const_b, out):
    f32, f32r, bf16 = mybir.dt.float32, mybir.dt.float32r, mybir.dt.bfloat16
    ALU, ACT, AX = mybir.AluOpType, mybir.ActivationFunctionType, mybir.AxisListType
    ds = bass.ds
    base = (nc.sbuf_base + 63) // 64 * 64

    def sb(name, shape, off_kb, dt=f32):
        return nc.alloc_sbuf_tensor_at(name, shape, dt, offset=base + int(off_kb * 1024))

    RAW = sb("RAW", [P, RING, 2, 512], 0)
    WHI = sb("WHI", [P, RING, 2, 512], 16, f32r)
    WLO = sb("WLO", [P, RING, 2, 512], 32, f32r)
    HHI = sb("HHI", [P, KT, T], 48, f32r)
    HLO = sb("HLO", [P, KT, T], 64, f32r)
    LN2G, LN2B = sb("LN2G", [P, D], 48), sb("LN2B", [P, D], 56)
    GB2, DGM2, ZT2 = sb("GB2", [P, D], 64), sb("DGM2", [P, 4, 512], 168), sb("ZT2", [P, 512], 76)
    FHI = sb("FHI", [P, FT, T], 80, f32r)
    FLO = sb("FLO", [P, FT, T], 80 + FT, f32r)
    MODR = sb("MODR", [P, RING, MOD_W], 80)
    ACC = sb("ACC", [P, 2, MOD_W], 96)
    PA = sb("PA", [P, 14, T], 104)
    DQK, DV, DG = sb("DQK", [P, 4, T], 104), sb("DV", [P, 2, GW], 108), sb("DG", [P, 2, GW], 112)
    BQ, BK = sb("BQ", [P, 4, T], 118), sb("BK", [P, 2, T], 122)
    BQI, BVW = sb("BQI", [P, 2, T], 124), sb("BVW", [P, 2, 68], 126)
    CQ, CK, CV = sb("CQ", [P, 4, T], 127), sb("CK", [P, 4, T], 131), sb("CV", [P, 2, GW], 135)
    W2A2, G2 = sb("W2A2", [P, GW], 139), sb("G2", [P, GW], 141)
    LNAG, LNAB = sb("LNAG", [P, GW], 147), sb("LNAB", [P, GW], 173)
    AL = sb("AL", [P, UNITS, T], 143)
    EM, SIG = sb("EM", [P, 2, P], 149), sb("SIG", [P, UNITS, T], 168.25)
    KKN, TA = sb("KKN", [P, T], 150), sb("TA", [P, T], 151)
    CU, EP = sb("CU", [P, 2, 129], 152), sb("EP", [P, 2, 129], 153.0625)
    LT, DI, DT = sb("LT", [P, 4, P], 154.25), sb("DI", [P, 4, P], 156.25), sb("DT", [P, 4, P], 158.25)
    XI, ET = sb("XI", [P, 4, P], 160.25), sb("ET", [P, 4, P], 162.25)
    GTR, FTR = sb("GTR", [P, 4, P], 154.25), sb("FTR", [P, 4, P], 156.25)
    VTA = sb("VTA", [P, 2, GW], 164.25)
    YSU, YSQ = sb("YSU", [P, 2, P], 175), sb("YSQ", [P, 2, GW], 168.25)
    MST = sb("MST", [P, HD], 172.5)
    TB, RK = sb("TB", [P, 2, 2, P], 180), sb("RK", [P, T], 182)
    RH, SA = sb("RH", [P, P], 183), sb("SA", [P, P], 183.5)
    AR, BH, KH = sb("AR", [P, 2, 2, P], 184), sb("BH", [P, T], 186), sb("KH", [P, T], 187)
    RN, SQ = sb("RN", [P, 4, T], 188), sb("SQ", [P, 4, T], 154.25)
    PB, PTB = sb("PB", [P, 2, 384], 147), sb("PTB", [P, 2, 384], 150)
    SC, RL, SEL = sb("SC", [P, 384], 153), sb("RL", [P, 2, T], 154.5), sb("SEL", [P, 384], 156.5, bf16)
    STD, BIA = sb("STD", [P, 2, 384], 157.25), sb("BIA", [P, HEADS, T], 160.25)
    X0, X1 = sb("X0", [P, 2, D], 176), sb("X1", [P, 2, D], 176)
    YG = [sb(f"Y{g}", [P, 2, GW], 176 + 4 * i) for i, g in enumerate("ABCD")]
    YA, YD = YG[0], YG[3]
    XT, HTMP = sb("XT", [P, KT, T], 120), sb("HTMP", [P, 4, T], 172)
    XR, GB1 = sb("XR", [P, 2, D], 104), sb("GB1", [P, D], 120)
    DGM1, ZT1 = sb("DGM1", [P, 2, 512], 128), sb("ZT1", [P, 512], 132)
    LN1G, LN1B = sb("LN1G", [P, D], 80), sb("LN1B", [P, D], 88)
    ACC2, MODR2 = sb("ACC2", [P, 2, MOD_W], 144), sb("MODR2", [P, RING, MOD_W], 152)
    CFT = sb("CFT", [P, CF_W], 192)
    PCOL, BMC, MC = sb("PCOL", [P, 256], 198), sb("BMC", [P, 96], 199), sb("MC", [P, 96], 199.5)
    SM = sb("SM", [P, 224], 199.875)
    CBT = sb("CBT", [P, CB_W], 200.75, bf16)
    PROW = sb("PROW", [P, 3, P], 172)
    GF, SF = sb("GF", [P, 4, T], 194), sb("SF", [P, 4, T], 201)

    def cf(name, n=128):
        return CFT[:, CF[name]:CF[name] + n]

    def cb(name, n=128, i=0):
        return CBT[:, CB[name] + i * 128:CB[name] + i * 128 + n]

    def pc(name, i=0):
        return PCOL[:, PR[name] + i:PR[name] + i + 1]

    def bc(ap, shape):
        return ap.unsqueeze(len(shape) - 1).broadcast_to(shape)

    IDENT, ONES, HEADS2, FLIP = cf("ident"), cf("ones"), cf("heads2"), cf("flip")
    IDB = cb("ident")
    OMU, CC = SM[:, 0:14], SM[:, 16:32]
    KMID, NKMID, IMID = SM[:, 32:34], SM[:, 34:36], SM[:, 36:38]
    BON = SM[:, 40:56]
    NM, SUM, REC = SM[:, 56:72], SM[:, 72:104], SM[:, 104:120]
    S1, S2, RS = SM[:, 120:136], SM[:, 136:152], SM[:, 152:168]
    W4, T8, CSG, EPS = SM[:, 168:176], SM[:, 176:184], SM[:, 184:200], SM[:, 200:203]
    CCOL, CC4 = SM[:, 204:220], SM[:, 184:188]
    BST, MV = SM[:, 56:104], SM[:, 104:112]
    SCG, SHB, CONV = SM[:, 120:136], SM[:, 136:152], SM[:, 152:168]
    SPARE = SM[:, 112:120]

    with ExitStack() as ctx:
        def sem(name):
            return ctx.enter_context(nc.semaphore(name))

        G = [ctx.enter_context(nc.psum_tensor(f"G{i}", [P, 512], f32)) for i in range(4)]
        M = [ctx.enter_context(nc.psum_tensor(f"M{i}", [P, 512], f32)) for i in range(4)]

        raw_in = [sem(f"raw_in{i}") for i in range(RING)]
        mod_in = [sem(f"mod_in{i}") for i in range(RING)]
        hi_done, lo_done = sem("hi_done"), sem("lo_done")
        w_used = sem("w_used")
        evac = [sem("evac_even"), sem("evac_odd")]
        mod_done, mod_sum, mod_col = sem("mod_done"), sem("mod_sum"), sem("mod_col")
        c_in, cf_in, x_in, prow_in = sem("c_in"), sem("cf_in"), sem("x_in"), sem("prow_in")
        late_in, lnp_in, ln2_in, bias_in = sem("late_in"), sem("lnp_in"), sem("ln2_in"), sem("bias_in")
        pcol_pe, pcol_done, silu_c = sem("pcol_pe"), sem("pcol_done"), sem("silu_c")
        xt_pe, xt_act = sem("xt_pe"), sem("xt_act")
        h_new, h_hi, h_lo = sem("h_new"), sem("h_hi"), sem("h_lo")
        mixed, gates = sem("mixed"), sem("gates")
        kn_sq, kn_pe, kn_sqrt, kn_done = sem("kn_sq"), sem("kn_pe"), sem("kn_sqrt"), sem("kn_done")
        rw_pe, rw_act, rw_dve = sem("rw_pe"), sem("rw_act"), sem("rw_dve")
        lora_pe, prep_dve, prep_act = sem("lora_pe"), sem("prep_dve"), sem("prep_act")
        lnab_in = sem("lnab_in")
        centred, squared, var_sum, std_done = sem("centred"), sem("squared"), sem("var_sum"), sem("std_done")
        a_gate, a_done = sem("a_gate"), sem("a_done")
        ix_pe, ix_act, ix_dve, sel_done = sem("ix_pe"), sem("ix_act"), sem("ix_dve"), sem("sel_done")
        at_s, at_max, at_exp, at_turn, at_pt, at_pv, at_y = (sem("at_" + n) for n in
                                                            ("s", "max", "exp", "turn", "pt", "pv", "y"))
        ret_s, ret_m, ret_pv, ret_y, d_done = (sem("ret_" + n) for n in ("s", "m", "pv", "y", "done"))
        y_pe, y_hi, y_lo = sem("y_pe"), sem("y_hi"), sem("y_lo")
        gb_dve, gb_pe, gb_act = sem("gb_dve"), sem("gb_pe"), sem("gb_act")
        ln_var, ln_std, zn_done, zn_pe = sem("ln_var"), sem("ln_std"), sem("zn_done"), sem("zn_pe")
        x1_done = sem("x1_done")
        conv_cp, g_pre, g_sig = sem("conv_cp"), sem("g_pre"), sem("g_sig")
        f_hi, f_lo = sem("f_hi"), sem("f_lo")
        out_ready, out_sent, scaled = [sem("out_ready0"), sem("out_ready1")], sem("out_sent"), sem("scaled")
        dve_own, zeroed = sem("dve_own"), sem("zeroed")

        EV = []
        for b in range(N_IN_BLOCKS):
            EV.append(N_EVAC_IN[b] + (EV[b - 2] if b >= 2 else 0))
        EV0 = EV[-2:]
        EV1 = [EV0[0] + 4, EV0[1] + 4]
        EV2 = [EV1[0] + 4 * N_UP, EV1[1] + 2 * N_UP]

        def raw_count(n):
            double = sum(1 for m in range(n % RING, n + 1, RING) if m // CH_IN in (3, 5))
            return 16 * (n // RING + 1 + double)

        RAW_SHIFT = raw_count(N0_OUT) - 16 * (N0_OUT // RING + 1)

        def pair(b):
            return G[2 * (b % 2)], G[2 * (b % 2) + 1]

        def dup_views(dst, s):
            d, r = dst[:, s, :, :], RAW[:, s, :, :]
            two = lambda lo: r[:, :, lo:lo + 64].unsqueeze(2).broadcast_to((P, 2, 2, 64))
            return [(d[:, :, 0:128].rearrange("p k (a n) -> p k a n", a=2), two(0)),
                    (d[:, :, 128:256].rearrange("p k (a n) -> p k a n", a=2), two(128)),
                    (d[:, :, 256:320], r[:, :, 64:128]), (d[:, :, 320:324], r[:, :, 192:196])]

        block = ctx.enter_context(nc.Block())

        @block.sync
        def _(sp):
            sp.dma_start(CCOL, c.rearrange("a (p t) -> (a p) t", t=KT)).then_inc(c_in, 16)
            sp.dma_start(CFT[:, :], const_f).then_inc(cf_in, 16)
            xv = x.rearrange("a (t p) d -> (a p) t d", p=P)
            for t in range(2):
                sp.dma_start(X0[:, t, :], xv[:, t, :]).then_inc(x_in, 16)
            r128 = lambda ap: ap.rearrange("a (j p) -> (a j) p", p=P)
            cw = lambda i: conv_w[0, i, :].rearrange("(j p) -> j p", p=P)
            for g, name, src, n in [
                    (0, "mu", r128(rwkv_mu), 14), (0, "w0", r128(rwkv_w0), 4), (0, "a0", r128(rwkv_a0), 4),
                    (0, "kk", r128(rwkv_kk), 4), (0, "ka", r128(rwkv_ka), 4),
                    (0, "rk", rwkv_rk.rearrange("a (j h) d -> (a j) (h d)", h=2), 4),
                    (0, "conv_b", r128(conv_b), FT), (0, "conv2", cw(2), FT), (1, "conv0", cw(0), FT),
                    (1, "conv1", cw(1), FT), (1, "ln1_g", r128(ln1_g), KT), (1, "ln1_b", r128(ln1_b), KT)]:
                r = PR[name] - 128 * g
                sp.dma_start(PROW[r:r + n, g, :], src).then_inc(prow_in, 16)
            sp.dma_start(PROW[0:96, 2, :], r128(b_mod)).then_inc(prow_in, 16)
            sp.dma_start(CBT[:, :], const_b.bitcast(bf16)).then_inc(late_in, 16)
            sp.dma_start(W2A2[0:64, :], rwkv_w2[0]).then_inc(late_in, 16)
            sp.dma_start(W2A2[64:128, :], rwkv_a2[0]).then_inc(late_in, 16)
            sp.dma_start(G2[:, :], rwkv_g2[0]).then_inc(late_in, 16)
            sp.dma_start(LNAG[:, :], rwkv_ln_g[0, :].partition_broadcast(P)).then_inc(late_in, 16)

            wi, wo, wu, wd = (w[0].rearrange("(t p) n -> p t n", p=P) for w in (w_in, w_out, w_up, w_down))
            bkv, bqi = B0 + GW, B0 + GW + 2 * HD
            cols = [[(0, GW)], [(GW, GW)], [(2 * GW, GW)], [(3 * GW, 256), (bqi, 256)], [(B0, GW)],
                    [(bkv, 128), (bqi + 256, 68)], [(C0, GW)], [(C0 + GW, GW)], [(C0 + 2 * GW, GW)],
                    [(D0, GW)], [(D0 + GW, GW)], [(D0 + 2 * GW, GW)]]

            def load_bias():
                sp.wait_ge(a_done, 1)
                sp.dma_start(BIA[:, :, :], bass.AP(tensor=chunk_rel_bias.tensor, offset=129,
                                                   ap=[[1, P], [513, HEADS], [1, T]])).then_inc(bias_in, 16)

            for n in range(N0_OUT):
                b, j = divmod(n, CH_IN)
                if n == CH_IN:
                    sp.wait_ge(h_lo, KT)
                    sp.dma_start(LNAB[:, :], rwkv_ln_b[0, :].partition_broadcast(P)).then_inc(lnab_in, 16)
                if n >= RING:
                    sp.wait_ge(lo_done, n - RING + 1)
                at = 0
                for c0, w in cols[b]:
                    sp.dma_start(RAW[:, n % RING, :, at:at + w], wi[:, 2 * j:2 * j + 2, c0:c0 + w])\
                      .then_inc(raw_in[n % RING], 16)
                    at += w
                if n == AT_FROM + AHEAD:
                    load_bias()
            with sp.Fori(0, N_OUT_BLOCKS) as b:
                for j in range(CH_IN):
                    sp.wait_ge(lo_done, b * CH_IN + (N0_OUT + j - RING + 1))
                    sp.dma_start(RAW[:, j % RING, :, :], wo[:, 2 * j:2 * j + 2, ds(b * 512, 512)])\
                      .then_inc(raw_in[j % RING], 16)
            with sp.Fori(0, N_UP) as i:
                for j in range(2 * CH_IN):
                    half, jj = divmod(j, CH_IN)
                    sp.wait_ge(lo_done, i * (2 * CH_IN) + (N0_UP + j - RING + 1))
                    sp.dma_start(RAW[:, j % RING, :, :],
                                 wu[:, 2 * jj:2 * jj + 2, ds(i * 512 + half * D_FF, 512)])\
                      .then_inc(raw_in[j % RING], 16)
            for b in range(N_DOWN_BLOCKS):
                for j in range(CH_DOWN):
                    n = N0_DOWN + b * CH_DOWN + j
                    sp.wait_ge(lo_done, n - RING + 1)
                    sp.dma_start(RAW[:, n % RING, :, :], wd[:, 2 * j:2 * j + 2, b * 512:(b + 1) * 512])\
                      .then_inc(raw_in[n % RING], 16)
                if b == 0:
                    sp.wait_ge(w_used, N0_DOWN)
                    sp.dma_start(LN2G[:, :], ln2_g[0, :].partition_broadcast(P)).then_inc(ln2_in, 16)
                    sp.dma_start(LN2B[:, :], ln2_b[0, :].partition_broadcast(P)).then_inc(ln2_in, 16)
            ov = out.rearrange("a (t p) d -> (a p) t d", p=P)
            for n in range(4):
                t, cols = n // 2, slice(n % 2 * (D // 2), (n % 2 + 1) * (D // 2))
                sp.wait_ge(out_ready[t], n % 2 + 1)
                sp.dma_start(ov[:, t, cols], X1[:, t, cols]).then_inc(out_sent, 16)
            sp.wait_ge(out_sent, 64)

        @block.gpsimd
        def _(pool):
            pool.memset(CU[:, :, 0:1], 0.0).then_inc(zeroed, 1)
            pool.memset(EPS[:, 0:1], LN_EPS).then_inc(zeroed, 1)
            wm = w_mod[0].rearrange("(p t) n -> p t n", t=KT)
            for t in range(KT):
                if t >= RING:
                    pool.wait_ge(mod_done, t - RING + 1)
                pool.dma_start(MODR[:, t % RING, :], wm[:, t, 0:MOD_W]).then_inc(mod_in[t % RING], 16)


            def parts(first, last):
                with pool.Fori(first, last) as m:
                    for t in range(KT):
                        pool.wait_ge(mod_done, m * KT + (t - RING + 1))
                        pool.dma_start(MODR[:, t % RING, :], wm[:, t, ds(m * MOD_W, MOD_W)])\
                            .then_inc(mod_in[t % RING], 16)

            parts(1, MOD_PARTS - 2)
            pool.wait_ge(y_lo, 8)
            pool.wait_ge(mod_done, MODS_IN)
            pool.memset(ACC2[:, :, :], 0.0).then_inc(zeroed, 1)
            xv = x.rearrange("a (t p) d -> (a p) t d", p=P)
            for t in range(2):
                pool.dma_start(XR[:, t, :], xv[:, t, :]).then_inc(lnp_in, 16)
            pool.dma_start(LN1G[:, :], ln1_g[0, :].partition_broadcast(P)).then_inc(lnp_in, 16)
            pool.dma_start(LN1B[:, :], ln1_b[0, :].partition_broadcast(P)).then_inc(lnp_in, 16)
            def last_parts(i, ks):
                for k in ks:
                    pool.wait_ge(mod_done, i * 8 + (MODS_IN + k - RING + 1))
                    row, m = i * 4 + k // 2, MOD_PARTS - 2 + k % 2
                    pool.dma_start(MODR2[:, k % RING:k % RING + 1, :], wm[:, ds(row, 1), m * MOD_W:(m + 1) * MOD_W])\
                        .then_inc(mod_in[k % RING], 16)

            last_parts(0, range(RING))
            pool.wait_ge(zn_pe, 8)
            pool.wait_ge(zn_done, 2)
            for c0 in range(0, D, 512):
                for t in range(2):
                    pool.tensor_tensor(X1[:, t, c0:c0 + 512], X1[:, t, c0:c0 + 512], LN1G[:, c0:c0 + 512], ALU.mult)\
                        .then_inc(x1_done, 1)
            for n, c0 in enumerate(range(0, D, 512)):
                for t in range(2):
                    pool.wait_ge(x1_done, 2 * n + t + 1)
                    pool.tensor_tensor(X1[:, t, c0:c0 + 512], X1[:, t, c0:c0 + 512], LN1B[:, c0:c0 + 512], ALU.add)\
                        .then_inc(x1_done, 1)
            last_parts(0, range(RING, 8))
            with pool.Fori(1, UP_MODS) as i:
                last_parts(i, range(8))
            for n in range(2):
                cols = slice(n * (D // 2), (n + 1) * (D // 2))
                pool.wait_ge(scaled, n + 1)
                pool.tensor_tensor(X1[:, 1, cols], X1[:, 1, cols], LN2B[:, cols], ALU.add).then_inc(out_ready[1], 1)

        @block.scalar
        def _(act):
            def split_hi(n):
                if n >= N_ALL:
                    return
                s = n % RING
                act.wait_ge(raw_in[s], raw_count(n))
                if n >= RING:
                    act.wait_ge(w_used, n - RING + 1)
                if n // CH_IN == 5:
                    for dst, src in dup_views(WHI, s):
                        ins = act.activation(dst, src, ACT.Copy)
                    ins.then_inc(hi_done, 1)
                else:
                    act.activation(WHI[:, s, :, :], RAW[:, s, :, :], ACT.Copy).then_inc(hi_done, 1)

            def split_hi_at(s, groups, n):
                act.wait_ge(raw_in[s], groups * 16 + (RAW_SHIFT + 16))
                act.wait_ge(w_used, n + (1 - RING))
                act.activation(WHI[:, s, :, :], RAW[:, s, :, :], ACT.Copy).then_inc(hi_done, 1)

            act.wait_ge(c_in, 16)
            act.activation(CSG, CCOL, ACT.Sigmoid).then_inc(silu_c, 1)
            for g, (dst, n) in enumerate([(PCOL[:, 0:122], 122), (PCOL[:, 128:248], 120), (BMC[:, :], 96)]):
                act.wait_ge(pcol_pe, g + 1)
                act.activation(dst, M[g][:, 0:n], ACT.Copy).then_inc(pcol_done, 1)
            for r in range(8):
                act.wait_ge(xt_pe, r + 1)
                act.activation(XT[:, 2 * r:2 * r + 2, :], G[r % 4][:, :], ACT.Copy).then_inc(xt_act, 1)
            for n in range(AHEAD):
                split_hi(n)
            for kt in range(KT):
                act.wait_ge(h_new, kt + 1)
                act.activation(HHI[:, kt, :], HTMP[:, kt % 4, :], ACT.Copy).then_inc(h_hi, 1)

            def evac_in(b):
                act.wait_ge(w_used, (b + 1) * CH_IN)
                e, banks = evac[b % 2], pair(b)
                if b <= 3:
                    for i in range(4 if b < 3 else 2):
                        act.activation(PA[:, 4 * b + i, :], banks[i // 2][:, (i % 2) * T:(i % 2) * T + T],
                                       ACT.Copy, scale=OMU[:, 4 * b + i:4 * b + i + 1]).then_inc(mixed, 1)
                    if b == 3:
                        act.activation(BQI[:, :, :], banks[1][:, :], ACT.Copy).then_inc(e, 1)
                elif b in (4, 6):
                    for i in range(2):
                        act.activation((BQ if b == 4 else CQ)[:, 2 * i:2 * i + 2, :], banks[i][:, :], ACT.Copy,
                                       scale=HD ** -0.5).then_inc(e, 1)
                elif b == 5:
                    act.activation(BK[:, :, :], banks[0][:, :], ACT.Copy).then_inc(e, 1)
                    act.activation(BVW[:, :, :], banks[1][:, 0:256].rearrange("p (t n) -> p t n", t=2)[:, :, 0:68],
                                   ACT.Copy).then_inc(e, 1)
                elif b == 7:
                    for i in range(2):
                        act.activation(CK[:, 2 * i:2 * i + 2, :], banks[i][:, :], ACT.Copy).then_inc(e, 1)
                elif b in (8, 10):
                    for i in range(2):
                        act.activation((CV if b == 8 else DV)[:, i, :], banks[i][:, :], ACT.Copy).then_inc(e, 1)
                elif b == 11:
                    for i in range(2):
                        act.activation(DG[:, i, :], banks[i][:, :], ACT.Sigmoid).then_inc(gates, 1)

            def setup(what):
                if what == "lora":
                    act.wait_ge(evac[1], EV[3])
                    act.activation(PA[0:64, 12, :], PA[0:64, 12, :], ACT.Tanh).then_inc(gates, 1)
                    act.activation(PA[:, 13, :], PA[:, 13, :], ACT.Sigmoid)
                    act.wait_ge(lora_pe, 2)
                    for u in range(UNITS):
                        for dst, bias, bank in ((SIG, "w0", 0), (AL, "a0", 2)):
                            ins = act.activation(dst[:, u, :], M[bank + u // 2][:, (u % 2) * T:(u % 2) * T + T],
                                                 ACT.Sigmoid, bias=pc(bias, u))
                    ins.then_inc(gates, 1)
                elif what == "squares":
                    for u in range(UNITS):
                        act.activation(SQ[:, u, :], PA[:, 4 + u, :], ACT.Square, scale=pc("kk", u)).then_inc(kn_sq, 1)
                elif what == "norms":
                    for i in range(2):
                        act.wait_ge(kn_pe, i + 1)
                        act.activation(RN[:, 2 * i:2 * i + 2, :], M[i][:, :], ACT.Sqrt).then_inc(kn_sqrt, 1)
                elif what == "cumulate":
                    decays(0)

            def decays(u):
                act.wait_ge(prep_dve, 2 * u + 1)
                if u:
                    act.wait_ge(rw_dve, step(RW_DVE, "state", u - 1))
                for i in range(2):
                    act.activation(EP[:, i, :], CU[:, i, :], ACT.Exp, scale=-KAPPA, bias=KMID[:, i:i + 1])
                    act.activation(EM[:, i, :], CU[:, i, 1:129], ACT.Exp, scale=KAPPA, bias=NKMID[:, i:i + 1])
                act.activation(IMID, NKMID, ACT.Exp).then_inc(prep_act, 1)

            def rwkv(u, stage):
                def pe():
                    act.wait_ge(rw_pe, step(RW, stage, u))
                if stage == "turn":
                    pe()
                    act.activation(TB[:, :, :, :], M[2][:, :], ACT.Copy)
                    act.activation(VTA[:, :, u * P:(u + 1) * P], M[3][:, 0:256], ACT.Copy)
                    act.activation(BON.rearrange("p (c h) -> p c h", c=2)[:, :, 2 * u:2 * u + 2],
                                   M[3][:, 256:260], ACT.Copy).then_inc(rw_act, 1)
                elif stage == "rhs0":
                    pe()
                    act.activation(RH[:, :], M[2][:, 0:128], ACT.Copy).then_inc(rw_act, 1)
                elif stage == "sa0":
                    pe()
                    act.activation(SA[:, :], M[3][:, 0:128], ACT.Copy).then_inc(rw_act, 1)
                elif stage == "state":
                    pe()
                    act.activation(YA[:, 0, u * P:(u + 1) * P], M[0][:, 0:128], ACT.Copy).then_inc(rw_act, 1)
                elif stage == "rhs1":
                    pe()
                    act.activation(RH[:, 0:64], M[2][:, 0:64], ACT.Copy)
                    act.activation(RH[:, 64:128], M[3][:, 0:64], ACT.Copy).then_inc(rw_act, 1)
                    if u + 1 < UNITS:
                        decays(u + 1)
                elif stage == "sa1":
                    pe()
                    act.activation(SA[:, :], M[0][:, 0:128], ACT.Copy).then_inc(rw_act, 1)
                elif stage == "y1":
                    pe()
                    act.activation(YA[:, 1, u * P:u * P + 64], M[2][:, 0:64], ACT.Copy)
                    act.activation(YA[:, 1, u * P + 64:(u + 1) * P], M[3][:, 0:64], ACT.Copy).then_inc(rw_act, 1)

            def head_norm(part, y, squares, s, count):
                if part == 0:
                    act.wait_ge(centred, count)
                    act.activation(squares, y, ACT.Square).then_inc(squared, 1)
                else:
                    act.wait_ge(var_sum, count)
                    act.activation(RS[:, s], S2[:, s], ACT.Sqrt).then_inc(std_done, 1)

            def indexer(i):
                act.wait_ge(ix_pe, i + 1)
                if i >= 2:
                    act.wait_ge(ix_dve, i - 1)
                w = P * (i // 4 + 1)
                act.activation(RL[:, i % 2, 0:w], M[i % 2][:, 0:w], ACT.Relu).then_inc(ix_act, 1)

            def attention(g, h):
                if h < HEADS:
                    i = g * HEADS + h
                    act.wait_ge(at_max, i + 1)
                    if i >= 2:
                        act.wait_ge(at_turn, i - 1)
                    for t, (a, b) in enumerate([(0, 128), (128, 384)]):
                        k = g * 16 + t * 8 + h
                        ins = act.activation(PB[:, i % 2, a:b], M[i % 2][:, a:b], ACT.Exp,
                                             bias=NM[:, 2 * h + t:2 * h + t + 1], accum_out=SUM[:, k:k + 1])
                    ins.then_inc(at_exp, 1)
                if 1 <= h <= HEADS:
                    i = g * HEADS + h - 1
                    act.wait_ge(at_turn, i + 1)
                    if i >= 2:
                        act.wait_ge(at_pv, i - 1)
                    act.activation(PTB[:, i % 2, :], M[2][:, 0:384], ACT.Copy).then_inc(at_pt, 1)

            def retention(a):
                if a == 4:
                    act.wait_ge(ret_pv, HEADS)
                    for t in range(2):
                        act.activation(YD[:, t, :], M[2 + t][:, :], ACT.Copy).then_inc(ret_y, 1)

            def norm_d(part):
                if part < 2:
                    head_norm(part, YD[:, :, :], YSQ[:, :, :], slice(0, 16), UNITS + 1)

            for n in range(N0_OUT):
                for half in range(2):
                    if half == 1:
                        split_hi(n + AHEAD)
                    u, stage = rw_stage(n, half)
                    kind, a = mix_step(n, half)
                    if (n, half) in SETUP:
                        setup(SETUP[n, half])
                    elif stage:
                        rwkv(u, stage)
                    elif kind == "indexer":
                        indexer(2 * a)
                        indexer(2 * a + 1)
                    elif kind == "attention":
                        attention(*divmod(a, HEADS + 2))
                    elif kind == "retention":
                        retention(a)
                    elif kind == "norm":
                        norm_d(a)
                    u, f = finish_step(n, half)
                    if f in (0, 1):
                        head_norm(f, YA[:, :, u * P:(u + 1) * P], YSU[:, :, :], slice(4 * u, 4 * u + 4), u + 1)
                if n == 10 * CH_IN - 1:
                    act.wait_ge(a_done, 1)
                if n % CH_IN == CH_IN - 1:
                    evac_in(n // CH_IN)

            for r in range(8):
                if r == 4:
                    for nb in range(4):
                        act.wait_ge(gb_pe, nb + 1)
                        act.activation(GB1[:, nb * 512:(nb + 1) * 512], M[nb][:, :], ACT.Copy).then_inc(gb_act, 1)
                act.wait_ge(y_pe, r + 1)
                act.activation(HHI[:, 2 * r:2 * r + 2, :], G[r % 4][:, :], ACT.Copy).then_inc(y_hi, 1)
            with act.Fori(0, N_OUT_BLOCKS) as b:
                for j in range(CH_IN):
                    split_hi_at((j + AHEAD) % RING, b * (CH_IN // RING) + (N0_OUT + j + AHEAD) // RING,
                                b * CH_IN + (N0_OUT + j + AHEAD))
            for t in range(2):
                act.wait_ge(ln_var, t + 1)
                act.activation(MV[:, 4 * t + 2:4 * t + 3], MV[:, 4 * t + 1:4 * t + 2], ACT.Sqrt,
                               bias=EPS[:, 0:1]).then_inc(ln_std, 1)
            for kt in range(KT):
                act.wait_ge(h_new, KT + kt + 1)
                act.activation(HHI[:, kt, :], HTMP[:, kt % 4, :], ACT.Copy).then_inc(h_hi, 1)
            with act.Fori(0, N_UP) as i:
                for j in range(2 * CH_IN):
                    split_hi_at((j + AHEAD) % RING, i * (2 * CH_IN // RING) + (N0_UP + j + AHEAD) // RING,
                                i * (2 * CH_IN) + (N0_UP + j + AHEAD))
                    if j == CH_IN - 1:
                        act.wait_ge(w_used, i * (2 * CH_IN) + (N0_UP + CH_IN))
                        act.wait_ge(conv_cp, i + 1)
                        for k in range(4):
                            act.activation(GF[:, k, :], G[k // 2][:, (k % 2) * T:(k % 2) * T + T], ACT.Identity,
                                           scale=CONV[:, 4 + k:5 + k], bias=CONV[:, k:k + 1]).then_inc(g_pre, 1)
                        act.wait_ge(evac[0], i * 4 + (EV1[0] + 4))
                        act.activation(SF[:, :, :], GF[:, :, :], ACT.Sigmoid).then_inc(g_sig, 1)
                    if j == 2 * CH_IN - 1:
                        act.wait_ge(x1_done, 16)
                        act.wait_ge(evac[1], i * 2 + (EV1[1] + 2))
                        act.activation(FHI[:, ds(i * 4, 4), :], GF[:, :, :], ACT.Copy).then_inc(f_hi, 1)
            for n in range(N0_DOWN, N_ALL):
                split_hi(n + AHEAD)
                if n == N0_DOWN:
                    act.wait_ge(gb_pe, 8)
                    act.wait_ge(w_used, N0_DOWN)
                    for nb in range(4):
                        act.activation(GB2[:, nb * 512:(nb + 1) * 512], M[nb][:, :], ACT.Copy).then_inc(gb_act, 1)
            for t in range(2):
                act.wait_ge(ln_var, 3 + t)
                act.activation(MV[:, 4 * t + 2:4 * t + 3], MV[:, 4 * t + 1:4 * t + 2], ACT.Sqrt,
                               bias=EPS[:, 0:1]).then_inc(ln_std, 1)

        @block.vector
        def _(dve):
            own = [0, None]

            def mark(ins):
                own[0] += 1
                return ins.then_inc(dve_own, 1)

            def settle():
                dve.wait_ge(dve_own, own[0] if own[1] is None else own[1] + own[0])

            def split_lo(n):
                if n >= N_ALL:
                    return
                s = n % RING
                dve.wait_ge(hi_done, n + 1)
                if n // CH_IN == 5:
                    for (dst, src), (h, _) in zip(dup_views(WLO, s), dup_views(WHI, s)):
                        ins = dve.tensor_tensor(dst, src, h.bitcast(f32), ALU.subtract)
                    ins.then_inc(lo_done, 1)
                else:
                    dve.tensor_tensor(WLO[:, s, :, :], RAW[:, s, :, :], WHI[:, s, :, :].bitcast(f32),
                                      ALU.subtract).then_inc(lo_done, 1)
                return

            def split_lo_at(s, n):
                dve.wait_ge(hi_done, n + 1)
                dve.tensor_tensor(WLO[:, s, :, :], RAW[:, s, :, :], WHI[:, s, :, :].bitcast(f32),
                                  ALU.subtract).then_inc(lo_done, 1)

            def mod_add(m, t):
                q = m * KT + t
                dve.wait_ge(mod_in[t % RING], 16 * (q // RING + 1))
                a, w, ck = ACC[:, m % 2, :], MODR[:, t % RING, :], CC[:, t:t + 1]
                if t == 0:
                    if m >= 2:
                        dve.wait_ge(mod_sum, m - 1)
                    ins = dve.tensor_scalar(a, w, ck, None, ALU.mult)
                else:
                    dve.wait_ge(mod_done, q)
                    ins = dve.scalar_tensor_tensor(a, w, ck, a, ALU.mult, ALU.add)
                ins.then_inc(mod_done, 1)

            def mod_cols(m):
                dve.wait_ge(mod_sum, m + 1)
                dve.tensor_tensor(MC[:, 8 * m:8 * m + 8], M[3][:, 0:8], BMC[:, 8 * m:8 * m + 8], ALU.add)\
                   .then_inc(mod_col, 1)

            dve.wait_ge(silu_c, 1)
            dve.wait_ge(c_in, 16)
            mark(dve.tensor_tensor(CC, CCOL, CSG, ALU.mult))
            settle()
            for t in range(KT):
                mod_add(0, t)
            dve.wait_ge(pcol_done, 3)
            mark(dve.tensor_scalar(OMU, PCOL[:, 0:14], -1.0, 1.0, ALU.mult, ALU.add))
            mark(dve.tensor_scalar(BMC[:, SC1:SH2], BMC[:, SC1:SH2], 1.0, None, ALU.add))
            mark(dve.tensor_scalar(BMC[:, SC2:96], BMC[:, SC2:96], 1.0, None, ALU.add))
            settle()
            mod_cols(0)
            for m in range(1, 4):
                for t in range(KT):
                    mod_add(m, t)
                mod_cols(m)
            for n in range(AHEAD):
                split_lo(n)

            def h_split(kt, done):
                dve.wait_ge(h_hi, done + kt + 1)
                dve.tensor_tensor(HLO[:, kt, :], HTMP[:, kt % 4, :], HHI[:, kt, :].bitcast(f32), ALU.subtract)\
                   .then_inc(h_lo, 1)

            dve.wait_ge(mod_col, 4)
            dve.wait_ge(xt_act, 8)
            for kt in range(KT):
                if kt >= 4:
                    dve.wait_ge(h_lo, kt - 3)
                dve.tensor_scalar(HTMP[:, kt % 4, :], XT[:, kt, :], MC[:, SC1 + kt:SC1 + kt + 1],
                                  MC[:, SH1 + kt:SH1 + kt + 1], ALU.mult, ALU.add).then_inc(h_new, 1)
                if kt >= 2:
                    h_split(kt - 2, 0)
            h_split(KT - 2, 0)
            h_split(KT - 1, 0)

            def evac_in(b):
                e, banks = evac[b % 2], pair(b)
                if b <= 3:
                    for i in range(4 if b < 3 else 2):
                        j = 4 * b + i
                        dve.wait_ge(mixed, 4 * b + 2 * (i // 2) + 2)
                        dve.scalar_tensor_tensor(PA[:, j, 1:T], banks[i // 2][:, (i % 2) * T:(i % 2) * T + T - 1],
                                                 pc("mu", j), PA[:, j, 1:T], ALU.mult, ALU.add).then_inc(e, 1)
                elif b == 9:
                    dve.wait_ge(w_used, (b + 1) * CH_IN)
                    for i in range(2):
                        dve.tensor_tensor(DQK[:, 2 * i:2 * i + 2, :], banks[i][:, :],
                                          cf("decay", 1024)[:, i * 512:(i + 1) * 512], ALU.mult).then_inc(e, 1)
                elif b == 11:
                    dve.wait_ge(gates, 4)
                    for i in range(2):
                        dve.tensor_tensor(DG[:, i, :], DG[:, i, :], banks[i][:, :], ALU.mult).then_inc(e, 1)

            def setup(what):
                if what == "norms":
                    for i in range(2):
                        dve.wait_ge(kn_sqrt, i + 1)
                        r = RN[:, 2 * i:2 * i + 2, :]
                        mark(dve.tensor_scalar(r, r, 1e-12, None, ALU.max))
                        settle()
                        mark(dve.reciprocal(r, r))
                elif what == "cumulate":
                    dve.wait_ge(zeroed, 2)
                    dve.wait_ge(late_in, 80)
                    dve.wait_ge(gates, 2)
                    settle()
                    cumulate(0)
                elif what == "hats":
                    hats(0)

            def cumulate(u):
                r, k = PA[:, u, :], PA[:, 4 + u, :]
                for i in range(2):
                    s = SIG[:, u, i * P:(i + 1) * P]
                    mark(dve.tensor_tensor_scan(CU[:, i, 1:129], s, s, 0.0, ALU.add, ALU.bypass))
                mark(dve.scalar_tensor_tensor(KKN[:, :], k, pc("kk", u), RN[:, u, :], ALU.mult, ALU.mult))
                mark(dve.tensor_scalar(TA[:, :], AL[:, u, :], -1.0, pc("ka", u), ALU.add, ALU.mult))
                settle()
                mark(dve.tensor_scalar(KMID, CU[:, :, 64], KAPPA, None, ALU.mult))
                dve.tensor_scalar(NKMID, CU[:, :, 64], -KAPPA, None, ALU.mult).then_inc(prep_dve, 1)
                mark(dve.tensor_tensor(BH[:, :], KKN[:, :], AL[:, u, :], ALU.mult))
                mark(dve.scalar_tensor_tensor(TA[:, :], TA[:, :], 1.0, k, ALU.add, ALU.mult))

            def hats(u):
                settle()
                dve.wait_ge(prep_act, u + 1)
                em = EM[:, :, :].rearrange("p c n -> p (c n)")
                mark(dve.tensor_tensor(BH[:, :], BH[:, :], em, ALU.mult))
                mark(dve.tensor_tensor(KH[:, :], TA[:, :], em, ALU.mult))
                dve.scalar_tensor_tensor(RK[:, :], PA[:, u, :], pc("rk", u), TA[:, :], ALU.mult, ALU.mult)\
                   .then_inc(prep_dve, 1)

            def rwkv(u, stage):
                def done(ins):
                    ins.then_inc(rw_dve, 1)

                def pe():
                    dve.wait_ge(rw_pe, step(RW, stage, u))

                r = PA[:, u, :]
                two = lambda ap: ap.rearrange("p (c n) -> p c n", c=2)
                if stage == "turn":
                    if u:
                        dve.wait_ge(rw_pe, step(RW, "y1", u - 1))
                    mark(dve.scalar_tensor_tensor(AR[:, :, 0, :], two(KKN[:, :]), -1.0, EP[:, :, 0:128],
                                                  ALU.mult, ALU.mult))
                    done(dve.tensor_tensor(AR[:, :, 1, :], two(r), EP[:, :, 1:129], ALU.mult))
                elif stage == "gram":
                    pe()
                    for h in range(2):
                        le = M[h][:, :].rearrange("p (c w n) -> p c w n", c=2, w=2)
                        mark(dve.tensor_tensor(LT[:, 2 * h:2 * h + 2, :], le[:, :, 0, :],
                                               cb("su").unsqueeze(1).broadcast_to((P, 2, P)), ALU.mult))
                        mark(dve.tensor_tensor(ET[:, 2 * h:2 * h + 2, :], le[:, :, 1, :],
                                               cb("iu").unsqueeze(1).broadcast_to((P, 2, P)), ALU.mult))
                        mark(dve.tensor_tensor(XI[:, 2 * h:2 * h + 2, :],
                                               M[2 + h][:, 0:256].rearrange("p (c n) -> p c n", c=2),
                                               cb("level").unsqueeze(1).broadcast_to((P, 2, P)), ALU.mult))
                    settle()
                    idb = IDENT.unsqueeze(1).broadcast_to((P, 4, P))
                    mark(dve.tensor_tensor(DT[:, :, :], LT[:, :, :],
                                           cb("level0t").unsqueeze(1).broadcast_to((P, 4, P)), ALU.mult))
                    mark(dve.tensor_tensor(DI[:, :, :], XI[:, :, :], idb, ALU.add))
                    settle()
                    done(dve.tensor_tensor(DT[:, :, :], DT[:, :, :], idb, ALU.add))
                elif stage.startswith("ld"):
                    pe()
                    done(dve.tensor_tensor(XI[:, :, :], M[2][:, :].rearrange("p (a n) -> p a n", a=4),
                                           cb("level", i=int(stage[2:])).unsqueeze(1).broadcast_to((P, 4, P)),
                                           ALU.mult))
                elif stage.startswith("dx"):
                    pe()
                    last = stage == f"dx{LEVELS}"
                    if not last:
                        done(dve.tensor_tensor(DI[:, :, :].rearrange("p a n -> p (a n)"), M[0][:, :],
                                               DI[:, :, :].rearrange("p a n -> p (a n)"), ALU.add))
                    ins = dve.tensor_tensor(DT[:, :, :].rearrange("p a n -> p (a n)"), M[1][:, :],
                                            DT[:, :, :].rearrange("p a n -> p (a n)"), ALU.add)
                    done(ins) if last else mark(ins)
                elif stage == "gram2":
                    pe()
                    for h in range(2):
                        gf = M[h][:, :].rearrange("p (c w n) -> p c w n", c=2, w=2)
                        mark(dve.tensor_tensor(GTR[:, 2 * h:2 * h + 2, :], gf[:, :, 0, :],
                                               cb("su").unsqueeze(1).broadcast_to((P, 2, P)), ALU.mult))
                        ins = dve.tensor_tensor(FTR[:, 2 * h:2 * h + 2, :], gf[:, :, 1, :],
                                                cb("iu").unsqueeze(1).broadcast_to((P, 2, P)), ALU.mult)
                    done(ins)
                elif stage == "rhs0" and u + 1 < UNITS:
                    cumulate(u + 1)
                elif stage == "sa1" and u + 1 < UNITS:
                    hats(u + 1)
                elif stage == "state":
                    pe()
                    for h in range(2):
                        p0 = 64 * h
                        ins = dve.tensor_scalar(MST[p0:p0 + 64, :], M[1][p0:p0 + 64, p0:p0 + 64],
                                                EP[p0:p0 + 64, 0, 128:129], IMID[p0:p0 + 64, 1:2],
                                                ALU.mult, ALU.mult)
                    done(ins)

            def head_norm(part, y, squares, s, count, eps):
                yv, sv = (a.rearrange("p t (h n) -> p t h n", n=HD) for a in (y, squares))
                heads = yv.shape[2]
                s1, s2, rs = (a[:, s].rearrange("p (t h) -> p t h", t=2) for a in (S1, S2, RS))
                spread = lambda a: a.unsqueeze(3).broadcast_to((P, 2, heads, HD))
                if part == 0:
                    mark(dve.tensor_reduce(s1, yv, AX.X, ALU.add))
                    settle()
                    mark(dve.tensor_scalar(s1, s1, -1.0 / HD, None, ALU.mult))
                    settle()
                    dve.tensor_tensor(yv, yv, spread(s1), ALU.add).then_inc(centred, 1)
                elif part == 1:
                    dve.wait_ge(squared, count)
                    mark(dve.tensor_reduce(s2, sv, AX.X, ALU.add))
                    settle()
                    dve.tensor_scalar(s2, s2, 1.0 / HD, eps, ALU.mult, ALU.add).then_inc(var_sum, 1)
                elif part == 2:
                    dve.wait_ge(std_done, count)
                    mark(dve.reciprocal(rs, rs))
                    settle()
                    mark(dve.tensor_tensor(yv, yv, spread(rs), ALU.mult))

            def finish(u, f):
                cu = slice(u * P, (u + 1) * P)
                y, v = YA[:, :, cu], VTA[:, :, cu]
                if f == 0:
                    dve.wait_ge(rw_act, step(RW_ACT, "y1", u))
                    dve.wait_ge(rw_pe, step(RW, "y1", u))
                if f < 3:
                    head_norm(f, y, YSU[:, :, :], slice(4 * u, 4 * u + 4), u + 1, A_EPS)
                two = lambda a: a[:, cu].unsqueeze(1).broadcast_to((P, 2, P))
                if f == 0:
                    vh = v.rearrange("p t (h n) -> p t h n", n=HD)
                    bonus = BON.rearrange("p (c h) -> p c h", c=2)[:, :, 2 * u:2 * u + 2]
                    mark(dve.tensor_tensor(vh, vh, bonus.unsqueeze(3).broadcast_to((P, 2, 2, HD)), ALU.mult))
                elif f == 2:
                    settle()
                    mark(dve.tensor_tensor(y, y, two(LNAG), ALU.mult))
                elif f == 3:
                    dve.wait_ge(lnab_in, 16)
                    settle()
                    mark(dve.tensor_tensor(y, y, two(LNAB), ALU.add))
                    settle()
                    mark(dve.tensor_tensor(y, y, v, ALU.add))

            def gate_a():
                settle()
                for t in range(2):
                    dve.wait_ge(a_gate, t + 1)
                    ins = dve.tensor_tensor(YA[:, t, :], M[t][:, :], YA[:, t, :], ALU.mult)
                ins.then_inc(a_done, 1)

            def indexer(i):
                if i == 0:
                    dve.wait_ge(evac[1], EV[5])
                    mark(dve.tensor_scalar(W4.rearrange("p (t h) -> p t h", t=2), BVW[:, :, 64:68],
                                           64 ** -0.5 * 4 ** -0.5, None, ALU.mult))
                    settle()
                t, h = divmod(i, 4)
                a, w = 128 * t, P * (t + 1)
                sc = SC[:, a:a + w]
                dve.wait_ge(ix_act, i + 1)
                if h:
                    dve.wait_ge(ix_dve, i)
                dve.scalar_tensor_tensor(sc, RL[:, i % 2, 0:w], W4[:, i:i + 1],
                                         sc if h else CBT[:, CB["band"] + a:CB["band"] + a + w],
                                         ALU.mult, ALU.add).then_inc(ix_dve, 1)

            def best_keys(rnd):
                t, r = divmod(rnd, TOPK // 8)
                sc = SC[:, 128 * t:128 * t + P * (t + 1)]
                if r == 0:
                    dve.wait_ge(ix_dve, 4 * t + 4)
                mark(dve.max(T8, sc))
                settle()
                mark(dve.match_replace(sc, T8, sc, TAKEN))
                settle()
                if r == TOPK // 8 - 1:
                    dve.tensor_scalar(SEL[:, 128 * t:128 * t + P * (t + 1)], sc, TAKEN, -BIG,
                                      ALU.not_equal, ALU.mult).then_inc(sel_done, 1)

            def attention(g, h):
                if h < HEADS:
                    i = g * HEADS + h
                    dve.wait_ge(at_s, i + 1)
                    for t, (a, b) in enumerate([(0, 128), (128, 384)]):
                        ins = dve.tensor_reduce(NM[:, 2 * h + t:2 * h + t + 1], M[i % 2][:, a:b], AX.X, ALU.max,
                                                negate=True)
                    ins.then_inc(at_max, 1)
                if h in (5, 9):
                    h0 = h - 5
                    dve.wait_ge(at_pv, g * HEADS + h0 + 4)
                    if g or h0:
                        dve.wait_ge(at_y, 2 * g + h0 // 4)
                    rec, sums = (a.rearrange("p (t h) -> p t h", t=2)[:, :, h0:h0 + 4]
                                 for a in (REC, SUM[:, 16 * g:16 * g + 16]))
                    mark(dve.reciprocal(rec, sums))
                    settle()
                    o = M[3][:, :].rearrange("p (h t n) -> p h t n", h=4, t=2)
                    for t in range(2):
                        ins = dve.tensor_tensor(
                            YG[2 - g][:, t, h0 * HD:(h0 + 4) * HD].rearrange("p (h n) -> p h n", n=HD),
                            o[:, :, t, :], bc(REC[:, 8 * t + h0:8 * t + h0 + 4], (P, 4, HD)), ALU.mult)
                    ins.then_inc(at_y, 1)

            def retention(a):
                for h in range(2 * a, min(2 * a + 2, HEADS)):
                    dve.wait_ge(ret_s, h + 1)
                    if h >= 2:
                        dve.wait_ge(ret_pv, h - 1)
                    dve.tensor_tensor(STD[:, h % 2, :], M[h % 2][:, 0:384], cb("ret", 384), ALU.mult)\
                       .then_inc(ret_m, 1)

            def norm_d(part):
                if part == 0:
                    dve.wait_ge(ret_y, 2)
                head_norm(part, YD[:, :, :], YSQ[:, :, :], slice(0, 16), UNITS + 1, RET_EPS)

            q = 4 * KT
            turns, last_turn = mod_turns(), None
            for n in range(N0_OUT):
                for half in range(2):
                    for _ in range(mods_at(n, half)):
                        mod_add(*divmod(q, KT))
                        q += 1
                    ld = rw_stage(n, half)[1].startswith("ld")
                    if half == 1 and not ld:
                        split_lo(n + AHEAD)
                    if last_turn is not None:
                        mod_cols(last_turn)
                    last_turn = turns.get((n, half))
                    u, stage = rw_stage(n, half)
                    kind, a = mix_step(n, half)
                    if (n, half) in SETUP:
                        setup(SETUP[n, half])
                    elif stage:
                        rwkv(u, stage)
                    elif kind == "indexer":
                        indexer(2 * a)
                        indexer(2 * a + 1)
                    elif kind == "attention":
                        attention(*divmod(a, HEADS + 2))
                    elif kind == "retention":
                        retention(a)
                    elif kind == "norm":
                        norm_d(a)
                    if half == 1 and ld:
                        split_lo(n + AHEAD)
                    u, f = finish_step(n, half)
                    if u is not None:
                        finish(u, f)
                    if kind == "attention" and a < TOPK // 8:
                        best_keys(2 * a)
                        best_keys(2 * a + 1)
                if n == 10 * CH_IN - 1:
                    gate_a()
                if n % CH_IN == CH_IN - 1:
                    evac_in(n // CH_IN)
            settle()
            dve.wait_ge(evac[1], EV[11])
            dve.tensor_tensor(YD[:, :, :], YD[:, :, :], DG[:, :, :], ALU.mult).then_inc(d_done, 1)
            mod_cols(8)
            mod_cols(9)

            def gate_rows(col, dgm, slots):
                for nb in range(4):
                    if nb >= slots:
                        dve.wait_ge(gb_pe, nb - slots + 1)
                    dve.tensor_tensor(dgm[:, nb % slots, :].rearrange("p (a n) -> p a n", a=4),
                                      IDENT.unsqueeze(1).broadcast_to((P, 4, P)),
                                      bc(MC[:, col + 4 * nb:col + 4 * nb + 4], (P, 4, P)), ALU.mult)\
                       .then_inc(gb_dve, 1)

            dve.wait_ge(mod_col, 6)
            gate_rows(GT1, DGM1, 2)
            for r in range(8):
                dve.wait_ge(y_hi, r + 1)
                dve.tensor_tensor(HLO[:, 2 * r:2 * r + 2, :].rearrange("p k n -> p (k n)"), G[r % 4][:, :],
                                  HHI[:, 2 * r:2 * r + 2, :].bitcast(f32).rearrange("p k n -> p (k n)"),
                                  ALU.subtract).then_inc(y_lo, 1)
            dve.wait_ge(gb_act, 4)
            dve.wait_ge(lnp_in, 64)

            OWN_OUT = 8
            n_own = own[0]
            with dve.Fori(0, N_OUT_BLOCKS // 2) as i:
                own[0], own[1] = n_own, i * OWN_OUT
                for j in range(2 * CH_IN):
                    split_lo_at((j + AHEAD) % RING, i * (2 * CH_IN) + (N0_OUT + j + AHEAD))
                    if j % CH_IN == CH_IN - 1:
                        bb = j // CH_IN
                        dve.wait_ge(w_used, i * (2 * CH_IN) + (N0_OUT + j + 1))
                        for t in range(2):
                            at = ds(i * 1024 + bb * 512, 512)
                            mark(dve.tensor_tensor(ZT1[:, :], G[2 * bb + t][:, :], GB1[:, at], ALU.mult))
                            settle()
                            mark(dve.scalar_tensor_tensor(X1[:, t, at], XR[:, t, at], ALPHA, ZT1[:, :],
                                                          ALU.mult, ALU.add))
                            settle()
                            dve.bn_stats(BST[:, ds(i * 12 + (t * 24 + bb * 6), 6)], X1[:, t, at])\
                               .then_inc(evac[bb], 1)
                assert own[0] - n_own == OWN_OUT
            own[0], own[1] = n_own + OWN_OUT * (N_OUT_BLOCKS // 2), None

            def layer_stats(t, done):
                dve.bn_aggr(MV[:, 4 * t:4 * t + 2], BST[:, 24 * t:24 * t + 24]).then_inc(ln_var, 1)

            def normalise(t, done):
                dve.wait_ge(ln_std, done + t + 1)
                mark(dve.reciprocal(MV[:, 4 * t + 3:4 * t + 4], MV[:, 4 * t + 2:4 * t + 3]))
                settle()
                return dve.tensor_scalar(X1[:, t, :], X1[:, t, :], MV[:, 4 * t:4 * t + 1],
                                         MV[:, 4 * t + 3:4 * t + 4], ALU.subtract, ALU.mult)

            dve.wait_ge(evac[0], EV1[0])
            dve.wait_ge(evac[1], EV1[1])
            for t in range(2):
                layer_stats(t, 0)
            dve.wait_ge(mod_col, MOD_PARTS - 2)
            mark(dve.tensor_tensor(SCG, PCOL[:, PR["ln1_g"]:PR["ln1_g"] + KT], MC[:, SC2:SC2 + KT], ALU.mult))
            mark(dve.tensor_tensor(SHB, PCOL[:, PR["ln1_b"]:PR["ln1_b"] + KT], MC[:, SC2:SC2 + KT], ALU.mult))
            settle()
            mark(dve.tensor_tensor(SHB, SHB, MC[:, SH2:SH2 + KT], ALU.add))
            for t in range(2):
                normalise(t, 0).then_inc(zn_done, 1)
            settle()
            for kt in range(KT):
                if kt % 2 == 0:
                    dve.wait_ge(zn_pe, kt // 2 + 1)
                if kt >= 4:
                    dve.wait_ge(h_lo, KT + kt - 3)
                dve.tensor_scalar(HTMP[:, kt % 4, :], G[kt // 2 % 4][:, (kt % 2) * T:(kt % 2) * T + T],
                                  SCG[:, kt:kt + 1], SHB[:, kt:kt + 1], ALU.mult, ALU.add).then_inc(h_new, 1)
                if kt >= 2:
                    h_split(kt - 2, KT)
            h_split(KT - 2, KT)
            h_split(KT - 1, KT)
            OWN_UP = 5
            n_own = own[0]

            def up_block(i, mods):
                own[0], own[1] = n_own, i * OWN_UP
                for j in range(2 * CH_IN):
                    split_lo_at((j + AHEAD) % RING, i * (2 * CH_IN) + (N0_UP + j + AHEAD))
                    if mods and j % 2:
                        k = j // 2
                        dve.wait_ge(mod_in[k % RING], i * 32 + (16 * MODS_IN // RING + 16 * (k // RING + 1)))
                        dve.wait_ge(conv_cp, i + 1)
                        dve.wait_ge(mod_done, i * 8 + (MODS_IN + k - 1))
                        a = ACC2[:, k % 2, :]
                        dve.scalar_tensor_tensor(a, MODR2[:, k % RING, :], CC4[:, k // 2:k // 2 + 1], a,
                                                 ALU.mult, ALU.add).then_inc(mod_done, 1)
                    if j == 0:
                        if mods:
                            dve.wait_ge(mod_done, i * 8 + MODS_IN)
                            dve.tensor_copy(CC4, CC[:, ds(i * 4, 4)])
                        dve.wait_ge(evac[0], i * 4 + EV1[0])
                        for k, name in enumerate(("conv_b", "conv2", "conv1", "conv0")):
                            ins = dve.tensor_copy(CONV[:, 4 * k:4 * k + 4], PCOL[:, ds(i * 4 + PR[name], 4)])
                        ins.then_inc(conv_cp, 1)
                    if j == CH_IN - 1:
                        dve.wait_ge(conv_cp, i + 1)
                        for k in range(4):
                            g = G[k // 2][:, (k % 2) * T:(k % 2) * T + T]
                            dve.wait_ge(g_pre, i * 4 + (2 * (k // 2) + 2))
                            mark(dve.scalar_tensor_tensor(GF[:, k, 1:T], g[:, 0:T - 1], CONV[:, 8 + k:9 + k],
                                                          GF[:, k, 1:T], ALU.mult, ALU.add))
                        settle()
                        for k in range(4):
                            g = G[k // 2][:, (k % 2) * T:(k % 2) * T + T]
                            dve.scalar_tensor_tensor(GF[:, k, 2:T], g[:, 0:T - 2], CONV[:, 12 + k:13 + k],
                                                     GF[:, k, 2:T], ALU.mult, ALU.add).then_inc(evac[0], 1)
                    if j == 2 * CH_IN - 1:
                        dve.wait_ge(evac[0], i * 4 + (EV1[0] + 4))
                        dve.wait_ge(g_sig, i + 1)
                        gf, sf = GF[:, :, :].rearrange("p k n -> p (k n)"), SF[:, :, :].rearrange("p k n -> p (k n)")
                        mark(dve.tensor_tensor(gf, gf, sf, ALU.mult))
                        settle()
                        dve.wait_ge(w_used, i * (2 * CH_IN) + (N0_UP + 2 * CH_IN))
                        for k in range(2):
                            dve.tensor_tensor(gf[:, 512 * k:512 * k + 512], G[2 + k][:, :],
                                              gf[:, 512 * k:512 * k + 512], ALU.mult).then_inc(evac[1], 1)
                        dve.wait_ge(evac[1], i * 2 + (EV1[1] + 2))
                        dve.wait_ge(f_hi, i + 1)
                        dve.tensor_tensor(FLO[:, ds(i * 4, 4), :], GF[:, :, :], FHI[:, ds(i * 4, 4), :].bitcast(f32),
                                          ALU.subtract).then_inc(f_lo, 1)
                assert own[0] - n_own == OWN_UP, own[0] - n_own

            dve.wait_ge(zeroed, 3)
            with dve.Fori(0, UP_MODS) as i:
                up_block(i, True)
            own[0], own[1] = n_own + OWN_UP * UP_MODS, None
            up_block(UP_MODS, False)
            own[0], own[1] = n_own + OWN_UP * (UP_MODS + 1), None
            dve.wait_ge(mod_sum, MOD_PARTS)
            dve.tensor_tensor(MC[:, GT2:GT2 + 16], M[3][:, 0:16], BMC[:, GT2:GT2 + 16], ALU.add).then_inc(mod_col, 1)
            dve.wait_ge(mod_col, MOD_PARTS - 1)
            gate_rows(GT2, DGM2, 4)
            with dve.Fori(UP_MODS + 1, N_UP) as i:
                up_block(i, False)
            own[0], own[1] = n_own + OWN_UP * N_UP, None

            dve.wait_ge(gb_act, 8)
            dve.wait_ge(x1_done, 16)
            for b in range(N_DOWN_BLOCKS):
                for j in range(CH_DOWN):
                    n = N0_DOWN + b * CH_DOWN + j
                    split_lo(n + AHEAD)
                at = slice(b * 512, (b + 1) * 512)
                dve.wait_ge(w_used, N0_DOWN + (b + 1) * CH_DOWN)
                for t in range(2):
                    mark(dve.tensor_tensor(ZT2[:, :], G[2 * (b % 2) + t][:, :], GB2[:, at], ALU.mult))
                    settle()
                    mark(dve.scalar_tensor_tensor(X1[:, t, at], X1[:, t, at], ALPHA, ZT2[:, :], ALU.mult, ALU.add))
                    settle()
                    mark(dve.bn_stats(BST[:, t * 24 + b * 6:t * 24 + b * 6 + 6], X1[:, t, at])) if b >= 2 else \
                        dve.bn_stats(BST[:, t * 24 + b * 6:t * 24 + b * 6 + 6], X1[:, t, at]).then_inc(evac[b % 2], 1)
            settle()
            dve.wait_ge(evac[1], EV2[1] + 2)
            dve.wait_ge(evac[0], EV2[0] + 2)
            for t in range(2):
                layer_stats(t, 2)
            dve.wait_ge(ln2_in, 32)
            mean, rstd = (lambda t: MV[:, 4 * t:4 * t + 1]), (lambda t: MV[:, 4 * t + 3:4 * t + 4])
            dve.wait_ge(ln_var, 4)
            halves = [slice(0, D // 2), slice(D // 2, D)]
            for t in (1, 0):
                for n in range(2):
                    x1 = X1[:, t, halves[n]]
                    mark(dve.scalar_tensor_tensor(x1, x1, mean(t), LN2G[:, halves[n]], ALU.subtract, ALU.mult))
                    if t == 1 and n == 0:
                        for tt in range(2):
                            dve.wait_ge(ln_std, 3 + tt)
                            mark(dve.reciprocal(rstd(tt), MV[:, 4 * tt + 2:4 * tt + 3]))
                    settle()
                    if t == 1:
                        dve.tensor_scalar(x1, x1, rstd(t), None, ALU.mult).then_inc(scaled, 1)
                    else:
                        dve.scalar_tensor_tensor(x1, x1, rstd(t), LN2B[:, halves[n]], ALU.mult, ALU.add)\
                            .then_inc(out_ready[0], 1)

        @block.tensor
        def _(pe):
            def mm(out_, l, r, start=False, stop=False):
                return pe.matmul(out_, l, r, start=start, stop=stop, skip_group_check=True)

            def fm(s, kk, kt, banks, start, stop, tiles=4):
                for i in range(tiles):
                    o = banks[i // 2][:, (i % 2) * T:(i % 2) * T + T]
                    wh, wl = (w[:, s, kk, i * P:(i + 1) * P] for w in (WHI, WLO))
                    mm(o, wh, HHI[:, kt, :], start=start and i % 2 == 0)
                    mm(o, wh, HLO[:, kt, :])
                    ins = mm(o, wl, HHI[:, kt, :], stop=stop)
                return ins

            def tm(s, kk, kt, banks, start, stop, ahi=None, alo=None):
                ahi, alo = (HHI, HLO) if ahi is None else (ahi, alo)
                for t in range(2):
                    lh, ll = (a[:, kt, t * P:(t + 1) * P] for a in (ahi, alo))
                    mm(banks[t][:, :], lh, WHI[:, s, kk, :], start=start)
                    mm(banks[t][:, :], lh, WLO[:, s, kk, :])
                    ins = mm(banks[t][:, :], ll, WHI[:, s, kk, :], stop=stop)
                return ins

            def mod_reduce(m, acc=ACC, at=0):
                for q in range(8):
                    ins = mm(M[3][:, at + q:at + q + 1], acc[:, m % 2, q * P:(q + 1) * P], ONES[:, 0:1], start=True, stop=True)
                ins.then_inc(mod_sum, 1)

            pe.wait_ge(cf_in, 16)
            pe.wait_ge(prow_in, 16 * 13)
            for g, n in enumerate((122, 120, 96)):
                pe.transpose(M[g][:, 0:n], PROW[0:n, g, :], IDENT[0:n, 0:n]).then_inc(pcol_pe, 1)
            pe.wait_ge(x_in, 32)
            for r in range(8):
                if r >= 4:
                    pe.wait_ge(xt_act, r - 3)
                for q in range(4):
                    kt, t = 2 * r + q // 2, q % 2
                    ins = pe.transpose(G[r % 4][:, q * P:(q + 1) * P], X0[:, t, kt * P:(kt + 1) * P], IDENT)
                ins.then_inc(xt_pe, 1)
            for m in range(4):
                pe.wait_ge(mod_done, (m + 1) * KT)
                if m:
                    pe.wait_ge(mod_col, m)
                mod_reduce(m)

            def w_in_half(n, kk):
                b, j = divmod(n, CH_IN)
                s, banks = n % RING, pair(b)
                if kk == 0:
                    pe.wait_ge(lo_done, n + 1)
                    if b == 0:
                        pe.wait_ge(h_lo, 2 * j + 2)
                        pe.wait_ge(xt_act, 8)
                    elif b >= 2 and j == 0:
                        pe.wait_ge(evac[b % 2], EV[b - 2])
                kt = 2 * j + kk
                first, last = kt == 0, kt == KT - 1
                if b in (8, 10, 11):
                    ins = tm(s, kk, kt, banks, first, last)
                elif b == 5:
                    fm(s, kk, kt, banks, first, last, tiles=2)
                    for t in range(2):
                        o = banks[1][:, t * P:t * P + 68]
                        lh, ll = (a[:, kt, t * P:(t + 1) * P] for a in (HHI, HLO))
                        mm(o, lh, WHI[:, s, kk, 256:324], start=first and t == 0)
                        mm(o, lh, WLO[:, s, kk, 256:324])
                        ins = mm(o, ll, WHI[:, s, kk, 256:324], stop=last)
                else:
                    ins = fm(s, kk, kt, banks, first, last)
                if kk == 1:
                    ins.then_inc(w_used, 1)

            rows = [slice(0, 64), slice(64, 128)]

            def setup(what):
                if what == "lora":
                    pe.wait_ge(mod_col, 5)
                    pe.wait_ge(gates, 1)
                    pe.wait_ge(late_in, 80)
                    for h in range(2):
                        for u in range(UNITS):
                            ins = mm(M[2 * h + u // 2][:, (u % 2) * T:(u % 2) * T + T],
                                     W2A2[rows[h], u * P:(u + 1) * P], PA[rows[h], 12, :], start=u % 2 == 0, stop=True)
                        ins.then_inc(lora_pe, 1)
                elif what == "norms":
                    pe.wait_ge(gates, 2)
                    for i in range(2):
                        pe.wait_ge(kn_sq, 2 * i + 2)
                        for q in range(2):
                            ins = mm(M[i][:, q * T:(q + 1) * T], HEADS2, SQ[:, 2 * i + q, :], start=q == 0, stop=True)
                        ins.then_inc(kn_pe, 1)

            def rwkv(u, stage):
                def after_dve(name):
                    pe.wait_ge(rw_dve, step(RW_DVE, name, u))

                def after_act(name):
                    pe.wait_ge(rw_act, step(RW_ACT, name, u))

                def prob(h, i):
                    return 2 * h + i

                cu = slice(u * P, (u + 1) * P)
                if stage == "turn":
                    pe.wait_ge(prep_dve, 2 * u + 2)
                    if u:
                        pe.wait_ge(rw_act, step(RW_ACT, "y1", u - 1))
                    else:
                        pe.wait_ge(kn_sqrt, 2)
                    for q, src in enumerate((BH, KH)):
                        for i in range(2):
                            pe.transpose(M[2][:, (2 * q + i) * P:(2 * q + i + 1) * P], src[:, i * P:(i + 1) * P], IDENT)
                    for i in range(2):
                        pe.transpose(M[3][:, i * P:(i + 1) * P], PA[:, 8 + u, i * P:(i + 1) * P], IDENT)
                    for i in range(2):
                        ins = mm(M[3][:, 256 + 2 * i:258 + 2 * i], RK[:, i * P:(i + 1) * P], HEADS2[:, 0:128:64],
                                 start=True, stop=True)
                elif stage == "gram":
                    after_act("turned")
                    after_dve("ar")
                    for h in range(2):
                        for i in range(2):
                            bh = BH[rows[h], i * P:(i + 1) * P]
                            mm(M[h][:, i * T:(i + 1) * T], bh, AR[rows[h], i, :, :], start=i == 0, stop=True)
                            ins = mm(M[2 + h][:, i * P:(i + 1) * P], AR[rows[h], i, 0, :], bh, start=i == 0, stop=True)
                elif stage.startswith("ld"):
                    l = int(stage[2:])
                    after_dve("inv0" if l == 1 else f"d{l - 1}")
                    for p in range(4):
                        ins = mm(M[2][:, p * P:(p + 1) * P], LT[:, p, :], DI[:, p, :], start=True, stop=True)
                elif stage.startswith("dx"):
                    l = int(stage[2:])
                    after_dve(f"x{l}")
                    for p in range(4):
                        if l < LEVELS:
                            mm(M[0][:, p * P:(p + 1) * P], DT[:, p, :], XI[:, p, :], start=True, stop=True)
                        ins = mm(M[1][:, p * P:(p + 1) * P], XI[:, p, :], DT[:, p, :], start=True, stop=True)
                elif stage == "gram2":
                    after_dve(f"d{LEVELS}")
                    for h in range(2):
                        for i in range(2):
                            ins = mm(M[h][:, i * T:(i + 1) * T], KH[rows[h], i * P:(i + 1) * P], AR[rows[h], i, :, :],
                                     start=i == 0, stop=True)
                elif stage == "rhs0":
                    after_dve("gf")
                    for h in range(2):
                        ins = mm(M[2][:, h * 64:h * 64 + 64], GTR[:, prob(h, 0), :],
                                 VTA[:, 0, u * P + h * 64:u * P + h * 64 + 64], start=True, stop=True)
                elif stage == "sa0":
                    after_act("rhs0")
                    for h in range(2):
                        ins = mm(M[3][:, h * 64:h * 64 + 64], DT[:, prob(h, 0), :], RH[:, h * 64:h * 64 + 64],
                                 start=True, stop=True)
                elif stage == "state":
                    after_act("sa0")
                    for h in range(2):
                        hc = slice(h * 64, h * 64 + 64)
                        mm(M[0][:, hc], ET[:, prob(h, 0), :], SA[:, hc], start=True)
                        mm(M[0][:, hc], FTR[:, prob(h, 0), :], VTA[:, 0, u * P + h * 64:u * P + h * 64 + 64], stop=True)
                    mm(M[1][:, 0:P], TB[:, 0, 0, :], SA[:, :], start=True)
                    ins = mm(M[1][:, 0:P], TB[:, 1, 0, :], VTA[:, 0, cu], stop=True)
                elif stage == "rhs1":
                    after_dve("state")
                    for h in range(2):
                        mm(M[2 + h][:, 0:64], AR[rows[h], 1, 0, :], MST[rows[h], :], start=True)
                        ins = mm(M[2 + h][:, 0:64], GTR[:, prob(h, 1), :],
                                 VTA[:, 1, u * P + h * 64:u * P + h * 64 + 64], stop=True)
                elif stage == "sa1":
                    after_act("rhs1")
                    for h in range(2):
                        ins = mm(M[0][:, h * 64:h * 64 + 64], DT[:, prob(h, 1), :], RH[:, h * 64:h * 64 + 64],
                                 start=True, stop=True)
                elif stage == "y1":
                    after_act("sa1")
                    for h in range(2):
                        hc = slice(h * 64, h * 64 + 64)
                        mm(M[2 + h][:, 0:64], AR[rows[h], 1, 1, :], MST[rows[h], :], start=True)
                        mm(M[2 + h][:, 0:64], ET[:, prob(h, 1), :], SA[:, hc])
                        ins = mm(M[2 + h][:, 0:64], FTR[:, prob(h, 1), :],
                                 VTA[:, 1, u * P + h * 64:u * P + h * 64 + 64], stop=True)
                ins.then_inc(rw_pe, 1)

            def gate_a():
                pe.wait_ge(rw_act, UNITS * len(RW_ACT))
                for t in range(2):
                    mm(M[t][:, :], PA[:, 13, t * P:(t + 1) * P], G2[:, :], start=True, stop=True).then_inc(a_gate, 1)

            def indexer(i):
                t, h = divmod(i, 4)
                if i == 0:
                    pe.wait_ge(a_done, 1)
                if i >= 2:
                    pe.wait_ge(ix_act, i - 1)
                w = P * (t + 1)
                mm(M[h % 2][:, 0:w], BQI[rows[h % 2], h // 2, t * P:(t + 1) * P], BK[rows[h % 2], 1, 0:w],
                   start=True, stop=True).then_inc(ix_pe, 1)

            def attention(g, h):
                q_, k_ = (CQ, CK) if g == 0 else (BQ, BK)
                if h < HEADS:
                    i = g * HEADS + h
                    if i >= 2:
                        pe.wait_ge(at_exp, i - 1)
                    elif i == 0:
                        pe.wait_ge(ix_act, 8)
                        pe.wait_ge(bias_in, 16)
                    if g == 1 and h == 0:
                        pe.wait_ge(sel_done, 2)
                    o, rh, kk = M[h % 2], rows[h % 2], (0 if g == 1 else h // 2)
                    if g == 1:
                        mm(o[:, 0:384], IDB, SEL[:, :], start=True)
                        mm(o[:, 0:384], cb("slope", i=h), cb("dist", 384))
                    else:
                        mm(o[:, 0:384], IDB, cb("band", 384), start=True)
                        mm(o[:, 0:128], BIA[:, h, 0:128], FLIP)
                        mm(o[:, 128:256], BIA[:, h, 128:256], FLIP)
                        mm(o[:, 256:384], BIA[:, h, 0:128], FLIP)
                    mm(o[:, 0:128], q_[rh, h // 2, 0:128], k_[rh, kk, 0:128])
                    mm(o[:, 128:384], q_[rh, h // 2, 128:256], k_[rh, kk, 0:256], stop=True).then_inc(at_s, 1)
                if 1 <= h <= HEADS:
                    i = g * HEADS + h - 1
                    pe.wait_ge(at_exp, i + 1)
                    if i >= 1:
                        pe.wait_ge(at_pt, i)
                    for b in range(3):
                        ins = pe.transpose(M[2][:, b * P:(b + 1) * P], PB[:, i % 2, b * P:(b + 1) * P], IDENT)
                    ins.then_inc(at_turn, 1)
                if h >= 2:
                    hh = h - 2
                    i = g * HEADS + hh
                    pe.wait_ge(at_pt, i + 1)
                    if hh % 4 == 0:
                        pe.wait_ge(at_y, i // 4) if i else pe.wait_ge(mod_col, 8)
                    vals = [BVW[:, t, 0:64] for t in range(2)] if g == 1 else \
                        [CV[:, t, hh * HD:(hh + 1) * HD] for t in range(2)]
                    o = M[3][:, (hh % 4) * P:(hh % 4 + 1) * P]
                    mm(o[:, 0:64], PTB[:, i % 2, 0:128], vals[0], start=True, stop=True)
                    mm(o[:, 64:128], PTB[:, i % 2, 128:256], vals[0], start=True)
                    mm(o[:, 64:128], PTB[:, i % 2, 256:384], vals[1], stop=True).then_inc(at_pv, 1)

            def retention(a):
                if a == 0:
                    pe.wait_ge(at_exp, 16)
                    pe.wait_ge(at_pt, 16)
                    pe.wait_ge(at_y, 4)
                    pe.wait_ge(evac[0], EV[10])
                    pe.wait_ge(evac[1], EV[9])
                for h in range(2 * a, min(2 * a + 2, HEADS + 1)):
                    if h < HEADS:
                        if h >= 2:
                            pe.wait_ge(ret_m, h - 1)
                        r, t = slice(32 * (h % 4), 32 * (h % 4) + 32), h // 4
                        o = M[h % 2]
                        mm(o[:, 0:256], DQK[r, 2 + t, 0:128], DQK[r, t, :], start=True, stop=True)
                        mm(o[:, 256:384], DQK[r, 2 + t, 128:256], DQK[r, t, 128:256], start=True, stop=True)\
                            .then_inc(ret_s, 1)
                    if h >= 1:
                        hh = h - 1
                        pe.wait_ge(ret_m, hh + 1)
                        hc, st = slice(hh * HD, (hh + 1) * HD), STD[:, hh % 2, :]
                        mm(M[2][:, hc], st[:, 0:128], DV[:, 0, hc], start=True, stop=True)
                        mm(M[3][:, hc], st[:, 128:256], DV[:, 0, hc], start=True)
                        mm(M[3][:, hc], st[:, 256:384], DV[:, 1, hc], stop=True).then_inc(ret_pv, 1)

            def norm_d(part):
                pass

            turns = mod_turns()
            for n in range(N0_OUT):
                for half in range(2):
                    w_in_half(n, half)
                    if (n, half) in turns:
                        m = turns[n, half]
                        if n >= RW_TO:
                            pe.wait_ge(rw_act, UNITS * len(RW_ACT))
                        pe.wait_ge(mod_done, (m + 1) * KT)
                        pe.wait_ge(mod_col, m)
                        mod_reduce(m)
                    u, stage = rw_stage(n, half)
                    kind, a = mix_step(n, half)
                    if (n, half) in SETUP:
                        setup(SETUP[n, half])
                    elif stage:
                        rwkv(u, stage)
                    elif kind == "indexer":
                        indexer(2 * a)
                        indexer(2 * a + 1)
                    elif kind == "attention":
                        attention(*divmod(a, HEADS + 2))
                    elif kind == "retention":
                        retention(a)
                    elif kind == "norm":
                        norm_d(a)
                if n == RW_TO:
                    gate_a()
            for m in (8, 9):
                pe.wait_ge(mod_done, (m + 1) * KT)
                pe.wait_ge(mod_col, m)
                pe.wait_ge(ret_y, 2)
                mod_reduce(m)

            def gate_rows(dgm, done, slots):
                for nb in range(4):
                    pe.wait_ge(gb_dve, done + nb + 1)
                    if nb == 3 and done == 0:
                        pe.wait_ge(mod_col, 10)
                    mm(M[nb][:, :], ONES, dgm[:, nb % slots, :], start=True, stop=True).then_inc(gb_pe, 1)

            for r in range(8):
                if r == 2:
                    pe.wait_ge(evac[1], EV[11])
                if r == 4:
                    gate_rows(DGM1, 0, 2)
                if r == 6:
                    pe.wait_ge(d_done, 1)
                if r >= 4:
                    pe.wait_ge(y_lo, r - 3)
                for q in range(4):
                    kt, t = 2 * r + q // 2, q % 2
                    ins = pe.transpose(G[r % 4][:, q * P:(q + 1) * P], YG[kt // 4][:, t, (kt % 4) * P:(kt % 4 + 1) * P],
                                       IDENT)
                ins.then_inc(y_pe, 1)
            pe.wait_ge(y_lo, 8)
            with pe.Fori(0, N_OUT_BLOCKS // 2) as i:
                for bb in range(2):
                    pe.wait_ge(evac[bb], i * 2 + EV0[bb])
                    for j in range(CH_IN):
                        pe.wait_ge(lo_done, i * (2 * CH_IN) + (N0_OUT + bb * CH_IN + j + 1))
                        for kk in range(2):
                            kt = 2 * j + kk
                            ins = tm(j % RING, kk, kt, pair(bb), kt == 0, kt == KT - 1)
                        ins.then_inc(w_used, 1)
            pe.wait_ge(zn_done, 2)
            for r in range(8):
                if r >= 4:
                    pe.wait_ge(h_new, KT + 2 * (r - 3))
                for q in range(4):
                    kt, t = 2 * r + q // 2, q % 2
                    ins = pe.transpose(G[r % 4][:, q * P:(q + 1) * P], X1[:, t, kt * P:(kt + 1) * P], IDENT)
                ins.then_inc(zn_pe, 1)

            def up_block(i, first=False):
                for half in range(2):
                    pe.wait_ge(evac[half], i * (4, 2)[half] + EV1[half])
                    for j in range(CH_IN):
                        if first:
                            pe.wait_ge(h_lo, KT + 2 * j + 2 if half == 0 else 2 * KT)
                        pe.wait_ge(lo_done, i * (2 * CH_IN) + (N0_UP + half * CH_IN + j + 1))
                        for kk in range(2):
                            kt = 2 * j + kk
                            ins = fm(j % RING, kk, kt, pair(half), kt == 0, kt == KT - 1)
                        ins.then_inc(w_used, 1)

            pe.wait_ge(h_new, 2 * KT)
            up_block(0, True)
            with pe.Fori(1, UP_MODS + 1) as i:
                up_block(i)
            pe.wait_ge(mod_done, MOD_PARTS * KT)
            pe.wait_ge(gb_act, 4)
            for m in (MOD_PARTS - 2, MOD_PARTS - 1):
                mod_reduce(m, ACC2, 8 * (m % 2))
            up_block(UP_MODS + 1)
            pe.wait_ge(mod_col, MOD_PARTS - 1)
            gate_rows(DGM2, 4, 4)
            with pe.Fori(UP_MODS + 2, N_UP) as i:
                up_block(i)
            pe.wait_ge(f_lo, N_UP - 1)
            with pe.Fori(0, N_DOWN_BLOCKS // 2) as i:
                for bb in range(2):
                    pe.wait_ge(evac[bb], i * 2 + EV2[bb])
                    for j in range(CH_DOWN):
                        n = bb * CH_DOWN + j
                        pe.wait_ge(lo_done, i * (2 * CH_DOWN) + (N0_DOWN + n + 1))
                        if bb == 0 and 2 * j + 2 > FT - 4:
                            pe.wait_ge(f_lo, N_UP)
                        for kk in range(2):
                            kt = 2 * j + kk
                            ins = tm(n % RING, kk, kt, pair(bb), kt == 0, kt == FT - 1, FHI, FLO)
                        ins.then_inc(w_used, 1)


_INS = ['x', 'c', 'w_mod', 'b_mod', 'w_in', 'rwkv_mu', 'rwkv_w0', 'rwkv_w2', 'rwkv_a0', 'rwkv_a2', 'rwkv_g2',
        'rwkv_kk', 'rwkv_ka', 'rwkv_rk', 'rwkv_ln_g', 'rwkv_ln_b', 'chunk_rel_bias', 'w_out', 'ln1_g', 'ln1_b',
        'w_up', 'conv_w', 'conv_b', 'w_down', 'ln2_g', 'ln2_b']


def _constants():
    import numpy as np
    p = np.arange(P)
    eye = np.eye(P)
    f = np.zeros((P, CF_W))
    f[:, 0:128] = eye
    f[:, 128:256] = 1.0
    f[:, 256:384] = (p[:, None] // HD) == (p[None, :] // HD)
    f[:, 384:512] = eye[:, ::-1]
    t = np.arange(T)
    for j in range(2):
        gamma = 1.0 - 2.0 ** (-5.0 - (4 * j + p // 32))
        f[:, 512 + j * T:512 + (j + 1) * T] = gamma[:, None] ** (t[None, :] - 128.0)
        f[:, 1024 + j * T:1024 + (j + 1) * T] = gamma[:, None] ** (128.0 - t[None, :]) * 32 ** -0.5
    b = np.zeros((P, CB_W))
    b[:, 0:128] = eye
    r, q = p[:, None], p[None, :]
    for l in range(LEVELS + 1):
        w = 2 ** l
        m = (r // (2 * w) == q // (2 * w)) & (r // w % 2 == 1) & (q // w % 2 == 0)
        b[:, CB["level"] + l * 128:CB["level"] + (l + 1) * 128] = m
        if l == 0:
            b[:, CB["level0t"]:CB["level0t"] + 128] = m.T
    b[:, CB["su"]:CB["su"] + 128] = r < q
    b[:, CB["iu"]:CB["iu"] + 128] = r <= q
    b[:, CB["ret"]:CB["ret"] + 384] = np.concatenate([r <= q, np.ones((P, P)), r <= q], 1)
    for h in range(HEADS):
        b[:, CB["slope"] + h * 128:CB["slope"] + (h + 1) * 128] = -eye * 2.0 ** -(h + 1)
    pairs = [(p, np.arange(P)), (p + P, np.arange(T))]
    b[:, CB["dist"]:CB["dist"] + 384] = np.concatenate([abs(a[:, None] - k[None, :]) for a, k in pairs], 1)
    b[:, CB["band"]:CB["band"] + 384] = np.concatenate(
        [np.where(k[None, :] < (a[:, None] // CHUNK + 1) * CHUNK, 0.0, -BIG) for a, k in pairs], 1)
    return f.astype(np.float32), (b.astype(np.float32).view(np.uint32) >> 16).astype(np.uint16)


def kernel(**inputs):
    import numpy as _np
    import concourse.bacc as _bacc
    from concourse import mybir as _mybir
    from concourse.bass_utils import run_bass_kernel_spmd as _run

    nc = _bacc.Bacc("TRN2", target_bir_lowering=False, num_devices=1)
    arrays, args = {}, []
    const_f, const_b = _constants()
    for name, a in [(n, inputs[n]) for n in _INS] + [("const_f", const_f), ("const_b", const_b)]:
        a = _np.ascontiguousarray(a)
        arrays[f"in_{name}_dram"] = a
        args.append(nc.dram_tensor(f"in_{name}_dram", a.shape, _mybir.dt.from_np(a.dtype), kind="ExternalInput").ap())
    args.append(nc.dram_tensor("out_0_dram", (1, T, D), _mybir.dt.float32, kind="ExternalOutput").ap())
    encoder_layer(nc, *args)
    r = _run(nc, [arrays], core_ids=[0])
    return r.results[0]["out_0_dram"]
```

```python
import concourse.bass as bass
from concourse import mybir
from contextlib import ExitStack

D, T, P = 2048, 256, 128
KT = D // P
CHUNK, HD = 64, 64
GW = 512
HEADS = GW // HD
D_FF = 256 * ((8 * D // 3 + 255) // 256)
FT = D_FF // P
A_COLS, B_COLS, C_COLS, D_COLS = 3 * GW + 256, GW + 2 * HD + 4 * 64 + 64 + 4, 3 * GW, 2 * 256 + 2 * GW
B0, C0, D0 = A_COLS, A_COLS + B_COLS, A_COLS + B_COLS + C_COLS
ALPHA = 2.0 ** 0.25
KAPPA = 0.6065306597126334
BIG = 1.0e30
TAKEN = -3.0e38
LN_EPS, A_EPS, RET_EPS = 1e-5, HD * 1e-5, 1e-5
TOPK = T // 4

RING = 4
AHEAD = 3
N_IN_BLOCKS, N_OUT_BLOCKS, N_UP, N_DOWN_BLOCKS = 12, 4, D_FF // 512, 4
CH_IN = KT // 2
CH_DOWN = FT // 2
N0_OUT = N_IN_BLOCKS * CH_IN
N0_UP = N0_OUT + N_OUT_BLOCKS * CH_IN
N0_DOWN = N0_UP + 2 * N_UP * CH_IN
N_ALL = N0_DOWN + N_DOWN_BLOCKS * CH_DOWN

MOD_W = 1024
MOD_PARTS = 6 * D // MOD_W
MODS_IN = (MOD_PARTS - 2) * KT
UP_MODS = 4
SH1, SC1, GT1, SH2, SC2, GT2 = (16 * i for i in range(6))

CF = dict(ident=0, ones=128, heads2=256, flip=384, decay=512)
CF_W = 512 + 1024
N_EVAC_IN = [4, 4, 4, 3, 2, 2, 2, 2, 2, 2, 2, 2]
LEVELS = 6
CB = dict(ident=0, level=128, level0t=128 + 7 * 128, su=128 + 8 * 128, iu=128 + 9 * 128,
          ret=128 + 10 * 128, slope=128 + 13 * 128, dist=128 + 21 * 128, band=128 + 24 * 128)
CB_W = 128 + 27 * 128
PR = dict(mu=0, w0=14, a0=18, kk=22, ka=26, rk=30, conv_b=34, conv2=34 + FT,
          conv0=128, conv1=128 + FT, ln1_g=128 + 2 * FT, ln1_b=128 + 2 * FT + 16)

RW = ["turn", "gram"] + [f"{s}{l}" for l in range(1, LEVELS + 1) for s in ("ld", "dx")] + \
     ["gram2", "rhs0", "sa0", "state", "rhs1", "sa1", "y1"]
RW_ACT = ["turned", "rhs0", "sa0", "y0", "rhs1", "sa1", "y1"]
RW_DVE = ["ar", "inv0"] + [f"{s}{l}" for l in range(1, LEVELS + 1) for s in ("x", "d")] + ["gf", "state"]
UNITS = HEADS // 2

FIRST_PARTS = [0, 2, 1, 3]
FIRST_CHUNKS = CH_IN
MODS_BESIDE_H = 4


def part_at(m):
    return FIRST_PARTS[m] if m < len(FIRST_PARTS) else m


def chunk_at(n):
    b, j = divmod(n, CH_IN)
    q = CH_IN // 2
    return (n // q % 2, n % q + n // CH_IN * q) if b < 2 else (b, j)


DONE_IN = [CH_IN + CH_IN // 2] + [CH_IN * (b + 1) for b in range(1, N_IN_BLOCKS)]

EARLY = [11, 15]

SETUP = {(20, 0): "squares", (20, 1): "norms", (22, 0): "inverse 0", (24, 0): "inverse 1", (26, 0): "inverse 2",
         (28, 0): "inverse 3", (32, 1): "lora", (33, 0): "cumulate", (34, 0): "hats"}
RW_FROM = 35
RW_TO = RW_FROM + UNITS * len(RW) // 2
AT_FROM = RW_TO + 2
MIX = [("indexer", i) for i in range(4)] + [("attention", i) for i in range(2 * (HEADS + 2))] + \
      [("retention", i) for i in range(5)] + [("norm", i) for i in range(2)]
FINISH = ["sa0", "state", "rhs1", "y1"]


def rw_stage(n, half):
    k = 2 * (n - RW_FROM) + half
    return (k // len(RW), RW[k % len(RW)]) if 0 <= k < UNITS * len(RW) else (None, "")


def finish_step(n, half):
    u, stage = rw_stage(n, half)
    if u and stage in FINISH:
        return u - 1, FINISH.index(stage)
    k = 2 * (n - RW_TO) + half
    return (UNITS - 1, k) if 0 <= k < 4 else (None, None)


def mix_step(n, half):
    a = 2 * (n - AT_FROM) + half
    return MIX[a] if 0 <= a < len(MIX) else (None, 0)


def mods_at(n, half):
    if n < RW_FROM:
        return int(half == 1 and n >= FIRST_CHUNKS + 6 and n % 3 != 1)
    if n < RW_TO:
        u, stage = rw_stage(n, half)
        spare = u == 0 and stage in FINISH or u == UNITS - 1 and stage in ("rhs0", "sa1")
        return 2 if stage == "gram" else int(stage in ("turn", "gram2") or stage.startswith("dx") or spare)
    return (2 if n == AT_FROM + 1 else 1) if AT_FROM <= n < N_IN_BLOCKS * CH_IN - 2 else 0


def mod_turns():
    turns, part, q = {}, 4, 4 * KT + MODS_BESIDE_H
    for k in range(2 * N_IN_BLOCKS * CH_IN):
        stage = (k - 2 * RW_FROM) % len(RW)
        free = k < 2 * (RW_FROM - 5) or (3 <= stage <= 12 if k < 2 * RW_TO else k < 2 * AT_FROM + 4)
        if part <= 7 and q >= (part + 1) * KT and free:
            turns[divmod(k, 2)] = part
            part += 1
        q += mods_at(*divmod(k, 2))
    assert part == 8 and q == MODS_IN, (part, q)
    return turns


def step(names, name, u):
    return u * len(names) + names.index(name) + 1


def encoder_layer(nc, x, c, w_mod, b_mod, w_in, rwkv_mu, rwkv_w0, rwkv_w2, rwkv_a0, rwkv_a2, rwkv_g2,
                  rwkv_kk, rwkv_ka, rwkv_rk, rwkv_ln_g, rwkv_ln_b, chunk_rel_bias, w_out, ln1_g, ln1_b,
                  w_up, conv_w, conv_b, w_down, ln2_g, ln2_b, const_f, const_b, out):
    f32, f32r, bf16 = mybir.dt.float32, mybir.dt.float32r, mybir.dt.bfloat16
    ALU, ACT, AX = mybir.AluOpType, mybir.ActivationFunctionType, mybir.AxisListType
    ds = bass.ds
    base = (nc.sbuf_base + 63) // 64 * 64

    def sb(name, shape, off_kb, dt=f32):
        return nc.alloc_sbuf_tensor_at(name, shape, dt, offset=base + int(off_kb * 1024))

    RAW = sb("RAW", [P, RING, 2, 512], 0)
    WHI = sb("WHI", [P, RING, 2, 512], 16, f32r)
    WLO = sb("WLO", [P, RING, 2, 512], 32, f32r)
    HHI = sb("HHI", [P, KT, T], 48, f32r)
    HLO = sb("HLO", [P, KT, T], 64, f32r)
    LN2G, LN2B = sb("LN2G", [P, D], 48), sb("LN2B", [P, D], 56)
    GB2, DGM2, ZT2 = sb("GB2", [P, D], 64), sb("DGM2", [P, 4, 512], 168), sb("ZT2", [P, 512], 76)
    FHI = sb("FHI", [P, FT, T], 80, f32r)
    FLO = sb("FLO", [P, FT, T], 80 + FT, f32r)
    MODR = sb("MODR", [P, RING, MOD_W], 80)
    ACC = sb("ACC", [P, 2, MOD_W], 96)
    PA = sb("PA", [P, 14, T], 104)
    DQK, DV, DG = sb("DQK", [P, 4, T], 104), sb("DV", [P, 2, GW], 108), sb("DG", [P, 2, GW], 112)
    BQ, BK = sb("BQ", [P, 4, T], 118), sb("BK", [P, 2, T], 122)
    BQI, BVW = sb("BQI", [P, 2, T], 124), sb("BVW", [P, 2, 68], 126)
    CQ, CK, CV = sb("CQ", [P, 4, T], 127), sb("CK", [P, 4, T], 131), sb("CV", [P, 2, GW], 135)
    W2A2, G2 = sb("W2A2", [P, GW], 139), sb("G2", [P, GW], 141)
    LNAG, LNAB = sb("LNAG", [P, GW], 147), sb("LNAB", [P, GW], 173)
    AL = sb("AL", [P, UNITS, T], 143)
    EM, SIG = sb("EM", [P, 2, P], 149), sb("SIG", [P, UNITS, T], 168.25)
    KKN, TA = sb("KKN", [P, T], 150), sb("TA", [P, T], 151)
    CU, EP = sb("CU", [P, 2, 129], 152), sb("EP", [P, 2, 129], 153.0625)
    LT, DI, DT = sb("LT", [P, 4, P], 154.25), sb("DI", [P, 4, P], 156.25), sb("DT", [P, 4, P], 158.25)
    XI, ET = sb("XI", [P, 4, P], 160.25), sb("ET", [P, 4, P], 162.25)
    GTR, FTR = sb("GTR", [P, 4, P], 154.25), sb("FTR", [P, 4, P], 156.25)
    VTA = sb("VTA", [P, 2, GW], 164.25)
    YSU, YSQ = sb("YSU", [P, 2, P], 175), sb("YSQ", [P, 2, GW], 168.25)
    MST = sb("MST", [P, HD], 172.5)
    TB, RK = sb("TB", [P, 2, 2, P], 180), sb("RK", [P, T], 182)
    RH, SA = sb("RH", [P, P], 183), sb("SA", [P, P], 183.5)
    AR, BH, KH = sb("AR", [P, 2, 2, P], 184), sb("BH", [P, T], 186), sb("KH", [P, T], 187)
    RN, SQ = sb("RN", [P, 4, T], 188), sb("SQ", [P, 4, T], 154.25)
    PB, PTB = sb("PB", [P, 2, 384], 147), sb("PTB", [P, 2, 384], 150)
    SC, RL, SEL = sb("SC", [P, 384], 153), sb("RL", [P, 2, T], 154.5), sb("SEL", [P, 384], 156.5, bf16)
    STD, BIA = sb("STD", [P, 2, 384], 157.25), sb("BIA", [P, HEADS, T], 160.25)
    X0, X1 = sb("X0", [P, 2, D], 176), sb("X1", [P, 2, D], 176)
    YG = [sb(f"Y{g}", [P, 2, GW], 176 + 4 * i) for i, g in enumerate("ABCD")]
    YA, YD = YG[0], YG[3]
    XT, HTMP = sb("XT", [P, KT, T], 120), sb("HTMP", [P, 4, T], 172)
    XR, GB1 = sb("XR", [P, 2, D], 104), sb("GB1", [P, D], 120)
    DGM1, ZT1 = sb("DGM1", [P, 4, 512], 128), sb("ZT1", [P, 512], 136)
    LN1G, LN1B = sb("LN1G", [P, D], 80), sb("LN1B", [P, D], 88)
    ACC2, MODR2 = sb("ACC2", [P, 2, MOD_W], 144), sb("MODR2", [P, RING, MOD_W], 152)
    CFT = sb("CFT", [P, CF_W], 192)
    PCOL, BMC, MC = sb("PCOL", [P, 256], 198), sb("BMC", [P, 96], 199), sb("MC", [P, 96], 199.5)
    SM = sb("SM", [P, 224], 199.875)
    CBT = sb("CBT", [P, CB_W], 200.75, bf16)
    PROW = sb("PROW", [P, 3, P], 172)
    GF, SF = sb("GF", [P, 4, T], 194), sb("SF", [P, 4, T], 201)

    def cf(name, n=128):
        return CFT[:, CF[name]:CF[name] + n]

    def cb(name, n=128, i=0):
        return CBT[:, CB[name] + i * 128:CB[name] + i * 128 + n]

    def pc(name, i=0):
        return PCOL[:, PR[name] + i:PR[name] + i + 1]

    def bc(ap, shape):
        return ap.unsqueeze(len(shape) - 1).broadcast_to(shape)

    IDENT, ONES, HEADS2, FLIP = cf("ident"), cf("ones"), cf("heads2"), cf("flip")
    IDB = cb("ident")
    OMU, CC = SM[:, 0:14], SM[:, 16:32]
    KMID, NKMID, IMID = SM[:, 32:34], SM[:, 34:36], SM[:, 36:38]
    BON = SM[:, 40:56]
    NM, SUM, REC = SM[:, 56:72], SM[:, 72:104], SM[:, 104:120]
    S1, S2, RS = SM[:, 120:136], SM[:, 136:152], SM[:, 152:168]
    W4, T8, CSG, EPS = SM[:, 168:176], SM[:, 176:184], SM[:, 184:200], SM[:, 200:203]
    CCOL, CC4 = SM[:, 204:220], SM[:, 184:188]
    BST, MV = SM[:, 56:104], SM[:, 104:112]
    SCG, SHB, CONV = SM[:, 120:136], SM[:, 136:152], SM[:, 152:168]

    with ExitStack() as ctx:
        def sem(name):
            return ctx.enter_context(nc.semaphore(name))

        G = [ctx.enter_context(nc.psum_tensor(f"G{i}", [P, 512], f32)) for i in range(4)]
        M = [ctx.enter_context(nc.psum_tensor(f"M{i}", [P, 512], f32)) for i in range(4)]

        raw_in = [sem(f"raw_in{i}") for i in range(RING)]
        mod_in = [sem(f"mod_in{i}") for i in range(RING)]
        hi_done, lo_done = sem("hi_done"), sem("lo_done")
        w_used = sem("w_used")
        evac = [sem("evac_even"), sem("evac_odd")]
        mod_done, mod_sum, mod_col = sem("mod_done"), sem("mod_sum"), sem("mod_col")
        c_in, cf_in, x_in, prow_in = sem("c_in"), sem("cf_in"), sem("x_in"), sem("prow_in")
        late_in, lnp_in, ln2_in, bias_in = sem("late_in"), sem("lnp_in"), sem("ln2_in"), sem("bias_in")
        pcol_pe, pcol_done, silu_c = sem("pcol_pe"), sem("pcol_done"), sem("silu_c")
        xt_pe, xt_act = sem("xt_pe"), sem("xt_act")
        h_new, h_hi, h_lo = sem("h_new"), sem("h_hi"), sem("h_lo")
        mixed, gates = sem("mixed"), sem("gates")
        kn_sq, kn_pe, kn_sqrt = sem("kn_sq"), sem("kn_pe"), sem("kn_sqrt")
        rw_pe, rw_act, rw_dve = sem("rw_pe"), sem("rw_act"), sem("rw_dve")
        lora_pe, prep_dve, prep_act = sem("lora_pe"), sem("prep_dve"), sem("prep_act")
        lnab_in = sem("lnab_in")
        centred, squared, var_sum, std_done = sem("centred"), sem("squared"), sem("var_sum"), sem("std_done")
        a_gate, a_done = sem("a_gate"), sem("a_done")
        ix_pe, ix_act, ix_dve, sel_done = sem("ix_pe"), sem("ix_act"), sem("ix_dve"), sem("sel_done")
        at_s, at_max, at_exp, at_turn, at_pt, at_pv, at_y = (sem("at_" + n) for n in
                                                            ("s", "max", "exp", "turn", "pt", "pv", "y"))
        ret_s, ret_m, ret_pv, ret_y, d_done = (sem("ret_" + n) for n in ("s", "m", "pv", "y", "done"))
        y_pe, y_hi, y_lo = sem("y_pe"), sem("y_hi"), sem("y_lo")
        gb_dve, gb_pe, gb_act = sem("gb_dve"), sem("gb_pe"), sem("gb_act")
        ln_var, ln_std, zn_done, zn_pe = sem("ln_var"), sem("ln_std"), sem("zn_done"), sem("zn_pe")
        x1_done = sem("x1_done")
        conv_cp, g_pre, g_sig = sem("conv_cp"), sem("g_pre"), sem("g_sig")
        f_hi, f_lo = sem("f_hi"), sem("f_lo")
        out_ready, out_sent, scaled = [sem("out_ready0"), sem("out_ready1")], sem("out_sent"), sem("scaled")
        dve_own, zeroed = sem("dve_own"), sem("zeroed")

        EV = []
        for b in range(N_IN_BLOCKS):
            EV.append(N_EVAC_IN[b] + (EV[b - 2] if b >= 2 else 0))
        EV0 = EV[-2:]
        EV1 = [EV0[0] + 4, EV0[1] + 4]
        EV2 = [EV1[0] + 4 * N_UP, EV1[1] + 2 * N_UP]

        def raw_count(n):
            double = sum(1 for m in range(n % RING, n + 1, RING) if m // CH_IN in (3, 5))
            return 16 * (n // RING + 1 + double)

        RAW_SHIFT = raw_count(N0_OUT) - 16 * (N0_OUT // RING + 1)

        def pair(b):
            return G[2 * (b % 2)], G[2 * (b % 2) + 1]

        def dup_views(dst, s):
            d, r = dst[:, s, :, :], RAW[:, s, :, :]
            two = lambda lo: r[:, :, lo:lo + 64].unsqueeze(2).broadcast_to((P, 2, 2, 64))
            return [(d[:, :, 0:128].rearrange("p k (a n) -> p k a n", a=2), two(0)),
                    (d[:, :, 128:256].rearrange("p k (a n) -> p k a n", a=2), two(128)),
                    (d[:, :, 256:320], r[:, :, 64:128]), (d[:, :, 320:324], r[:, :, 192:196])]

        block = ctx.enter_context(nc.Block())

        @block.sync
        def _(sp):
            sp.dma_start(CCOL, c.rearrange("a (p t) -> (a p) t", t=KT)).then_inc(c_in, 16)
            sp.dma_start(CFT[:, :], const_f).then_inc(cf_in, 16)
            xv = x.rearrange("a (t p) d -> (a p) t d", p=P)
            for t in range(2):
                sp.dma_start(X0[:, t, :], xv[:, t, :]).then_inc(x_in, 16)
            r128 = lambda ap: ap.rearrange("a (j p) -> (a j) p", p=P)
            cw = lambda i: conv_w[0, i, :].rearrange("(j p) -> j p", p=P)
            for g, name, src, n in [
                    (0, "mu", r128(rwkv_mu), 14), (0, "w0", r128(rwkv_w0), 4), (0, "a0", r128(rwkv_a0), 4),
                    (0, "kk", r128(rwkv_kk), 4), (0, "ka", r128(rwkv_ka), 4),
                    (0, "rk", rwkv_rk.rearrange("a (j h) d -> (a j) (h d)", h=2), 4),
                    (0, "conv_b", r128(conv_b), FT), (0, "conv2", cw(2), FT), (1, "conv0", cw(0), FT),
                    (1, "conv1", cw(1), FT), (1, "ln1_g", r128(ln1_g), KT), (1, "ln1_b", r128(ln1_b), KT)]:
                r = PR[name] - 128 * g
                sp.dma_start(PROW[r:r + n, g, :], src).then_inc(prow_in, 16)
            sp.dma_start(PROW[0:96, 2, :], r128(b_mod)).then_inc(prow_in, 16)
            wi, wo, wu, wd = (w[0].rearrange("(t p) n -> p t n", p=P) for w in (w_in, w_out, w_up, w_down))
            bkv, bqi = B0 + GW, B0 + GW + 2 * HD
            cols = [[(0, GW)], [(GW, GW)], [(2 * GW, GW)], [(3 * GW, 256), (bqi, 256)], [(B0, GW)],
                    [(bkv, 128), (bqi + 256, 68)], [(C0, GW)], [(C0 + GW, GW)], [(C0 + 2 * GW, GW)],
                    [(D0, GW)], [(D0 + GW, GW)], [(D0 + 2 * GW, GW)]]

            def load_bias():
                sp.wait_ge(a_done, 1)
                sp.dma_start(BIA[:, :, :], bass.AP(tensor=chunk_rel_bias.tensor, offset=129,
                                                   ap=[[1, P], [513, HEADS], [1, T]])).then_inc(bias_in, 16)

            for n in range(N0_OUT):
                b, j = chunk_at(n)
                if n == CH_IN + RING:
                    sp.dma_start(CBT[:, :], const_b.bitcast(bf16)).then_inc(late_in, 16)
                    sp.dma_start(W2A2[0:64, :], rwkv_w2[0]).then_inc(late_in, 16)
                    sp.dma_start(W2A2[64:128, :], rwkv_a2[0]).then_inc(late_in, 16)
                    sp.dma_start(G2[:, :], rwkv_g2[0]).then_inc(late_in, 16)
                    sp.dma_start(LNAG[:, :], rwkv_ln_g[0, :].partition_broadcast(P)).then_inc(late_in, 16)
                if n == 2 * CH_IN:
                    sp.wait_ge(h_lo, KT)
                    sp.dma_start(LNAB[:, :], rwkv_ln_b[0, :].partition_broadcast(P)).then_inc(lnab_in, 16)
                if n >= RING:
                    sp.wait_ge(lo_done, n - RING + 1)
                at = 0
                for c0, w in cols[b]:
                    sp.dma_start(RAW[:, n % RING, :, at:at + w], wi[:, 2 * j:2 * j + 2, c0:c0 + w])\
                      .then_inc(raw_in[n % RING], 16)
                    at += w
                if n == AT_FROM + AHEAD:
                    load_bias()
            with sp.Fori(0, N_OUT_BLOCKS) as b:
                for j in range(CH_IN):
                    sp.wait_ge(lo_done, b * CH_IN + (N0_OUT + j - RING + 1))
                    sp.dma_start(RAW[:, j % RING, :, :], wo[:, 2 * j:2 * j + 2, ds(b * 512, 512)])\
                      .then_inc(raw_in[j % RING], 16)
            with sp.Fori(0, N_UP) as i:
                for j in range(2 * CH_IN):
                    half, jj = divmod(j, CH_IN)
                    sp.wait_ge(lo_done, i * (2 * CH_IN) + (N0_UP + j - RING + 1))
                    sp.dma_start(RAW[:, j % RING, :, :],
                                 wu[:, 2 * jj:2 * jj + 2, ds(i * 512 + half * D_FF, 512)])\
                      .then_inc(raw_in[j % RING], 16)
            for b in range(N_DOWN_BLOCKS):
                for j in range(CH_DOWN):
                    n = N0_DOWN + b * CH_DOWN + j
                    sp.wait_ge(lo_done, n - RING + 1)
                    sp.dma_start(RAW[:, n % RING, :, :], wd[:, 2 * j:2 * j + 2, b * 512:(b + 1) * 512])\
                      .then_inc(raw_in[n % RING], 16)
                if b == 0:
                    sp.wait_ge(w_used, N0_DOWN)
                    sp.dma_start(LN2G[:, :], ln2_g[0, :].partition_broadcast(P)).then_inc(ln2_in, 16)
                    sp.dma_start(LN2B[:, :], ln2_b[0, :].partition_broadcast(P)).then_inc(ln2_in, 16)
            ov = out.rearrange("a (t p) d -> (a p) t d", p=P)
            for n in range(4):
                t, cols = 1 - n // 2, slice(n % 2 * (D // 2), (n % 2 + 1) * (D // 2))
                sp.wait_ge(out_ready[t], n % 2 + 1)
                sp.dma_start(ov[:, t, cols], X1[:, t, cols]).then_inc(out_sent, 16)
            sp.wait_ge(out_sent, 64)

        @block.gpsimd
        def _(pool):
            pool.memset(CU[:, :, 0:1], 0.0).then_inc(zeroed, 1)
            pool.memset(EPS[:, 0:1], LN_EPS).then_inc(zeroed, 1)
            wm = w_mod[0].rearrange("(p t) n -> p t n", t=KT)
            for q in range(4 * KT):
                m, t = divmod(q, KT)
                if q >= RING:
                    pool.wait_ge(mod_done, q - RING + 1)
                pool.dma_start(MODR[:, t % RING, :], wm[:, t, part_at(m) * MOD_W:(part_at(m) + 1) * MOD_W])\
                    .then_inc(mod_in[t % RING], 16)

            def parts(first, last):
                with pool.Fori(first, last) as m:
                    for t in range(KT):
                        pool.wait_ge(mod_done, m * KT + (t - RING + 1))
                        pool.dma_start(MODR[:, t % RING, :], wm[:, t, ds(m * MOD_W, MOD_W)])\
                            .then_inc(mod_in[t % RING], 16)

            parts(4, MOD_PARTS - 2)
            pool.wait_ge(d_done, 1)
            pool.wait_ge(mod_done, MODS_IN)
            pool.memset(ACC2[:, :, :], 0.0).then_inc(zeroed, 1)
            xv = x.rearrange("a (t p) d -> (a p) t d", p=P)
            for t in range(2):
                pool.dma_start(XR[:, t, :], xv[:, t, :]).then_inc(lnp_in, 16)
            pool.dma_start(LN1G[:, :], ln1_g[0, :].partition_broadcast(P)).then_inc(lnp_in, 16)
            pool.dma_start(LN1B[:, :], ln1_b[0, :].partition_broadcast(P)).then_inc(lnp_in, 16)
            def last_parts(i, ks):
                for k in ks:
                    pool.wait_ge(mod_done, i * 8 + (MODS_IN + k - RING + 1))
                    row, m = i * 4 + k // 2, MOD_PARTS - 2 + k % 2
                    pool.dma_start(MODR2[:, k % RING:k % RING + 1, :], wm[:, ds(row, 1), m * MOD_W:(m + 1) * MOD_W])\
                        .then_inc(mod_in[k % RING], 16)

            last_parts(0, range(RING))
            pool.wait_ge(zn_pe, 8)
            pool.wait_ge(zn_done, 2)
            for c0 in range(0, D, 512):
                for t in range(2):
                    pool.tensor_tensor(X1[:, t, c0:c0 + 512], X1[:, t, c0:c0 + 512], LN1G[:, c0:c0 + 512], ALU.mult)\
                        .then_inc(x1_done, 1)
            for n, c0 in enumerate(range(0, D, 512)):
                for t in range(2):
                    pool.wait_ge(x1_done, 2 * n + t + 1)
                    pool.tensor_tensor(X1[:, t, c0:c0 + 512], X1[:, t, c0:c0 + 512], LN1B[:, c0:c0 + 512], ALU.add)\
                        .then_inc(x1_done, 1)
            last_parts(0, range(RING, 8))
            with pool.Fori(1, UP_MODS) as i:
                last_parts(i, range(8))
            for n in range(2):
                cols = slice(n * (D // 2), (n + 1) * (D // 2))
                pool.wait_ge(scaled, n + 1)
                pool.tensor_tensor(X1[:, 1, cols], X1[:, 1, cols], LN2B[:, cols], ALU.add).then_inc(out_ready[1], 1)

        @block.scalar
        def _(act):
            def split_hi(n):
                if n >= N_ALL:
                    return
                s = n % RING
                act.wait_ge(raw_in[s], raw_count(n))
                if n >= RING:
                    act.wait_ge(w_used, n - RING + 1)
                if n // CH_IN == 5:
                    for dst, src in dup_views(WHI, s):
                        ins = act.activation(dst, src, ACT.Copy)
                    ins.then_inc(hi_done, 1)
                else:
                    act.activation(WHI[:, s, :, :], RAW[:, s, :, :], ACT.Copy).then_inc(hi_done, 1)

            def split_hi_at(s, groups, n):
                act.wait_ge(raw_in[s], groups * 16 + (RAW_SHIFT + 16))
                act.wait_ge(w_used, n + (1 - RING))
                act.activation(WHI[:, s, :, :], RAW[:, s, :, :], ACT.Copy).then_inc(hi_done, 1)

            act.wait_ge(c_in, 16)
            act.activation(CSG, CCOL, ACT.Sigmoid).then_inc(silu_c, 1)
            for g, (dst, n) in enumerate([(PCOL[:, 0:122], 122), (PCOL[:, 128:248], 120), (BMC[:, :], 96)]):
                act.wait_ge(pcol_pe, g + 1)
                act.activation(dst, M[g][:, 0:n], ACT.Copy).then_inc(pcol_done, 1)
            for r in range(8):
                act.wait_ge(xt_pe, r + 1)
                act.activation(XT[:, 2 * r:2 * r + 2, :], G[r % 4][:, :], ACT.Copy).then_inc(xt_act, 1)
            for n in range(AHEAD):
                split_hi(n)
            for kt in range(KT):
                if kt == KT // 2:
                    for n in range(FIRST_CHUNKS):
                        split_hi(n + AHEAD)
                act.wait_ge(h_new, kt + 1)
                act.activation(HHI[:, kt, :], HTMP[:, kt % 4, :], ACT.Copy).then_inc(h_hi, 1)

            def evac_in(b):
                act.wait_ge(w_used, DONE_IN[b])
                e, banks = evac[b % 2], pair(b)
                if b <= 3:
                    for i in range(4 if b < 3 else 2):
                        act.activation(PA[:, 4 * b + i, :], banks[i // 2][:, (i % 2) * T:(i % 2) * T + T],
                                       ACT.Copy, scale=OMU[:, 4 * b + i:4 * b + i + 1]).then_inc(mixed, 1)
                    if b == 3:
                        act.activation(BQI[:, :, :], banks[1][:, :], ACT.Copy).then_inc(e, 1)
                elif b in (4, 6):
                    for i in range(2):
                        act.activation((BQ if b == 4 else CQ)[:, 2 * i:2 * i + 2, :], banks[i][:, :], ACT.Copy,
                                       scale=HD ** -0.5).then_inc(e, 1)
                elif b == 5:
                    act.activation(BK[:, :, :], banks[0][:, :], ACT.Copy).then_inc(e, 1)
                    act.activation(BVW[:, :, :], banks[1][:, 0:256].rearrange("p (t n) -> p t n", t=2)[:, :, 0:68],
                                   ACT.Copy).then_inc(e, 1)
                elif b == 7:
                    for i in range(2):
                        act.activation(CK[:, 2 * i:2 * i + 2, :], banks[i][:, :], ACT.Copy).then_inc(e, 1)
                elif b in (8, 10):
                    for i in range(2):
                        act.activation((CV if b == 8 else DV)[:, i, :], banks[i][:, :], ACT.Copy).then_inc(e, 1)
                elif b == 11:
                    for i in range(2):
                        act.activation(DG[:, i, :], banks[i][:, :], ACT.Sigmoid).then_inc(gates, 1)

            def setup(what):
                if what == "lora":
                    act.wait_ge(evac[1], EV[3])
                    act.activation(PA[0:64, 12, :], PA[0:64, 12, :], ACT.Tanh).then_inc(gates, 1)
                    act.activation(PA[:, 13, :], PA[:, 13, :], ACT.Sigmoid)
                    act.wait_ge(lora_pe, 2)
                    for u in range(UNITS):
                        for dst, bias, bank in ((SIG, "w0", 0), (AL, "a0", 2)):
                            ins = act.activation(dst[:, u, :], M[bank + u // 2][:, (u % 2) * T:(u % 2) * T + T],
                                                 ACT.Sigmoid, bias=pc(bias, u))
                    ins.then_inc(gates, 1)
                elif what == "squares":
                    act.wait_ge(evac[1], EV[1])
                    for u in range(UNITS):
                        act.activation(SQ[:, u, :], PA[:, 4 + u, :], ACT.Square, scale=pc("kk", u)).then_inc(kn_sq, 1)
                elif what == "norms":
                    for i in range(2):
                        act.wait_ge(kn_pe, i + 1)
                        act.activation(RN[:, 2 * i:2 * i + 2, :], M[i][:, :], ACT.Sqrt).then_inc(kn_sqrt, 1)
                elif what == "cumulate":
                    decays(0)

            def decays(u):
                act.wait_ge(prep_dve, 2 * u + 1)
                if u:
                    act.wait_ge(rw_dve, step(RW_DVE, "state", u - 1))
                for i in range(2):
                    act.activation(EP[:, i, :], CU[:, i, :], ACT.Exp, scale=-KAPPA, bias=KMID[:, i:i + 1])
                    act.activation(EM[:, i, :], CU[:, i, 1:129], ACT.Exp, scale=KAPPA, bias=NKMID[:, i:i + 1])
                act.activation(IMID, NKMID, ACT.Exp).then_inc(prep_act, 1)

            def rwkv(u, stage):
                def pe():
                    act.wait_ge(rw_pe, step(RW, stage, u))
                if stage == "turn":
                    pe()
                    act.activation(TB[:, :, :, :], M[2][:, :], ACT.Copy)
                    act.activation(VTA[:, :, u * P:(u + 1) * P], M[3][:, 0:256], ACT.Copy)
                    act.activation(BON.rearrange("p (c h) -> p c h", c=2)[:, :, 2 * u:2 * u + 2],
                                   M[3][:, 256:260], ACT.Copy).then_inc(rw_act, 1)
                elif stage == "rhs0":
                    pe()
                    act.activation(RH[:, :], M[2][:, 0:128], ACT.Copy).then_inc(rw_act, 1)
                elif stage == "sa0":
                    pe()
                    act.activation(SA[:, :], M[3][:, 0:128], ACT.Copy).then_inc(rw_act, 1)
                elif stage == "state":
                    pe()
                    act.activation(YA[:, 0, u * P:(u + 1) * P], M[0][:, 0:128], ACT.Copy).then_inc(rw_act, 1)
                elif stage == "rhs1":
                    pe()
                    act.activation(RH[:, 0:64], M[2][:, 0:64], ACT.Copy)
                    act.activation(RH[:, 64:128], M[3][:, 0:64], ACT.Copy).then_inc(rw_act, 1)
                    if u + 1 < UNITS:
                        decays(u + 1)
                elif stage == "sa1":
                    pe()
                    act.activation(SA[:, :], M[0][:, 0:128], ACT.Copy).then_inc(rw_act, 1)
                elif stage == "y1":
                    pe()
                    act.activation(YA[:, 1, u * P:u * P + 64], M[2][:, 0:64], ACT.Copy)
                    act.activation(YA[:, 1, u * P + 64:(u + 1) * P], M[3][:, 0:64], ACT.Copy).then_inc(rw_act, 1)

            def head_norm(part, y, squares, s, count):
                if part == 0:
                    act.wait_ge(centred, count)
                    act.activation(squares, y, ACT.Square).then_inc(squared, 1)
                else:
                    act.wait_ge(var_sum, count)
                    act.activation(RS[:, s], S2[:, s], ACT.Sqrt).then_inc(std_done, 1)

            def indexer(i):
                act.wait_ge(ix_pe, i + 1)
                if i >= 2:
                    act.wait_ge(ix_dve, i - 1)
                w = P * (i // 4 + 1)
                act.activation(RL[:, i % 2, 0:w], M[i % 2][:, 0:w], ACT.Relu).then_inc(ix_act, 1)

            def attention(g, h):
                if h < HEADS:
                    i = g * HEADS + h
                    act.wait_ge(at_max, i + 1)
                    if i >= 2:
                        act.wait_ge(at_turn, i - 1)
                    for t, (a, b) in enumerate([(0, 128), (128, 384)]):
                        k = g * 16 + t * 8 + h
                        ins = act.activation(PB[:, i % 2, a:b], M[i % 2][:, a:b], ACT.Exp,
                                             bias=NM[:, 2 * h + t:2 * h + t + 1], accum_out=SUM[:, k:k + 1])
                    ins.then_inc(at_exp, 1)
                if 1 <= h <= HEADS:
                    i = g * HEADS + h - 1
                    act.wait_ge(at_turn, i + 1)
                    if i >= 2:
                        act.wait_ge(at_pv, i - 1)
                    act.activation(PTB[:, i % 2, :], M[2][:, 0:384], ACT.Copy).then_inc(at_pt, 1)

            def retention(a):
                if a == 4:
                    act.wait_ge(ret_pv, HEADS)
                    for t in range(2):
                        act.activation(YD[:, t, :], M[2 + t][:, :], ACT.Copy).then_inc(ret_y, 1)

            def norm_d(part, late=False):
                if part == 0 or late:
                    head_norm(part, YD[:, :, :], YSQ[:, :, :], slice(0, 16), UNITS + 1)

            due = None, None
            for n in range(FIRST_CHUNKS, N0_OUT):
                for half in range(2):
                    u, f = due
                    if f in (0, 1):
                        head_norm(f, YA[:, :, u * P:(u + 1) * P], YSU[:, :, :], slice(4 * u, 4 * u + 4), u + 1)
                    if half == 1:
                        split_hi(n + AHEAD)
                    u, stage = rw_stage(n, half)
                    kind, a = mix_step(n, half)
                    if (n, half) in SETUP:
                        setup(SETUP[n, half])
                    elif stage:
                        rwkv(u, stage)
                    elif kind == "indexer":
                        indexer(2 * a)
                        indexer(2 * a + 1)
                    elif kind == "attention":
                        attention(*divmod(a, HEADS + 2))
                    elif kind == "retention":
                        retention(a)
                    elif kind == "norm":
                        norm_d(a)
                    due = finish_step(n, half)
                if n == 10 * CH_IN - 1:
                    act.wait_ge(a_done, 1)
                if n + 1 in DONE_IN[:-1]:
                    evac_in(DONE_IN.index(n + 1))

            def y_tiles(rs):
                for r in rs:
                    act.wait_ge(y_pe, r + 1)
                    act.activation(HHI[:, 2 * r:2 * r + 2, :], M[r % 4][:, :], ACT.Copy).then_inc(y_hi, 1)

            y_tiles(range(4))
            norm_d(1, late=True)
            evac_in(N_IN_BLOCKS - 1)
            y_tiles((4, 5))
            for n in range(N0_OUT, N0_OUT + 4):
                split_hi(n + AHEAD)
            y_tiles((6, 7))
            for n in range(N0_OUT + 4, N0_OUT + 6):
                split_hi(n + AHEAD)
            for nb in range(4):
                act.wait_ge(gb_pe, nb + 1)
                act.activation(GB1[:, nb * 512:(nb + 1) * 512], M[nb][:, :], ACT.Copy).then_inc(gb_act, 1)
            for n in range(N0_OUT + 6, N0_UP):
                split_hi(n + AHEAD)
            for t in range(2):
                act.wait_ge(ln_var, t + 1)
                act.activation(MV[:, 4 * t + 2:4 * t + 3], MV[:, 4 * t + 1:4 * t + 2], ACT.Sqrt,
                               bias=EPS[:, 0:1]).then_inc(ln_std, 1)
            for kt in range(KT):
                act.wait_ge(h_new, KT + kt + 1)
                act.activation(HHI[:, kt, :], HTMP[:, kt % 4, :], ACT.Copy).then_inc(h_hi, 1)
                if kt in EARLY:
                    split_hi(N0_UP + AHEAD + EARLY.index(kt))
            def up_block(i, early=0):
                for j in range(2 * CH_IN):
                    if j >= early:
                        split_hi_at((j + AHEAD) % RING, i * (2 * CH_IN // RING) + (N0_UP + j + AHEAD) // RING,
                                    i * (2 * CH_IN) + (N0_UP + j + AHEAD))
                    if j == CH_IN - 1:
                        act.wait_ge(w_used, i * (2 * CH_IN) + (N0_UP + CH_IN))
                        act.wait_ge(conv_cp, i + 1)
                        for k in range(4):
                            act.activation(GF[:, k, :], G[k // 2][:, (k % 2) * T:(k % 2) * T + T], ACT.Identity,
                                           scale=CONV[:, 4 + k:5 + k], bias=CONV[:, k:k + 1]).then_inc(g_pre, 1)
                        act.wait_ge(evac[0], i * 4 + (EV1[0] + 4))
                        act.activation(SF[:, :, :], GF[:, :, :], ACT.Sigmoid).then_inc(g_sig, 1)
                    if j == 2 * CH_IN - 1:
                        act.wait_ge(x1_done, 16)
                        act.wait_ge(evac[1], i * 2 + (EV1[1] + 2))
                        act.activation(FHI[:, ds(i * 4, 4), :], GF[:, :, :], ACT.Copy).then_inc(f_hi, 1)

            up_block(0, len(EARLY))
            with act.Fori(1, N_UP) as i:
                up_block(i)
            for n in range(N0_DOWN, N_ALL):
                split_hi(n + AHEAD)
                if n == N0_DOWN:
                    act.wait_ge(gb_pe, 8)
                    act.wait_ge(w_used, N0_DOWN)
                    for nb in range(4):
                        act.activation(GB2[:, nb * 512:(nb + 1) * 512], M[nb][:, :], ACT.Copy).then_inc(gb_act, 1)
            for t in range(2):
                act.wait_ge(ln_var, 3 + t)
                act.activation(MV[:, 4 * t + 2:4 * t + 3], MV[:, 4 * t + 1:4 * t + 2], ACT.Sqrt,
                               bias=EPS[:, 0:1]).then_inc(ln_std, 1)

        @block.vector
        def _(dve):
            own = [0, None]

            def mark(ins):
                own[0] += 1
                return ins.then_inc(dve_own, 1)

            def settle():
                dve.wait_ge(dve_own, own[0] if own[1] is None else own[1] + own[0])

            def split_lo(n):
                if n >= N_ALL:
                    return
                s = n % RING
                dve.wait_ge(hi_done, n + 1)
                if n // CH_IN == 5:
                    for (dst, src), (h, _) in zip(dup_views(WLO, s), dup_views(WHI, s)):
                        ins = dve.tensor_tensor(dst, src, h.bitcast(f32), ALU.subtract)
                    ins.then_inc(lo_done, 1)
                else:
                    dve.tensor_tensor(WLO[:, s, :, :], RAW[:, s, :, :], WHI[:, s, :, :].bitcast(f32),
                                          ALU.subtract).then_inc(lo_done, 1)

            def split_lo_at(s, n):
                dve.wait_ge(hi_done, n + 1)
                dve.tensor_tensor(WLO[:, s, :, :], RAW[:, s, :, :], WHI[:, s, :, :].bitcast(f32),
                                  ALU.subtract).then_inc(lo_done, 1)

            def mod_add(m, t):
                q = m * KT + t
                dve.wait_ge(mod_in[t % RING], 16 * (q // RING + 1))
                a, w, ck = ACC[:, m % 2, :], MODR[:, t % RING, :], CC[:, t:t + 1]
                if t == 0:
                    if m >= 2:
                        dve.wait_ge(mod_sum, m - 1)
                    ins = dve.tensor_scalar(a, w, ck, None, ALU.mult)
                else:
                    dve.wait_ge(mod_done, q)
                    ins = dve.scalar_tensor_tensor(a, w, ck, a, ALU.mult, ALU.add)
                ins.then_inc(mod_done, 1)

            def mod_cols(m):
                dve.wait_ge(mod_sum, m + 1)
                at = slice(8 * part_at(m), 8 * part_at(m) + 8)
                dve.tensor_tensor(MC[:, at], M[3][:, 0:8], BMC[:, at], ALU.add)\
                   .then_inc(mod_col, 1)

            dve.wait_ge(silu_c, 1)
            dve.wait_ge(c_in, 16)
            mark(dve.tensor_tensor(CC, CCOL, CSG, ALU.mult))
            settle()
            for t in range(KT):
                mod_add(0, t)
            dve.wait_ge(pcol_done, 3)
            mark(dve.tensor_scalar(OMU, PCOL[:, 0:14], -1.0, 1.0, ALU.mult, ALU.add))
            mark(dve.tensor_scalar(BMC[:, SC1:SH2], BMC[:, SC1:SH2], 1.0, None, ALU.add))
            mark(dve.tensor_scalar(BMC[:, SC2:96], BMC[:, SC2:96], 1.0, None, ALU.add))
            settle()
            for t in range(KT):
                mod_add(1, t)
                if t == 3:
                    mod_cols(0)
                if t >= KT - AHEAD:
                    split_lo(t - (KT - AHEAD))

            def h_split(kt, done):
                dve.wait_ge(h_hi, done + kt + 1)
                dve.tensor_tensor(HLO[:, kt, :], HTMP[:, kt % 4, :], HHI[:, kt, :].bitcast(f32), ALU.subtract)\
                   .then_inc(h_lo, 1)

            dve.wait_ge(xt_act, 8)
            for half in range(2):
                mod_add(2 * half + 2, 0)
                mod_cols(2 * half + 1)
                dve.wait_ge(mod_col, 2 * half + 2)
                kts = range(half * KT // 2, (half + 1) * KT // 2)
                for kt in kts:
                    if kt >= 4:
                        dve.wait_ge(h_lo, kt - 3)
                    dve.tensor_scalar(HTMP[:, kt % 4, :], XT[:, kt, :], MC[:, SC1 + kt:SC1 + kt + 1],
                                      MC[:, SH1 + kt:SH1 + kt + 1], ALU.mult, ALU.add).then_inc(h_new, 1)
                    if kt >= kts[2]:
                        h_split(kt - 2, 0)
                    if kt % 2 and kt < kts[-1]:
                        mod_add(2 * half + 2, (kt - kts[0] + 1) // 2)
                h_split(kts[-2], 0)
                h_split(kts[-1], 0)
                if half == 0:
                    for t in range(MODS_BESIDE_H, 2 * KT):
                        mod_add(2 + t // KT, t % KT)
                        if t == KT:
                            mod_cols(2)
                        if t % 2 and t // 2 - 2 < FIRST_CHUNKS:
                            split_lo(t // 2 - 2 + AHEAD)

            def evac_in(b):
                e, banks = evac[b % 2], pair(b)
                if b <= 3:
                    for i in range(4 if b < 3 else 2):
                        j = 4 * b + i
                        dve.wait_ge(mixed, 4 * b + 2 * (i // 2) + 2)
                        dve.scalar_tensor_tensor(PA[:, j, 1:T], banks[i // 2][:, (i % 2) * T:(i % 2) * T + T - 1],
                                                 pc("mu", j), PA[:, j, 1:T], ALU.mult, ALU.add).then_inc(e, 1)
                elif b == 9:
                    dve.wait_ge(w_used, DONE_IN[b])
                    for i in range(2):
                        dve.tensor_tensor(DQK[:, 2 * i:2 * i + 2, :], banks[i][:, :],
                                          cf("decay", 1024)[:, i * 512:(i + 1) * 512], ALU.mult).then_inc(e, 1)
                elif b == 11:
                    dve.wait_ge(gates, 4)
                    for i in range(2):
                        dve.tensor_tensor(DG[:, i, :], DG[:, i, :], banks[i][:, :], ALU.mult).then_inc(e, 1)

            def setup(what):
                if what == "norms":
                    for i in range(2):
                        dve.wait_ge(kn_sqrt, i + 1)
                        r = RN[:, 2 * i:2 * i + 2, :]
                        mark(dve.tensor_scalar(r, r, 1e-12, None, ALU.max))
                elif what.startswith("inverse"):
                    settle()
                    r = RN[:, int(what[-1]), :]
                    mark(dve.reciprocal(r, r))
                elif what == "cumulate":
                    dve.wait_ge(zeroed, 2)
                    dve.wait_ge(late_in, 80)
                    dve.wait_ge(gates, 2)
                    settle()
                    cumulate(0)
                elif what == "hats":
                    hats(0)

            def cumulate(u):
                r, k = PA[:, u, :], PA[:, 4 + u, :]
                for i in range(2):
                    s = SIG[:, u, i * P:(i + 1) * P]
                    mark(dve.tensor_tensor_scan(CU[:, i, 1:129], s, s, 0.0, ALU.add, ALU.bypass))
                mark(dve.scalar_tensor_tensor(KKN[:, :], k, pc("kk", u), RN[:, u, :], ALU.mult, ALU.mult))
                mark(dve.tensor_scalar(TA[:, :], AL[:, u, :], -1.0, pc("ka", u), ALU.add, ALU.mult))
                settle()
                mark(dve.tensor_scalar(KMID, CU[:, :, 64], KAPPA, None, ALU.mult))
                dve.tensor_scalar(NKMID, CU[:, :, 64], -KAPPA, None, ALU.mult).then_inc(prep_dve, 1)
                mark(dve.tensor_tensor(BH[:, :], KKN[:, :], AL[:, u, :], ALU.mult))
                mark(dve.scalar_tensor_tensor(TA[:, :], TA[:, :], 1.0, k, ALU.add, ALU.mult))

            def hats(u):
                settle()
                dve.wait_ge(prep_act, u + 1)
                em = EM[:, :, :].rearrange("p c n -> p (c n)")
                mark(dve.tensor_tensor(BH[:, :], BH[:, :], em, ALU.mult))
                mark(dve.tensor_tensor(KH[:, :], TA[:, :], em, ALU.mult))
                dve.scalar_tensor_tensor(RK[:, :], PA[:, u, :], pc("rk", u), TA[:, :], ALU.mult, ALU.mult)\
                   .then_inc(prep_dve, 1)

            def rwkv(u, stage):
                def done(ins):
                    ins.then_inc(rw_dve, 1)

                def pe():
                    dve.wait_ge(rw_pe, step(RW, stage, u))

                r = PA[:, u, :]
                two = lambda ap: ap.rearrange("p (c n) -> p c n", c=2)
                if stage == "turn":
                    if u:
                        dve.wait_ge(rw_pe, step(RW, "y1", u - 1))
                    mark(dve.scalar_tensor_tensor(AR[:, :, 0, :], two(KKN[:, :]), -1.0, EP[:, :, 0:128],
                                                  ALU.mult, ALU.mult))
                    done(dve.tensor_tensor(AR[:, :, 1, :], two(r), EP[:, :, 1:129], ALU.mult))
                elif stage == "gram":
                    pe()
                    le = [M[h][:, :].rearrange("p (c w n) -> p c w n", c=2, w=2) for h in range(2)]
                    for h in range(2):
                        mark(dve.tensor_tensor(LT[:, 2 * h:2 * h + 2, :], le[h][:, :, 0, :],
                                               cb("su").unsqueeze(1).broadcast_to((P, 2, P)), ALU.mult))
                    for h in range(2):
                        mark(dve.tensor_tensor(XI[:, 2 * h:2 * h + 2, :],
                                               M[2 + h][:, 0:256].rearrange("p (c n) -> p c n", c=2),
                                               cb("level").unsqueeze(1).broadcast_to((P, 2, P)), ALU.mult))
                    settle()
                    idb = IDENT.unsqueeze(1).broadcast_to((P, 4, P))
                    done(dve.tensor_tensor(DI[:, :, :], XI[:, :, :], idb, ALU.add))
                    mark(dve.tensor_tensor(DT[:, :, :], LT[:, :, :],
                                           cb("level0t").unsqueeze(1).broadcast_to((P, 4, P)), ALU.mult))
                    for h in range(2):
                        mark(dve.tensor_tensor(ET[:, 2 * h:2 * h + 2, :], le[h][:, :, 1, :],
                                               cb("iu").unsqueeze(1).broadcast_to((P, 2, P)), ALU.mult))
                    settle()
                    mark(dve.tensor_tensor(DT[:, :, :], DT[:, :, :], idb, ALU.add))
                elif stage.startswith("ld"):
                    pe()
                    done(dve.tensor_tensor(XI[:, :, :], M[2][:, :].rearrange("p (a n) -> p a n", a=4),
                                           cb("level", i=int(stage[2:])).unsqueeze(1).broadcast_to((P, 4, P)),
                                           ALU.mult))
                elif stage.startswith("dx"):
                    pe()
                    last = stage == f"dx{LEVELS}"
                    if not last:
                        done(dve.tensor_tensor(DI[:, :, :].rearrange("p a n -> p (a n)"), M[0][:, :],
                                               DI[:, :, :].rearrange("p a n -> p (a n)"), ALU.add))
                    ins = dve.tensor_tensor(DT[:, :, :].rearrange("p a n -> p (a n)"), M[1][:, :],
                                            DT[:, :, :].rearrange("p a n -> p (a n)"), ALU.add)
                    done(ins) if last else mark(ins)
                elif stage == "gram2":
                    pe()
                    for h in range(2):
                        gf = M[h][:, :].rearrange("p (c w n) -> p c w n", c=2, w=2)
                        mark(dve.tensor_tensor(GTR[:, 2 * h:2 * h + 2, :], gf[:, :, 0, :],
                                               cb("su").unsqueeze(1).broadcast_to((P, 2, P)), ALU.mult))
                        ins = dve.tensor_tensor(FTR[:, 2 * h:2 * h + 2, :], gf[:, :, 1, :],
                                                cb("iu").unsqueeze(1).broadcast_to((P, 2, P)), ALU.mult)
                    done(ins)
                elif stage == "rhs0" and u + 1 < UNITS:
                    cumulate(u + 1)
                elif stage == "sa1" and u + 1 < UNITS:
                    hats(u + 1)
                elif stage == "state":
                    pe()
                    for h in range(2):
                        p0 = 64 * h
                        ins = dve.tensor_scalar(MST[p0:p0 + 64, :], M[1][p0:p0 + 64, p0:p0 + 64],
                                                EP[p0:p0 + 64, 0, 128:129], IMID[p0:p0 + 64, 1:2],
                                                ALU.mult, ALU.mult)
                    done(ins)

            def head_norm(part, y, squares, s, count, eps):
                yv, sv = (a.rearrange("p t (h n) -> p t h n", n=HD) for a in (y, squares))
                heads = yv.shape[2]
                s1, s2, rs = (a[:, s].rearrange("p (t h) -> p t h", t=2) for a in (S1, S2, RS))
                spread = lambda a: a.unsqueeze(3).broadcast_to((P, 2, heads, HD))
                if part == 0:
                    mark(dve.tensor_reduce(s1, yv, AX.X, ALU.add))
                    settle()
                    mark(dve.tensor_scalar(s1, s1, -1.0 / HD, None, ALU.mult))
                    settle()
                    dve.tensor_tensor(yv, yv, spread(s1), ALU.add).then_inc(centred, 1)
                elif part == 1:
                    dve.wait_ge(squared, count)
                    mark(dve.tensor_reduce(s2, sv, AX.X, ALU.add))
                    settle()
                    dve.tensor_scalar(s2, s2, 1.0 / HD, eps, ALU.mult, ALU.add).then_inc(var_sum, 1)
                elif part == 2:
                    dve.wait_ge(std_done, count)
                    mark(dve.reciprocal(rs, rs))
                    settle()
                    mark(dve.tensor_tensor(yv, yv, spread(rs), ALU.mult))

            def finish(u, f):
                cu = slice(u * P, (u + 1) * P)
                y, v = YA[:, :, cu], VTA[:, :, cu]
                if f == 0:
                    dve.wait_ge(rw_act, step(RW_ACT, "y1", u))
                    dve.wait_ge(rw_pe, step(RW, "y1", u))
                if f < 3:
                    head_norm(f, y, YSU[:, :, :], slice(4 * u, 4 * u + 4), u + 1, A_EPS)
                two = lambda a: a[:, cu].unsqueeze(1).broadcast_to((P, 2, P))
                if f == 0:
                    vh = v.rearrange("p t (h n) -> p t h n", n=HD)
                    bonus = BON.rearrange("p (c h) -> p c h", c=2)[:, :, 2 * u:2 * u + 2]
                    mark(dve.tensor_tensor(vh, vh, bonus.unsqueeze(3).broadcast_to((P, 2, 2, HD)), ALU.mult))
                elif f == 2:
                    settle()
                    mark(dve.tensor_tensor(y, y, two(LNAG), ALU.mult))
                elif f == 3:
                    dve.wait_ge(lnab_in, 16)
                    settle()
                    mark(dve.tensor_tensor(y, y, two(LNAB), ALU.add))
                    settle()
                    mark(dve.tensor_tensor(y, y, v, ALU.add))

            def gate_a():
                settle()
                for t in range(2):
                    dve.wait_ge(a_gate, t + 1)
                    ins = dve.tensor_tensor(YA[:, t, :], M[t][:, :], YA[:, t, :], ALU.mult)
                ins.then_inc(a_done, 1)

            def indexer(i):
                if i == 0:
                    dve.wait_ge(evac[1], EV[5])
                    mark(dve.tensor_scalar(W4.rearrange("p (t h) -> p t h", t=2), BVW[:, :, 64:68],
                                           64 ** -0.5 * 4 ** -0.5, None, ALU.mult))
                    settle()
                t, h = divmod(i, 4)
                a, w = 128 * t, P * (t + 1)
                sc = SC[:, a:a + w]
                dve.wait_ge(ix_act, i + 1)
                if h:
                    dve.wait_ge(ix_dve, i)
                dve.scalar_tensor_tensor(sc, RL[:, i % 2, 0:w], W4[:, i:i + 1],
                                         sc if h else CBT[:, CB["band"] + a:CB["band"] + a + w],
                                         ALU.mult, ALU.add).then_inc(ix_dve, 1)

            def best_keys(rnd):
                t, r = divmod(rnd, TOPK // 8)
                sc = SC[:, 128 * t:128 * t + P * (t + 1)]
                if r == 0:
                    dve.wait_ge(ix_dve, 4 * t + 4)
                mark(dve.max(T8, sc))
                settle()
                mark(dve.match_replace(sc, T8, sc, TAKEN))
                settle()
                if r == TOPK // 8 - 1:
                    dve.tensor_scalar(SEL[:, 128 * t:128 * t + P * (t + 1)], sc, TAKEN, -BIG,
                                      ALU.not_equal, ALU.mult).then_inc(sel_done, 1)

            def attention(g, h):
                if h < HEADS:
                    i = g * HEADS + h
                    dve.wait_ge(at_s, i + 1)
                    for t, (a, b) in enumerate([(0, 128), (128, 384)]):
                        ins = dve.tensor_reduce(NM[:, 2 * h + t:2 * h + t + 1], M[i % 2][:, a:b], AX.X, ALU.max,
                                                negate=True)
                    ins.then_inc(at_max, 1)
                if h in (5, 9):
                    h0 = h - 5
                    dve.wait_ge(at_pv, g * HEADS + h0 + 4)
                    if g or h0:
                        dve.wait_ge(at_y, 2 * g + h0 // 4)
                    rec, sums = (a.rearrange("p (t h) -> p t h", t=2)[:, :, h0:h0 + 4]
                                 for a in (REC, SUM[:, 16 * g:16 * g + 16]))
                    mark(dve.reciprocal(rec, sums))
                    settle()
                    o = M[3][:, :].rearrange("p (h t n) -> p h t n", h=4, t=2)
                    for t in range(2):
                        ins = dve.tensor_tensor(
                            YG[2 - g][:, t, h0 * HD:(h0 + 4) * HD].rearrange("p (h n) -> p h n", n=HD),
                            o[:, :, t, :], bc(REC[:, 8 * t + h0:8 * t + h0 + 4], (P, 4, HD)), ALU.mult)
                    ins.then_inc(at_y, 1)

            def retention(a):
                for h in range(2 * a, min(2 * a + 2, HEADS)):
                    dve.wait_ge(ret_s, h + 1)
                    if h >= 2:
                        dve.wait_ge(ret_pv, h - 1)
                    dve.tensor_tensor(STD[:, h % 2, :], M[h % 2][:, 0:384], cb("ret", 384), ALU.mult)\
                       .then_inc(ret_m, 1)

            def norm_d(part):
                if part == 0:
                    dve.wait_ge(ret_y, 2)
                head_norm(part, YD[:, :, :], YSQ[:, :, :], slice(0, 16), UNITS + 1, RET_EPS)

            def gate_rows(col, dgm, nbs=range(4)):
                for nb in nbs:
                    dve.tensor_tensor(dgm[:, nb, :].rearrange("p (a n) -> p a n", a=4),
                                      IDENT.unsqueeze(1).broadcast_to((P, 4, P)),
                                      bc(MC[:, col + 4 * nb:col + 4 * nb + 4], (P, 4, P)), ALU.mult)\
                       .then_inc(gb_dve, 1)

            q = 4 * KT + MODS_BESIDE_H
            turns, last_turn = mod_turns(), None
            for n in range(FIRST_CHUNKS, N0_OUT):
                for half in range(2):
                    for _ in range(mods_at(n, half)):
                        mod_add(*divmod(q, KT))
                        q += 1
                    ld = rw_stage(n, half)[1].startswith("ld")
                    if half == 1 and not ld:
                        split_lo(n + AHEAD)
                    if last_turn is not None:
                        mod_cols(last_turn)
                    last_turn = turns.get((n, half))
                    u, stage = rw_stage(n, half)
                    kind, a = mix_step(n, half)
                    if (n, half) in SETUP:
                        setup(SETUP[n, half])
                    elif stage:
                        rwkv(u, stage)
                    elif kind == "indexer":
                        indexer(2 * a)
                        indexer(2 * a + 1)
                    elif kind == "attention":
                        attention(*divmod(a, HEADS + 2))
                    elif kind == "retention":
                        retention(a)
                    elif kind == "norm":
                        norm_d(a)
                    if half == 1 and ld:
                        split_lo(n + AHEAD)
                    u, f = finish_step(n, half)
                    if u is not None:
                        finish(u, f)
                    if kind == "attention" and 13 <= a < 17:
                        dve.wait_ge(mod_col, 6)
                        gate_rows(GT1, DGM1, [a - 13])
                    if kind == "attention" and a < TOPK // 8:
                        best_keys(2 * a)
                        best_keys(2 * a + 1)
                if n == AT_FROM - 1:
                    gate_a()
                if n + 1 in DONE_IN[:-1]:
                    evac_in(DONE_IN.index(n + 1))
            def two_parts(col):
                dve.wait_ge(mod_sum, col // 8 + 2)
                dve.tensor_tensor(MC[:, col:col + 16], M[3][:, 0:16], BMC[:, col:col + 16], ALU.add)\
                   .then_inc(mod_col, 2)


            def y_tiles(rs):
                for r in rs:
                    dve.wait_ge(y_hi, r + 1)
                    dve.tensor_tensor(HLO[:, 2 * r:2 * r + 2, :].rearrange("p k n -> p (k n)"), M[r % 4][:, :],
                                      HHI[:, 2 * r:2 * r + 2, :].bitcast(f32).rearrange("p k n -> p (k n)"),
                                      ALU.subtract).then_inc(y_lo, 1)

            y_tiles(range(4))
            norm_d(2)
            evac_in(N_IN_BLOCKS - 1)
            settle()
            dve.wait_ge(evac[1], EV[11])
            dve.tensor_tensor(YD[:, :, :], YD[:, :, :], DG[:, :, :], ALU.mult).then_inc(d_done, 1)
            y_tiles((4, 5))

            for b in range(N_OUT_BLOCKS):
                for j in range(CH_IN):
                    split_lo(N0_OUT + b * CH_IN + j + AHEAD)
                    if b == 0 and j == 3:
                        y_tiles((6, 7))
                dve.wait_ge(w_used, N0_OUT + (b + 1) * CH_IN)
                dve.wait_ge(gb_act, 4)
                dve.wait_ge(lnp_in, 64)
                at = slice(b * 512, (b + 1) * 512)
                for t in range(2):
                    mark(dve.tensor_tensor(ZT1[:, :], G[2 * (b % 2) + t][:, :], GB1[:, at], ALU.mult))
                    settle()
                    mark(dve.scalar_tensor_tensor(X1[:, t, at], XR[:, t, at], ALPHA, ZT1[:, :], ALU.mult, ALU.add))
                    settle()
                    dve.bn_stats(BST[:, t * 24 + b * 6:t * 24 + b * 6 + 6], X1[:, t, at]).then_inc(evac[b % 2], 1)
                if b == 0:
                    two_parts(SC2)

            def layer_stats(t):
                dve.bn_aggr(MV[:, 4 * t:4 * t + 2], BST[:, 24 * t:24 * t + 24]).then_inc(ln_var, 1)

            def normalise(t):
                dve.wait_ge(ln_std, t + 1)
                mark(dve.reciprocal(MV[:, 4 * t + 3:4 * t + 4], MV[:, 4 * t + 2:4 * t + 3]))
                settle()
                return dve.tensor_scalar(X1[:, t, :], X1[:, t, :], MV[:, 4 * t:4 * t + 1],
                                         MV[:, 4 * t + 3:4 * t + 4], ALU.subtract, ALU.mult)

            dve.wait_ge(evac[0], EV1[0])
            dve.wait_ge(evac[1], EV1[1])
            for t in range(2):
                layer_stats(t)
            dve.wait_ge(mod_col, MOD_PARTS - 2)
            mark(dve.tensor_tensor(SCG, PCOL[:, PR["ln1_g"]:PR["ln1_g"] + KT], MC[:, SC2:SC2 + KT], ALU.mult))
            mark(dve.tensor_tensor(SHB, PCOL[:, PR["ln1_b"]:PR["ln1_b"] + KT], MC[:, SC2:SC2 + KT], ALU.mult))
            settle()
            mark(dve.tensor_tensor(SHB, SHB, MC[:, SH2:SH2 + KT], ALU.add))
            for t in range(2):
                normalise(t).then_inc(zn_done, 1)
            settle()
            for kt in range(KT):
                if kt % 2 == 0:
                    dve.wait_ge(zn_pe, kt // 2 + 1)
                if kt >= 4:
                    dve.wait_ge(h_lo, KT + kt - 3)
                dve.tensor_scalar(HTMP[:, kt % 4, :], M[kt // 2 % 4][:, (kt % 2) * T:(kt % 2) * T + T],
                                  SCG[:, kt:kt + 1], SHB[:, kt:kt + 1], ALU.mult, ALU.add).then_inc(h_new, 1)
                if kt >= 2:
                    h_split(kt - 2, KT)
                if kt in EARLY:
                    split_lo(N0_UP + AHEAD + EARLY.index(kt))
            h_split(KT - 2, KT)
            h_split(KT - 1, KT)
            OWN_UP = 5
            n_own = own[0]

            def up_block(i, mods, early=0):
                own[0], own[1] = n_own, i * OWN_UP
                for j in range(2 * CH_IN):
                    if j >= early:
                        split_lo_at((j + AHEAD) % RING, i * (2 * CH_IN) + (N0_UP + j + AHEAD))
                    if mods and j % 2:
                        k = j // 2
                        dve.wait_ge(mod_in[k % RING], i * 32 + (16 * MODS_IN // RING + 16 * (k // RING + 1)))
                        dve.wait_ge(conv_cp, i + 1)
                        dve.wait_ge(mod_done, i * 8 + (MODS_IN + k - 1))
                        a = ACC2[:, k % 2, :]
                        dve.scalar_tensor_tensor(a, MODR2[:, k % RING, :], CC4[:, k // 2:k // 2 + 1], a,
                                                 ALU.mult, ALU.add).then_inc(mod_done, 1)
                    if j == 0:
                        if mods:
                            dve.wait_ge(mod_done, i * 8 + MODS_IN)
                            dve.tensor_copy(CC4, CC[:, ds(i * 4, 4)])
                        dve.wait_ge(evac[0], i * 4 + EV1[0])
                        for k, name in enumerate(("conv_b", "conv2", "conv1", "conv0")):
                            ins = dve.tensor_copy(CONV[:, 4 * k:4 * k + 4], PCOL[:, ds(i * 4 + PR[name], 4)])
                        ins.then_inc(conv_cp, 1)
                    if j == CH_IN - 1:
                        dve.wait_ge(conv_cp, i + 1)
                        for k in range(4):
                            g = G[k // 2][:, (k % 2) * T:(k % 2) * T + T]
                            dve.wait_ge(g_pre, i * 4 + (2 * (k // 2) + 2))
                            mark(dve.scalar_tensor_tensor(GF[:, k, 1:T], g[:, 0:T - 1], CONV[:, 8 + k:9 + k],
                                                          GF[:, k, 1:T], ALU.mult, ALU.add))
                        settle()
                        for k in range(4):
                            g = G[k // 2][:, (k % 2) * T:(k % 2) * T + T]
                            dve.scalar_tensor_tensor(GF[:, k, 2:T], g[:, 0:T - 2], CONV[:, 12 + k:13 + k],
                                                     GF[:, k, 2:T], ALU.mult, ALU.add).then_inc(evac[0], 1)
                    if j == 2 * CH_IN - 1:
                        dve.wait_ge(evac[0], i * 4 + (EV1[0] + 4))
                        dve.wait_ge(g_sig, i + 1)
                        gf, sf = GF[:, :, :].rearrange("p k n -> p (k n)"), SF[:, :, :].rearrange("p k n -> p (k n)")
                        mark(dve.tensor_tensor(gf, gf, sf, ALU.mult))
                        settle()
                        dve.wait_ge(w_used, i * (2 * CH_IN) + (N0_UP + 2 * CH_IN))
                        for k in range(2):
                            dve.tensor_tensor(gf[:, 512 * k:512 * k + 512], G[2 + k][:, :],
                                              gf[:, 512 * k:512 * k + 512], ALU.mult).then_inc(evac[1], 1)
                        dve.wait_ge(evac[1], i * 2 + (EV1[1] + 2))
                        dve.wait_ge(f_hi, i + 1)
                        dve.tensor_tensor(FLO[:, ds(i * 4, 4), :], GF[:, :, :], FHI[:, ds(i * 4, 4), :].bitcast(f32),
                                          ALU.subtract).then_inc(f_lo, 1)
                assert own[0] - n_own == OWN_UP, own[0] - n_own

            dve.wait_ge(zeroed, 3)
            up_block(0, True, len(EARLY))
            with dve.Fori(1, UP_MODS) as i:
                up_block(i, True)
            own[0], own[1] = n_own + OWN_UP * UP_MODS, None
            up_block(UP_MODS, False)
            own[0], own[1] = n_own + OWN_UP * (UP_MODS + 1), None
            two_parts(GT2)
            dve.wait_ge(mod_col, MOD_PARTS)
            gate_rows(GT2, DGM2)
            with dve.Fori(UP_MODS + 1, N_UP) as i:
                up_block(i, False)
            own[0], own[1] = n_own + OWN_UP * N_UP, None

            dve.wait_ge(gb_act, 8)
            dve.wait_ge(x1_done, 16)
            for b in range(N_DOWN_BLOCKS):
                for j in range(CH_DOWN):
                    n = N0_DOWN + b * CH_DOWN + j
                    split_lo(n + AHEAD)
                at = slice(b * 512, (b + 1) * 512)
                dve.wait_ge(w_used, N0_DOWN + (b + 1) * CH_DOWN)
                for t in range(2):
                    mark(dve.tensor_tensor(ZT2[:, :], G[2 * (b % 2) + t][:, :], GB2[:, at], ALU.mult))
                    settle()
                    mark(dve.scalar_tensor_tensor(X1[:, t, at], X1[:, t, at], ALPHA, ZT2[:, :], ALU.mult, ALU.add))
                    settle()
                    mark(dve.bn_stats(BST[:, t * 24 + b * 6:t * 24 + b * 6 + 6], X1[:, t, at])) if b >= 2 else \
                        dve.bn_stats(BST[:, t * 24 + b * 6:t * 24 + b * 6 + 6], X1[:, t, at]).then_inc(evac[b % 2], 1)
            settle()
            dve.wait_ge(evac[1], EV2[1] + 2)
            dve.wait_ge(evac[0], EV2[0] + 2)
            for t in range(2):
                layer_stats(t)
            dve.wait_ge(ln2_in, 32)
            mean, rstd = (lambda t: MV[:, 4 * t:4 * t + 1]), (lambda t: MV[:, 4 * t + 3:4 * t + 4])
            dve.wait_ge(ln_var, 4)
            halves = [slice(0, D // 2), slice(D // 2, D)]
            for t in (1, 0):
                for n in range(2):
                    x1 = X1[:, t, halves[n]]
                    mark(dve.scalar_tensor_tensor(x1, x1, mean(t), LN2G[:, halves[n]], ALU.subtract, ALU.mult))
                    if t == 1 and n == 0:
                        for tt in range(2):
                            dve.wait_ge(ln_std, 3 + tt)
                            mark(dve.reciprocal(rstd(tt), MV[:, 4 * tt + 2:4 * tt + 3]))
                    settle()
                    if t == 1:
                        dve.tensor_scalar(x1, x1, rstd(t), None, ALU.mult).then_inc(scaled, 1)
                    else:
                        dve.scalar_tensor_tensor(x1, x1, rstd(t), LN2B[:, halves[n]], ALU.mult, ALU.add)\
                            .then_inc(out_ready[0], 1)

        @block.tensor
        def _(pe):
            def mm(out_, l, r, start=False, stop=False):
                return pe.matmul(out_, l, r, start=start, stop=stop, skip_group_check=True)

            def fm(s, kk, kt, banks, start, stop, tiles=4):
                for i in range(tiles):
                    o = banks[i // 2][:, (i % 2) * T:(i % 2) * T + T]
                    wh, wl = (w[:, s, kk, i * P:(i + 1) * P] for w in (WHI, WLO))
                    mm(o, wh, HHI[:, kt, :], start=start and i % 2 == 0)
                    mm(o, wh, HLO[:, kt, :])
                    ins = mm(o, wl, HHI[:, kt, :], stop=stop)
                return ins

            def tm(s, kk, kt, banks, start, stop, ahi=None, alo=None):
                ahi, alo = (HHI, HLO) if ahi is None else (ahi, alo)
                for t in range(2):
                    lh, ll = (a[:, kt, t * P:(t + 1) * P] for a in (ahi, alo))
                    mm(banks[t][:, :], lh, WHI[:, s, kk, :], start=start)
                    mm(banks[t][:, :], lh, WLO[:, s, kk, :])
                    ins = mm(banks[t][:, :], ll, WHI[:, s, kk, :], stop=stop)
                return ins

            def mod_reduce(m, acc=ACC, at=0):
                for q in range(8):
                    ins = mm(M[3][:, at + q:at + q + 1], acc[:, m % 2, q * P:(q + 1) * P], ONES[:, 0:1],
                             start=True, stop=True)
                ins.then_inc(mod_sum, 1)

            pe.wait_ge(cf_in, 16)
            pe.wait_ge(prow_in, 16 * 13)
            for g, n in enumerate((122, 120, 96)):
                pe.transpose(M[g][:, 0:n], PROW[0:n, g, :], IDENT[0:n, 0:n]).then_inc(pcol_pe, 1)
            pe.wait_ge(x_in, 32)
            for r in range(8):
                if r >= 4:
                    pe.wait_ge(xt_act, r - 3)
                for q in range(4):
                    kt, t = 2 * r + q // 2, q % 2
                    ins = pe.transpose(G[r % 4][:, q * P:(q + 1) * P], X0[:, t, kt * P:(kt + 1) * P], IDENT)
                ins.then_inc(xt_pe, 1)

            def first_parts(ms):
                for m in ms:
                    pe.wait_ge(mod_done, (m + 1) * KT)
                    if m:
                        pe.wait_ge(mod_col, m)
                    mod_reduce(m)

            def w_in_half(n, kk):
                b, j = chunk_at(n)
                s, banks = n % RING, pair(b)
                if kk == 0:
                    pe.wait_ge(lo_done, n + 1)
                    if b < 2:
                        pe.wait_ge(h_lo, 2 * j + 2)
                        pe.wait_ge(xt_act, 8)
                    elif b >= 2 and j == 0:
                        pe.wait_ge(evac[b % 2], EV[b - 2])
                kt = 2 * j + kk
                first, last = kt == 0, kt == KT - 1
                if b in (8, 10, 11):
                    ins = tm(s, kk, kt, banks, first, last)
                elif b == 5:
                    fm(s, kk, kt, banks, first, last, tiles=2)
                    for t in range(2):
                        o = banks[1][:, t * P:t * P + 68]
                        lh, ll = (a[:, kt, t * P:(t + 1) * P] for a in (HHI, HLO))
                        mm(o, lh, WHI[:, s, kk, 256:324], start=first and t == 0)
                        mm(o, lh, WLO[:, s, kk, 256:324])
                        ins = mm(o, ll, WHI[:, s, kk, 256:324], stop=last)
                else:
                    ins = fm(s, kk, kt, banks, first, last)
                if kk == 1:
                    ins.then_inc(w_used, 1)

            rows = [slice(0, 64), slice(64, 128)]

            def setup(what):
                if what == "lora":
                    pe.wait_ge(kn_sqrt, 2)
                    pe.wait_ge(gates, 1)
                    pe.wait_ge(late_in, 80)
                    for h in range(2):
                        for u in range(UNITS):
                            ins = mm(M[2 * h + u // 2][:, (u % 2) * T:(u % 2) * T + T],
                                     W2A2[rows[h], u * P:(u + 1) * P], PA[rows[h], 12, :], start=u % 2 == 0, stop=True)
                        ins.then_inc(lora_pe, 1)
                elif what == "norms":
                    pe.wait_ge(mod_col, 4)
                    for i in range(2):
                        pe.wait_ge(kn_sq, 2 * i + 2)
                        for q in range(2):
                            ins = mm(M[i][:, q * T:(q + 1) * T], HEADS2, SQ[:, 2 * i + q, :], start=q == 0, stop=True)
                        ins.then_inc(kn_pe, 1)

            def rwkv(u, stage):
                def after_dve(name):
                    pe.wait_ge(rw_dve, step(RW_DVE, name, u))

                def after_act(name):
                    pe.wait_ge(rw_act, step(RW_ACT, name, u))

                def prob(h, i):
                    return 2 * h + i

                cu = slice(u * P, (u + 1) * P)
                if stage == "turn":
                    pe.wait_ge(prep_dve, 2 * u + 2)
                    if u:
                        pe.wait_ge(rw_act, step(RW_ACT, "y1", u - 1))
                    else:
                        pe.wait_ge(gates, 2)
                    for q, src in enumerate((BH, KH)):
                        for i in range(2):
                            pe.transpose(M[2][:, (2 * q + i) * P:(2 * q + i + 1) * P], src[:, i * P:(i + 1) * P], IDENT)
                    for i in range(2):
                        pe.transpose(M[3][:, i * P:(i + 1) * P], PA[:, 8 + u, i * P:(i + 1) * P], IDENT)
                    for i in range(2):
                        ins = mm(M[3][:, 256 + 2 * i:258 + 2 * i], RK[:, i * P:(i + 1) * P], HEADS2[:, 0:128:64],
                                 start=True, stop=True)
                elif stage == "gram":
                    after_act("turned")
                    after_dve("ar")
                    for h in range(2):
                        for i in range(2):
                            bh = BH[rows[h], i * P:(i + 1) * P]
                            mm(M[h][:, i * T:(i + 1) * T], bh, AR[rows[h], i, :, :], start=i == 0, stop=True)
                            ins = mm(M[2 + h][:, i * P:(i + 1) * P], AR[rows[h], i, 0, :], bh, start=i == 0, stop=True)
                elif stage.startswith("ld"):
                    l = int(stage[2:])
                    after_dve("inv0" if l == 1 else f"d{l - 1}")
                    for p in range(4):
                        ins = mm(M[2][:, p * P:(p + 1) * P], LT[:, p, :], DI[:, p, :], start=True, stop=True)
                elif stage.startswith("dx"):
                    l = int(stage[2:])
                    after_dve(f"x{l}")
                    for p in range(4):
                        if l < LEVELS:
                            mm(M[0][:, p * P:(p + 1) * P], DT[:, p, :], XI[:, p, :], start=True, stop=True)
                        ins = mm(M[1][:, p * P:(p + 1) * P], XI[:, p, :], DT[:, p, :], start=True, stop=True)
                elif stage == "gram2":
                    after_dve(f"d{LEVELS}")
                    for h in range(2):
                        for i in range(2):
                            ins = mm(M[h][:, i * T:(i + 1) * T], KH[rows[h], i * P:(i + 1) * P], AR[rows[h], i, :, :],
                                     start=i == 0, stop=True)
                elif stage == "rhs0":
                    after_dve("gf")
                    for h in range(2):
                        ins = mm(M[2][:, h * 64:h * 64 + 64], GTR[:, prob(h, 0), :],
                                 VTA[:, 0, u * P + h * 64:u * P + h * 64 + 64], start=True, stop=True)
                elif stage == "sa0":
                    after_act("rhs0")
                    for h in range(2):
                        ins = mm(M[3][:, h * 64:h * 64 + 64], DT[:, prob(h, 0), :], RH[:, h * 64:h * 64 + 64],
                                 start=True, stop=True)
                elif stage == "state":
                    after_act("sa0")
                    for h in range(2):
                        hc = slice(h * 64, h * 64 + 64)
                        mm(M[0][:, hc], ET[:, prob(h, 0), :], SA[:, hc], start=True)
                        mm(M[0][:, hc], FTR[:, prob(h, 0), :], VTA[:, 0, u * P + h * 64:u * P + h * 64 + 64], stop=True)
                    mm(M[1][:, 0:P], TB[:, 0, 0, :], SA[:, :], start=True)
                    ins = mm(M[1][:, 0:P], TB[:, 1, 0, :], VTA[:, 0, cu], stop=True)
                elif stage == "rhs1":
                    after_dve("state")
                    for h in range(2):
                        mm(M[2 + h][:, 0:64], AR[rows[h], 1, 0, :], MST[rows[h], :], start=True)
                        ins = mm(M[2 + h][:, 0:64], GTR[:, prob(h, 1), :],
                                 VTA[:, 1, u * P + h * 64:u * P + h * 64 + 64], stop=True)
                elif stage == "sa1":
                    after_act("rhs1")
                    for h in range(2):
                        ins = mm(M[0][:, h * 64:h * 64 + 64], DT[:, prob(h, 1), :], RH[:, h * 64:h * 64 + 64],
                                 start=True, stop=True)
                elif stage == "y1":
                    after_act("sa1")
                    for h in range(2):
                        hc = slice(h * 64, h * 64 + 64)
                        mm(M[2 + h][:, 0:64], AR[rows[h], 1, 1, :], MST[rows[h], :], start=True)
                        mm(M[2 + h][:, 0:64], ET[:, prob(h, 1), :], SA[:, hc])
                        ins = mm(M[2 + h][:, 0:64], FTR[:, prob(h, 1), :],
                                 VTA[:, 1, u * P + h * 64:u * P + h * 64 + 64], stop=True)
                ins.then_inc(rw_pe, 1)

            def gate_a():
                pe.wait_ge(rw_act, UNITS * len(RW_ACT))
                for t in range(2):
                    mm(M[t][:, :], PA[:, 13, t * P:(t + 1) * P], G2[:, :], start=True, stop=True).then_inc(a_gate, 1)

            def indexer(i):
                t, h = divmod(i, 4)
                if i == 0:
                    pe.wait_ge(a_done, 1)
                if i >= 2:
                    pe.wait_ge(ix_act, i - 1)
                w = P * (t + 1)
                mm(M[h % 2][:, 0:w], BQI[rows[h % 2], h // 2, t * P:(t + 1) * P], BK[rows[h % 2], 1, 0:w],
                   start=True, stop=True).then_inc(ix_pe, 1)

            def attention(g, h):
                q_, k_ = (CQ, CK) if g == 0 else (BQ, BK)
                if h < HEADS:
                    i = g * HEADS + h
                    if i >= 2:
                        pe.wait_ge(at_exp, i - 1)
                    elif i == 0:
                        pe.wait_ge(ix_act, 8)
                        pe.wait_ge(bias_in, 16)
                    if g == 1 and h == 0:
                        pe.wait_ge(sel_done, 2)
                    o, rh, kk = M[h % 2], rows[h % 2], (0 if g == 1 else h // 2)
                    if g == 1:
                        mm(o[:, 0:384], IDB, SEL[:, :], start=True)
                        mm(o[:, 0:384], cb("slope", i=h), cb("dist", 384))
                    else:
                        mm(o[:, 0:384], IDB, cb("band", 384), start=True)
                        mm(o[:, 0:128], BIA[:, h, 0:128], FLIP)
                        mm(o[:, 128:256], BIA[:, h, 128:256], FLIP)
                        mm(o[:, 256:384], BIA[:, h, 0:128], FLIP)
                    mm(o[:, 0:128], q_[rh, h // 2, 0:128], k_[rh, kk, 0:128])
                    mm(o[:, 128:384], q_[rh, h // 2, 128:256], k_[rh, kk, 0:256], stop=True).then_inc(at_s, 1)
                if 1 <= h <= HEADS:
                    i = g * HEADS + h - 1
                    pe.wait_ge(at_exp, i + 1)
                    if i >= 1:
                        pe.wait_ge(at_pt, i)
                    for b in range(3):
                        ins = pe.transpose(M[2][:, b * P:(b + 1) * P], PB[:, i % 2, b * P:(b + 1) * P], IDENT)
                    ins.then_inc(at_turn, 1)
                if h >= 2:
                    hh = h - 2
                    i = g * HEADS + hh
                    pe.wait_ge(at_pt, i + 1)
                    if hh % 4 == 0:
                        pe.wait_ge(at_y, i // 4) if i else pe.wait_ge(mod_col, 8)
                    vals = [BVW[:, t, 0:64] for t in range(2)] if g == 1 else \
                        [CV[:, t, hh * HD:(hh + 1) * HD] for t in range(2)]
                    o = M[3][:, (hh % 4) * P:(hh % 4 + 1) * P]
                    mm(o[:, 0:64], PTB[:, i % 2, 0:128], vals[0], start=True, stop=True)
                    mm(o[:, 64:128], PTB[:, i % 2, 128:256], vals[0], start=True)
                    mm(o[:, 64:128], PTB[:, i % 2, 256:384], vals[1], stop=True).then_inc(at_pv, 1)

            def retention(a):
                if a == 0:
                    pe.wait_ge(at_exp, 16)
                    pe.wait_ge(at_pt, 16)
                    pe.wait_ge(at_y, 4)
                    pe.wait_ge(evac[0], EV[10])
                    pe.wait_ge(evac[1], EV[9])
                for h in range(2 * a, min(2 * a + 2, HEADS + 1)):
                    if h < HEADS:
                        if h >= 2:
                            pe.wait_ge(ret_m, h - 1)
                        r, t = slice(32 * (h % 4), 32 * (h % 4) + 32), h // 4
                        o = M[h % 2]
                        mm(o[:, 0:256], DQK[r, 2 + t, 0:128], DQK[r, t, :], start=True, stop=True)
                        mm(o[:, 256:384], DQK[r, 2 + t, 128:256], DQK[r, t, 128:256], start=True, stop=True)\
                            .then_inc(ret_s, 1)
                    if h >= 1:
                        hh = h - 1
                        pe.wait_ge(ret_m, hh + 1)
                        hc, st = slice(hh * HD, (hh + 1) * HD), STD[:, hh % 2, :]
                        mm(M[2][:, hc], st[:, 0:128], DV[:, 0, hc], start=True, stop=True)
                        mm(M[3][:, hc], st[:, 128:256], DV[:, 0, hc], start=True)
                        mm(M[3][:, hc], st[:, 256:384], DV[:, 1, hc], stop=True).then_inc(ret_pv, 1)

            def norm_d(part):
                pass

            turns = mod_turns()
            first_parts((0, 1))
            for n in range(N0_OUT):
                if n == FIRST_CHUNKS:
                    first_parts((2, 3))
                for half in range(2):
                    w_in_half(n, half)
                    if (n, half) in turns:
                        m = turns[n, half]
                        if n >= RW_TO:
                            pe.wait_ge(rw_act, UNITS * len(RW_ACT))
                        pe.wait_ge(mod_done, (m + 1) * KT)
                        pe.wait_ge(mod_col, m)
                        mod_reduce(m)
                    u, stage = rw_stage(n, half)
                    kind, a = mix_step(n, half)
                    if (n, half) in SETUP:
                        setup(SETUP[n, half])
                    elif stage:
                        rwkv(u, stage)
                    elif kind == "indexer":
                        indexer(2 * a)
                        indexer(2 * a + 1)
                    elif kind == "attention":
                        attention(*divmod(a, HEADS + 2))
                    elif kind == "retention":
                        retention(a)
                    elif kind == "norm":
                        norm_d(a)
                if n == RW_TO:
                    gate_a()
            def gate_rows(dgm, done, banks):
                for nb in range(4):
                    pe.wait_ge(gb_dve, done + nb + 1)
                    mm(banks[nb][:, :], ONES, dgm[:, nb, :], start=True, stop=True).then_inc(gb_pe, 1)

            def y_tiles(rs):
                for r in rs:
                    if r >= 4:
                        pe.wait_ge(y_lo, r - 3)
                    for q in range(4):
                        kt, t = 2 * r + q // 2, q % 2
                        y = YG[kt // 4][:, t, (kt % 4) * P:(kt % 4 + 1) * P]
                        ins = pe.transpose(M[r % 4][:, q * P:(q + 1) * P], y, IDENT)
                    ins.then_inc(y_pe, 1)

            def w_out_chunks(b, js):
                for j in js:
                    if j == 0:
                        pe.wait_ge(evac[b % 2], EV0[b % 2] + 2 * (b // 2))
                    if b == 0:
                        pe.wait_ge(y_lo, j + 1)
                    pe.wait_ge(lo_done, N0_OUT + b * CH_IN + j + 1)
                    for kk in range(2):
                        kt = 2 * j + kk
                        ins = tm(j % RING, kk, kt, pair(b), kt == 0, kt == KT - 1)
                    ins.then_inc(w_used, 1)

            pe.wait_ge(ret_m, HEADS)
            pe.wait_ge(ret_y, 2)
            y_tiles(range(6))
            w_out_chunks(0, range(4))
            pe.wait_ge(d_done, 1)
            y_tiles((6, 7))
            w_out_chunks(0, (4, 5))
            pe.wait_ge(y_lo, 8)
            gate_rows(DGM1, 0, M)
            w_out_chunks(0, (6, 7))
            pe.wait_ge(mod_done, MODS_IN)
            pe.wait_ge(gb_act, 4)
            for m in (8, 9):
                mod_reduce(m, at=8 * (m % 2))
            for b in range(1, N_OUT_BLOCKS):
                w_out_chunks(b, range(CH_IN))
            pe.wait_ge(mod_col, 10)
            pe.wait_ge(zn_done, 2)
            for r in range(8):
                if r >= 4:
                    pe.wait_ge(h_new, KT + 2 * (r - 3))
                for q in range(4):
                    kt, t = 2 * r + q // 2, q % 2
                    ins = pe.transpose(M[r % 4][:, q * P:(q + 1) * P], X1[:, t, kt * P:(kt + 1) * P], IDENT)
                ins.then_inc(zn_pe, 1)

            def up_block(i, first=False):
                for half in range(2):
                    pe.wait_ge(evac[half], i * (4, 2)[half] + EV1[half])
                    for j in range(CH_IN):
                        if first:
                            pe.wait_ge(h_lo, KT + 2 * j + 2 if half == 0 else 2 * KT)
                        pe.wait_ge(lo_done, i * (2 * CH_IN) + (N0_UP + half * CH_IN + j + 1))
                        for kk in range(2):
                            kt = 2 * j + kk
                            ins = fm(j % RING, kk, kt, pair(half), kt == 0, kt == KT - 1)
                        ins.then_inc(w_used, 1)

            up_block(0, True)
            with pe.Fori(1, UP_MODS + 1) as i:
                up_block(i)
            pe.wait_ge(mod_done, MOD_PARTS * KT)
            for m in (MOD_PARTS - 2, MOD_PARTS - 1):
                mod_reduce(m, ACC2, 8 * (m % 2))
            up_block(UP_MODS + 1)
            pe.wait_ge(mod_col, MOD_PARTS)
            gate_rows(DGM2, 4, M)
            with pe.Fori(UP_MODS + 2, N_UP) as i:
                up_block(i)
            pe.wait_ge(f_lo, N_UP - 1)
            with pe.Fori(0, N_DOWN_BLOCKS // 2) as i:
                for bb in range(2):
                    pe.wait_ge(evac[bb], i * 2 + EV2[bb])
                    for j in range(CH_DOWN):
                        n = bb * CH_DOWN + j
                        pe.wait_ge(lo_done, i * (2 * CH_DOWN) + (N0_DOWN + n + 1))
                        if bb == 0 and 2 * j + 2 > FT - 4:
                            pe.wait_ge(f_lo, N_UP)
                        for kk in range(2):
                            kt = 2 * j + kk
                            ins = tm(n % RING, kk, kt, pair(bb), kt == 0, kt == FT - 1, FHI, FLO)
                        ins.then_inc(w_used, 1)


_INS = ['x', 'c', 'w_mod', 'b_mod', 'w_in', 'rwkv_mu', 'rwkv_w0', 'rwkv_w2', 'rwkv_a0', 'rwkv_a2', 'rwkv_g2',
        'rwkv_kk', 'rwkv_ka', 'rwkv_rk', 'rwkv_ln_g', 'rwkv_ln_b', 'chunk_rel_bias', 'w_out', 'ln1_g', 'ln1_b',
        'w_up', 'conv_w', 'conv_b', 'w_down', 'ln2_g', 'ln2_b']


def _constants():
    import numpy as np
    p = np.arange(P)
    eye = np.eye(P)
    f = np.zeros((P, CF_W))
    f[:, 0:128] = eye
    f[:, 128:256] = 1.0
    f[:, 256:384] = (p[:, None] // HD) == (p[None, :] // HD)
    f[:, 384:512] = eye[:, ::-1]
    t = np.arange(T)
    for j in range(2):
        gamma = 1.0 - 2.0 ** (-5.0 - (4 * j + p // 32))
        f[:, 512 + j * T:512 + (j + 1) * T] = gamma[:, None] ** (t[None, :] - 128.0)
        f[:, 1024 + j * T:1024 + (j + 1) * T] = gamma[:, None] ** (128.0 - t[None, :]) * 32 ** -0.5
    b = np.zeros((P, CB_W))
    b[:, 0:128] = eye
    r, q = p[:, None], p[None, :]
    for l in range(LEVELS + 1):
        w = 2 ** l
        m = (r // (2 * w) == q // (2 * w)) & (r // w % 2 == 1) & (q // w % 2 == 0)
        b[:, CB["level"] + l * 128:CB["level"] + (l + 1) * 128] = m
        if l == 0:
            b[:, CB["level0t"]:CB["level0t"] + 128] = m.T
    b[:, CB["su"]:CB["su"] + 128] = r < q
    b[:, CB["iu"]:CB["iu"] + 128] = r <= q
    b[:, CB["ret"]:CB["ret"] + 384] = np.concatenate([r <= q, np.ones((P, P)), r <= q], 1)
    for h in range(HEADS):
        b[:, CB["slope"] + h * 128:CB["slope"] + (h + 1) * 128] = -eye * 2.0 ** -(h + 1)
    pairs = [(p, np.arange(P)), (p + P, np.arange(T))]
    b[:, CB["dist"]:CB["dist"] + 384] = np.concatenate([abs(a[:, None] - k[None, :]) for a, k in pairs], 1)
    b[:, CB["band"]:CB["band"] + 384] = np.concatenate(
        [np.where(k[None, :] < (a[:, None] // CHUNK + 1) * CHUNK, 0.0, -BIG) for a, k in pairs], 1)
    return f.astype(np.float32), (b.astype(np.float32).view(np.uint32) >> 16).astype(np.uint16)


def kernel(**inputs):
    import numpy as _np
    import concourse.bacc as _bacc
    from concourse import mybir as _mybir
    from concourse.bass_utils import run_bass_kernel_spmd as _run

    nc = _bacc.Bacc("TRN2", target_bir_lowering=False, num_devices=1)
    arrays, args = {}, []
    const_f, const_b = _constants()
    for name, a in [(n, inputs[n]) for n in _INS] + [("const_f", const_f), ("const_b", const_b)]:
        a = _np.ascontiguousarray(a)
        arrays[f"in_{name}_dram"] = a
        args.append(nc.dram_tensor(f"in_{name}_dram", a.shape, _mybir.dt.from_np(a.dtype), kind="ExternalInput").ap())
    args.append(nc.dram_tensor("out_0_dram", (1, T, D), _mybir.dt.float32, kind="ExternalOutput").ap())
    encoder_layer(nc, *args)
    r = _run(nc, [arrays], core_ids=[0])
    return r.results[0]["out_0_dram"]
```
